# Optimizing a Trainium2 kernel written in Bass

```python
import math
import jax, jax.numpy as jnp
from jax import lax
import numpy as np

D_MODEL = 1024
BATCH = 1
SEQ = 128
DEPTH = 2
DEC_BATCH = 1
DEC_SEQ = 128
PAST_LEN = 128

GRID_W = 64
SGU_GROUPS = 4
SGU_GROUP_W = 64
SGU_W = SGU_GROUPS * SGU_GROUP_W
SGU_CHUNK = 128
DIFF_HEADS = 4
DIFF_QK = 64
DIFF_V = 2 * DIFF_QK
Q_BLOCK = 128
ROPE_BASE = 10000.0
GLA_HEADS = 4
GLA_DK = 64
GLA_DV = 64
GLA_RANK = 16
GLA_GATE_NORM = 16.0
GLA_CHUNK = 64
PROJ_SIZES = (SGU_W, SGU_W, DIFF_HEADS * 2 * DIFF_QK, DIFF_HEADS * 2 * DIFF_QK, DIFF_HEADS * DIFF_V,
              GLA_HEADS * GLA_DK, GLA_HEADS * GLA_DK, GLA_HEADS * GLA_DV, GLA_HEADS * GLA_DV, GLA_RANK, GLA_RANK)
D_PROJ = sum(PROJ_SIZES)
D_MIX = SGU_W + DIFF_HEADS * DIFF_V + GLA_HEADS * GLA_DV
N_EXPERTS = 16
N_GROUPS = 4
EXPERTS_PER_GROUP = N_EXPERTS // N_GROUPS
TOP_K = 2
D_EXPERT = 512
EPS = 1e-6

kernel_name = 'hybrid_diffusion_prefix_step'

def _rms(x):
    xf = x.astype(jnp.float32)
    return (xf * lax.rsqrt(jnp.mean(xf * xf, axis=-1, keepdims=True) + EPS)).astype(x.dtype)

def _modulate(h, shift, scale):
    return h * (1.0 + scale) + shift

def _adaln(cond, w, b):
    mod = (cond @ w + b)[:, None, :]
    return jnp.split(mod, 6, axis=-1)

def _split_points():
    return np.cumsum(PROJ_SIZES)[:-1].tolist()

def _spatial_gating(u, v, w_s, b_s):
    B, N, _ = u.shape
    u = jax.nn.gelu(u)
    v = _rms(jax.nn.gelu(v).reshape(B, N // SGU_CHUNK, SGU_CHUNK, SGU_GROUPS, SGU_GROUP_W))
    s = jnp.einsum('gpq,bnqgc->bnpgc', w_s, v) + b_s.T[None, None, :, :, None]
    return u * s.reshape(B, N, SGU_W)

def _axial_rope(x):
    n = x.shape[-2]
    n_rows = n // GRID_W
    pos_r = jnp.repeat(jnp.arange(n_rows), GRID_W)
    pos_c = jnp.tile(jnp.arange(GRID_W), n_rows)
    half = DIFF_QK // 2
    nf = half // 2
    freqs = ROPE_BASE ** (-jnp.arange(nf, dtype=jnp.float32) / nf)

    def rot(a, pos):
        ang = pos.astype(jnp.float32)[:, None] * freqs
        cos, sin = jnp.cos(ang), jnp.sin(ang)
        a1, a2 = a[..., :nf].astype(jnp.float32), a[..., nf:].astype(jnp.float32)
        return jnp.concatenate([a1 * cos - a2 * sin, a2 * cos + a1 * sin], axis=-1)

    out = jnp.concatenate([rot(x[..., :half], pos_r), rot(x[..., half:], pos_c)], axis=-1)
    return out.astype(x.dtype)

def _diff_attention(q, k, v, lam):
    B, H, _, Nq, dh = q.shape
    nb = Nq // Q_BLOCK
    qb = jnp.moveaxis(q.reshape(B, H, 2, nb, Q_BLOCK, dh), 3, 0)
    scale = dh ** -0.5

    def block(q_blk):
        s = jnp.einsum('bhiqd,bhikd->bhiqk', q_blk, k).astype(jnp.float32) * scale
        p = jax.nn.softmax(s, axis=-1)
        w = p[:, :, 0] - lam * p[:, :, 1]
        return jnp.einsum('bhqk,bhkv->bhqv', w.astype(v.dtype), v)

    o = lax.map(block, qb)
    return jnp.moveaxis(o, 0, 2).reshape(B, H, Nq, v.shape[-1])

def _gla_chunked(q, k, v, g, s0):
    B, H, N, _ = q.shape
    DV = v.shape[-1]
    nc = N // GLA_CHUNK
    q, k, v, g = (t.astype(jnp.float32).reshape(B, H, nc, GLA_CHUNK, t.shape[-1]) for t in (q, k, v, g))
    b = jnp.cumsum(g, axis=3)
    b_last = b[:, :, :, -1:, :]
    q_dec = q * jnp.exp(b)
    k_inv = k * jnp.exp(-b)
    k_end = k * jnp.exp(b_last - b)
    causal = jnp.tril(jnp.ones((GLA_CHUNK, GLA_CHUNK), dtype=bool))
    attn = jnp.where(causal, jnp.einsum('bhcid,bhcjd->bhcij', q_dec, k_inv), 0.0)
    o_intra = jnp.einsum('bhcij,bhcjv->bhciv', attn, v)

    def step(s, inp):
        q_c, k_c, v_c, dec_c = inp
        o_c = jnp.einsum('bhld,bhdv->bhlv', q_c, s)
        s = dec_c[..., None] * s + jnp.einsum('bhld,bhlv->bhdv', k_c, v_c)
        return s, o_c

    xs = (jnp.moveaxis(q_dec, 2, 0), jnp.moveaxis(k_end, 2, 0), jnp.moveaxis(v, 2, 0),
          jnp.moveaxis(jnp.exp(b_last[:, :, :, 0, :]), 2, 0))
    s_fin, o_inter = lax.scan(step, s0.astype(jnp.float32), xs)
    o = o_intra + jnp.moveaxis(o_inter, 0, 2)
    return o.reshape(B, H, N, DV), s_fin

def _token_mixers(h, w_in, w_out, sgu_w, sgu_b, q_g, k_g, lam, lam_init, diff_g, gla_w2, gla_b, gla_g,
                  ctx_k=None, ctx_v=None, ctx_state=None):
    B, N, _ = h.shape
    proj = h @ w_in
    a_u, a_v, bq, bk, bv, cq, ck, cv, cr, lr_f, lr_b = jnp.split(proj, _split_points(), axis=-1)

    o_a = _spatial_gating(a_u, a_v, sgu_w, sgu_b)

    q = (_rms(bq.reshape(B, N, DIFF_HEADS, 2, DIFF_QK)) * q_g).transpose(0, 2, 3, 1, 4)
    k = (_rms(bk.reshape(B, N, DIFF_HEADS, 2, DIFF_QK)) * k_g).transpose(0, 2, 3, 1, 4)
    v = bv.reshape(B, N, DIFF_HEADS, DIFF_V).transpose(0, 2, 1, 3)

    to_heads = lambda t, d: t.reshape(B, N, GLA_HEADS, d).transpose(0, 2, 1, 3)
    gq = to_heads(cq, GLA_DK) * (GLA_DK ** -0.5)
    gk = to_heads(ck, GLA_DK)
    gv = to_heads(cv, GLA_DV)
    gr = to_heads(cr, GLA_DV)
    g_f = to_heads(jax.nn.log_sigmoid((lr_f @ gla_w2[0] + gla_b[0]).astype(jnp.float32)) / GLA_GATE_NORM, GLA_DK)
    g_b = to_heads(jax.nn.log_sigmoid((lr_b @ gla_w2[1] + gla_b[1]).astype(jnp.float32)) / GLA_GATE_NORM, GLA_DK)

    if ctx_k is None:
        o_b = _diff_attention(q, k, v, lam)
        s0_f = jnp.zeros((B, GLA_HEADS, GLA_DK, GLA_DV), jnp.float32)
        s0_b = s0_f
    else:
        q_r, k_r = _axial_rope(q), _axial_rope(k)
        o_b = _diff_attention(q_r, jnp.concatenate([ctx_k, k_r], axis=3),
                              jnp.concatenate([ctx_v, v], axis=2), lam)
        s0_f, s0_b = ctx_state[:, 0], ctx_state[:, 1]
    o_b = (_rms(o_b) * diff_g * (1.0 - lam_init)).transpose(0, 2, 1, 3).reshape(B, N, DIFF_HEADS * DIFF_V)

    flip = lambda t: jnp.flip(t, axis=2)
    o_f, s_f = _gla_chunked(gq, gk, gv, g_f, s0_f)
    o_r, s_b = _gla_chunked(flip(gq), flip(gk), flip(gv), flip(g_b), s0_b)
    o_c = _rms(o_f + flip(o_r)) * gla_g * jax.nn.silu(gr.astype(jnp.float32))
    o_c = o_c.transpose(0, 2, 1, 3).reshape(B, N, GLA_HEADS * GLA_DV)

    out = (jnp.concatenate([o_a, o_b.astype(o_a.dtype), o_c.astype(o_a.dtype)], axis=-1) @ w_out).astype(h.dtype)
    if ctx_k is None:
        return out, k, v, jnp.stack([s_f, s_b], axis=1)
    return out

def _moe(h, router_w, router_bias, w1, w3, w2):
    B, N, D = h.shape
    t = h.reshape(B * N, D)
    aff = jax.nn.sigmoid((t @ router_w).astype(jnp.float32))
    sel = aff + router_bias.astype(jnp.float32)
    grp_score = lax.top_k(sel.reshape(-1, N_GROUPS, EXPERTS_PER_GROUP), 2)[0].sum(-1)
    best = jnp.argmax(grp_score, axis=-1)
    in_grp = (jnp.arange(N_EXPERTS) // EXPERTS_PER_GROUP)[None, :] == best[:, None]
    _, idx = lax.top_k(jnp.where(in_grp, sel, -jnp.inf), TOP_K)
    w = jnp.take_along_axis(aff, idx, axis=-1)
    w = w / jnp.sum(w, axis=-1, keepdims=True)
    gates = jnp.sum(jax.nn.one_hot(idx, N_EXPERTS, dtype=jnp.float32) * w[..., None], axis=1)
    hid = jax.nn.silu(jnp.einsum('td,edf->tef', t, w1)) * jnp.einsum('td,edf->tef', t, w3)
    y = jnp.einsum('tef,efd->td', hid * gates[:, :, None].astype(hid.dtype), w2)
    return y.reshape(B, N, D).astype(h.dtype)

def _normal(key, shape, scale):
    return jax.random.normal(key, shape, jnp.float32) * scale

def setup_inputs(seed: int = 0) -> dict:
    key = jax.random.key(seed)
    ks = jax.random.split(key, 32)
    D, E, F = D_MODEL, N_EXPERTS, D_EXPERT
    return {
        'x_prompt': _normal(ks[0], (BATCH, SEQ, D), 1.0),
        'x_sample': _normal(ks[1], (DEC_BATCH, DEC_SEQ, D), 1.0),
        'cache_k': _normal(ks[2], (DEC_BATCH, DEPTH, DIFF_HEADS, 2, PAST_LEN, DIFF_QK), 1.0),
        'cache_v': _normal(ks[3], (DEC_BATCH, DEPTH, DIFF_HEADS, PAST_LEN, DIFF_V), 1.0),
        'state_gla': _normal(ks[4], (DEC_BATCH, DEPTH, 2, GLA_HEADS, GLA_DK, GLA_DV), 1.0),
        'c': _normal(ks[5], (DEC_BATCH, D), 1.0),
        'c_ctx': _normal(ks[6], (D,), 1.0),
        'w_in': _normal(ks[7], (DEPTH, D, D_PROJ), D ** -0.5),
        'w_out': _normal(ks[8], (DEPTH, D_MIX, D), D_MIX ** -0.5),
        'sgu_w': _normal(ks[9], (DEPTH, SGU_GROUPS, SGU_CHUNK, SGU_CHUNK), SGU_CHUNK ** -0.5),
        'sgu_b': 1.0 + _normal(ks[10], (DEPTH, SGU_GROUPS, SGU_CHUNK), 0.1),
        'q_norm_g': 1.0 + _normal(ks[11], (DEPTH, DIFF_QK), 0.1),
        'k_norm_g': 1.0 + _normal(ks[12], (DEPTH, DIFF_QK), 0.1),
        'diff_lambda': _normal(ks[13], (DEPTH, 4, DIFF_QK), 0.1),
        'diff_norm_g': 1.0 + _normal(ks[14], (DEPTH, DIFF_V), 0.1),
        'gla_w2': _normal(ks[15], (DEPTH, 2, GLA_RANK, GLA_HEADS * GLA_DK), GLA_RANK ** -0.5),
        'gla_b': _normal(ks[16], (DEPTH, 2, GLA_HEADS * GLA_DK), 0.1),
        'gla_norm_g': 1.0 + _normal(ks[17], (DEPTH, GLA_DV), 0.1),
        'norm1_g': 1.0 + _normal(ks[18], (DEPTH, D), 0.1),
        'norm2_g': 1.0 + _normal(ks[19], (DEPTH, D), 0.1),
        'ada_w': _normal(ks[20], (DEPTH, D, 6 * D), 0.5 * D ** -0.5),
        'ada_b': _normal(ks[21], (DEPTH, 6 * D), 0.02),
        'router_w': _normal(ks[22], (D, E), D ** -0.5),
        'router_bias': _normal(ks[23], (E,), 0.01),
        'moe_w1': _normal(ks[24], (DEPTH, E, D, F), D ** -0.5),
        'moe_w3': _normal(ks[25], (DEPTH, E, D, F), D ** -0.5),
        'moe_w2': _normal(ks[26], (DEPTH, E, F, D), F ** -0.5),
    }

def reference(x_prompt, x_sample, cache_k, cache_v, state_gla, c, c_ctx, w_in, w_out, sgu_w, sgu_b,
              q_norm_g, k_norm_g, diff_lambda, diff_norm_g, gla_w2, gla_b, gla_norm_g, norm1_g, norm2_g,
              ada_w, ada_b, router_w, router_bias, moe_w1, moe_w3, moe_w2):
    cond_ctx = jax.nn.silu(c_ctx)[None, :]
    cond_lat = jax.nn.silu(c)
    xp, xs = x_prompt, x_sample
    new_k, new_v, new_s = [], [], []
    for l in range(DEPTH):
        lam_init = 0.8 - 0.6 * math.exp(-0.3 * l)
        lq1, lk1, lq2, lk2 = diff_lambda[l].astype(jnp.float32)
        lam = jnp.exp(jnp.sum(lq1 * lk1)) - jnp.exp(jnp.sum(lq2 * lk2)) + lam_init
        mix_w = (w_in[l], w_out[l], sgu_w[l], sgu_b[l], q_norm_g[l], k_norm_g[l], lam, lam_init,
                 diff_norm_g[l], gla_w2[l], gla_b[l], gla_norm_g[l])
        moe_w = (router_w, router_bias, moe_w1[l], moe_w3[l], moe_w2[l])

        sh1, sc1, g1, sh2, sc2, g2 = _adaln(cond_ctx, ada_w[l], ada_b[l])
        o, k_l, v_l, s_l = _token_mixers(_modulate(_rms(xp) * norm1_g[l], sh1, sc1), *mix_w)
        xp = xp + g1 * o
        xp = xp + g2 * _moe(_modulate(_rms(xp) * norm2_g[l], sh2, sc2), *moe_w)
        new_k.append(k_l)
        new_v.append(v_l)
        new_s.append(s_l)

        sh1, sc1, g1, sh2, sc2, g2 = _adaln(cond_lat, ada_w[l], ada_b[l])
        o = _token_mixers(_modulate(_rms(xs) * norm1_g[l], sh1, sc1), *mix_w,
                          ctx_k=cache_k[:, l], ctx_v=cache_v[:, l], ctx_state=state_gla[:, l])
        xs = xs + g1 * o
        xs = xs + g2 * _moe(_modulate(_rms(xs) * norm2_g[l], sh2, sc2), *moe_w)

    return (xp, xs, jnp.stack(new_k, axis=1), jnp.stack(new_v, axis=1), jnp.stack(new_s, axis=1))


_drawn_inputs = setup_inputs


def setup_inputs(seed=0):
    import zlib

    import numpy as np

    out = dict(_drawn_inputs(seed))
    spreads = {}
    factors = {}
    for name, (base, spread) in spreads.items():
        noise = np.random.default_rng([zlib.crc32(name.encode()), seed]).standard_normal(out[name].shape)
        drawn = base * np.exp(spread * noise) if base else spread * noise
        out[name] = __import__('jax').numpy.asarray(drawn.astype(out[name].dtype))
    for name, factor in factors.items():
        out[name] = (out[name] * factor).astype(out[name].dtype)
    return out
```

```python
from contextlib import ExitStack
import math

import numpy as np
import concourse.bass as bass
from concourse import mybir

P = 128
NS = 2
D = 1024
KT = D // P
DEPTH = 2
DPROJ = 3104
CW = 512
F = 512
FT = F // P
E = 16
NP_ = E // 2
CAP = 64
ROUNDS = NS * P // CAP
EPS = 1e-6
H = 4
QK = 64
U0, V0, BQ, BK, BV, CQ, CK, CV, CR, LR = 0, 256, 512, 1024, 1536, 2048, 2304, 2560, 2816, 3072
NADA = 6 * D // CW
PROJ = [(LR, 32), (CQ, 512), (CV, 512), (BQ, 512), (BK, 512), (BV, 512), (U0, 512)]
NROWS = 48 + 8 + 8 + 4

F32 = mybir.dt.float32
I32 = mybir.dt.int32
ALU = mybir.AluOpType
ACT = mybir.ActivationFunctionType
X = mybir.AxisListType.X

C_ID, C_ONE, C_TRIF, C_TRIB, C_REMF, C_REMB, C_STRICT = (i * P for i in range(7))
C_CHUNK = 7 * P
C_IOTA = C_CHUNK + 3
C_SEL = C_IOTA + CAP
C_LOWER = C_SEL + 2
C_COS = C_LOWER + 16
C_SIN = C_COS + QK
NCONST = C_SIN + QK


def constants():
    t = np.arange(P)
    a, b = t[:, None], t[None, :]
    same = (a // 64) == (b // 64)
    g = np.float32(1.0 / 16.0)
    c = np.zeros((P, NCONST), np.float32)
    c[:, C_ID:C_ID + P] = a == b
    c[:, C_ONE:C_ONE + P] = 1.0
    c[:, C_TRIF:C_TRIF + P] = ((a <= b) & same) * g
    c[:, C_TRIB:C_TRIB + P] = ((a >= b) & same) * g
    c[:, C_REMF:C_REMF + P] = ((a > b) & same) * g
    c[:, C_REMB:C_REMB + P] = ((a < b) & same) * g
    c[:, C_STRICT:C_STRICT + P] = a < b
    for i, h in enumerate((0, 1, 0)):
        c[:, C_CHUNK + i] = (t // 64 == h) * g
    c[:, C_IOTA:C_IOTA + CAP] = np.arange(CAP)
    for i in range(NS):
        c[:, C_SEL + i] = t % 32 == i
    j, i = np.arange(4)[:, None], np.arange(4)[None, :]
    c[:, C_LOWER:C_LOWER + 16] = (i < j).astype(np.float32).reshape(-1)
    fr = (np.float32(10000.0) ** (-np.arange(16, dtype=np.float32) / np.float32(16))).astype(np.float32)
    for n, pos in enumerate((t // 64, t % 64)):
        ang = pos.astype(np.float32)[:, None] * fr
        c[:, C_COS + 32 * n:C_COS + 32 * n + 32] = np.concatenate([np.cos(ang)] * 2, 1)
        c[:, C_SIN + 32 * n:C_SIN + 32 * n + 32] = np.concatenate([-np.sin(ang), np.sin(ang)], 1)
    return c


def plan(l):
    ada_next = [("ada", l + 1, a) for a in range(NADA)] if l + 1 < DEPTH else []

    def fill(n):
        return [ada_next.pop(0) for _ in range(min(n, len(ada_next)))]

    p = [("params", l, 0)]
    if l == 0:
        p += [("ada", 0, a) for a in range(NADA)] + [("adaout", 0, 0)]
    p += [("mod", l, 0), ("norm", l, 0)]
    p += [("proj", l, 0), ("proj", l, 1), ("glaA", l, 0), ("proj", l, 2), ("glaB", l, 0), ("proj", l, 3),
          ("glaC", l, 0), ("proj", l, 4), ("glaD", l, 0), ("proj", l, 5), ("glaE", l, 0), ("proj", l, 6),
          ("glaF", l, 0)]
    p += [("qkt", l, 0), ("glaA", l, 1), *fill(2), ("sc", l, 0), ("glaB", l, 1), *fill(2), ("wt", l, 0),
          ("glaC", l, 1), *fill(2), ("pv", l, 0), ("glaD", l, 1), ("qkt", l, 1), ("glaE", l, 1), *fill(2),
          ("sgu", l, 0), ("glaF", l, 1), ("sc", l, 1), *fill(2), ("wt", l, 1), *fill(2), ("pv", l, 1),
          ("catT", l, 0), ("wout", l, 0), ("wout", l, 1), ("norm", l, 1)]
    if l + 1 < DEPTH:
        p += [("adaout", l + 1, 0)]
    return p + [("route", l, 0), ("moe", l, 0)]


def hybrid_step(nc, A, outs):
    y_p, y_s, new_k, new_v, new_s = outs
    with ExitStack() as ctx:
        def sb(name, shape, dt=F32):
            return ctx.enter_context(nc.sbuf_tensor(name, shape, dt))

        names = """x_in const_in rows_c_in params_in kcache_out vcache_out state_out y_out
        rows_t rowsc_t cond0 cond ada_row ada_col ada_colc mod_ready ada_used w1_used
        lam sq_ready ss_ready ms_ready rstd_ready xn_ready ht_dve ht_act
        proj ev lrt lrtc zz lng gg cum exps qkd qkt_gla qkt_gla_c attn attn_m zeroed kv o_part st1 og og_sq og_ms og_rs og_done sg_done
        qk_sq qk_ms qk_rs qk_done vms vrs v_done qkT qkTc sc nmax pexp wmix wT wTc pv o_sq o_ms o_rs ob_done
        wsT wsTc sgu_s sgu_done catT catTc wout xadd
        htok htokc logit aff mask pos posm
        x_t x_tc fin_t fin_c
        pmat gat gat_a gat_d h13 silu hid hidt pgt yt tr tr_p ytok_a ytok_d scat acc_d acc_end
        dve_chain act_chain pool_chain flag""".split()
        S = {n: ctx.enter_context(nc.semaphore(n)) for n in names}
        s_ab = [ctx.enter_context(nc.semaphore(f"chunk_in{i}")) for i in range(2)]
        s_slot = [ctx.enter_context(nc.semaphore(f"expert_w_in{i}")) for i in range(6)]
        OV = [{n: ctx.enter_context(nc.semaphore(f"over{l}_{n}")) for n in
               "w p gat gat_c h13 silu hid tr hidt yt tr_p tr_c scat acc".split()} for l in range(DEPTH)]

        const = sb("const", [P, NCONST])
        slots = [sb(f"expert_w{i}", [P, 4096]) for i in range(6)]
        ab = [sb(f"chunk{i}", [P, 4096]) for i in range(2)]
        xT = sb("xT", [P, KT, NS, P])
        hb = sb("hT", [P, KT, NS, P])
        pr = sb("pr", [P, NS, DPROJ])
        gl = sb("gl", [P, 3072])
        at = sb("at", [P, 2560])
        cols = sb("cols", [P, NROWS])
        mod = sb("mod", [P, 48, NS])
        ada = sb("ada", [P, 48, NS])
        wsT = sb("wsT", [P, H, P])
        cvc = sb("cvc", [P, H, P])
        st0 = sb("st0", [P, 2, 2, QK])
        w2gla = sb("w2gla", [33, 512])
        lrT = sb("lrT", [33, P])
        qkg = sb("qkg", [P, 2, QK])
        dg = sb("dg", [P, P])
        glag = sb("glag", [P, QK])
        rw = sb("rw", [P, KT, E])
        rbias = sb("rbias", [P, E])
        small = sb("small", [P, 448])
        half = sb("half", [P, 1])
        posm = sb("posm", [P, NS, E + 2])
        gates = sb("gates", [P, NS, E + 2])
        flag = sb("flag", [1, 1], I32)
        PB = [ctx.enter_context(nc.psum_tensor(f"bank{i}", [P, 512], F32)) for i in range(8)]

        dlam = at[:, 0:256].rearrange("p (a d) -> p a d", a=4)
        rows, rowsc = at[0:NROWS, 256:384], at[0:16, 384:512]
        wst = at[:, 512:1024].rearrange("p (g q) -> p g q", g=H)
        ckc = at[:, 2048:2560].rearrange("p (g d) -> p g d", d=QK)
        sgtmp = at[:, 1024:1280]
        adar = [slots[5][:, CW * i:CW * i + CW] for i in range(2)]
        cond = slots[5][:, 2 * CW:2 * CW + 32 * KT].rearrange("p (k c) -> p k c", c=32)
        rsq = gl[:, 0:512].rearrange("p (a t) -> p a t", a=2)

        ident = const[:, C_ID:C_ID + P]
        ones = const[:, C_ONE:C_ONE + P]

        def sm(a, n):
            return small[:, a:a + n]
        lam = sm(0, 8)
        ssum = sm(8, 8)
        SSQ, QMS, QRS, SMX, SSM = 16, 48, 80, 112, 144
        sg = [sm(192, 0)]

        def glv(a, n):
            return gl[:, a:a + n]
        g_sb, qd, ki, ke, kiT = glv(0, 512), glv(512, 512), glv(1024, 512), glv(1536, 512), glv(2048, 512)
        qdT = g_sb
        attnT = glv(512, 1024)
        st1 = glv(2560, 256).rearrange("p (a b v) -> p a b v", a=2, b=2)
        st2 = glv(2816, 256).rearrange("p (a b v) -> p a b v", a=2, b=2)
        atT = [at[:, 0:1024], at[:, 1024:2560]]
        dec = sm(192, 8)

        prf = pr[:, :, :].rearrange("p s c -> p (s c)")
        htok = prf[:, 0:2048].rearrange("p (s d) -> p s d", s=NS)
        accT = prf[:, 2048:4096]
        hg = prf[:, 4096:5120].rearrange("p (k c) -> p k c", k=KT)
        hidT = prf[:, 5120:5632].rearrange("p (f c) -> p f c", f=FT)
        ytok = gl[:, 0:1024]
        pm = gl[:, 1024:1280].rearrange("p (s c) -> p s c", s=NS)
        pg = gl[:, 1280:1536].rearrange("p (s c) -> p s c", s=NS)
        pgT = gl[:, 1536:1792]
        sg1 = gl[:, 1792:2304]
        hid = gl[:, 2304:2816]
        iotar = gl[:, 2816:2880]
        x_tok = prf[:, 0:2048].rearrange("p (s d) -> p s d", s=NS)

        ORDER = (0, 3, 1, 4, 2, 5)

        plans = [plan(l) for l in range(DEPTH)]
        chunks = []
        for l in range(DEPTH):
            for st, ll, n in plans[l]:
                if st in ("ada", "proj", "wout"):
                    chunks.append((st, ll, n))
        order = {c: i for i, c in enumerate(chunks)}

        def chunk_src(c):
            st, l, n = c
            if st == "ada":
                return A["ada_w"][l, :, CW * n:CW * (n + 1)], CW
            if st == "wout":
                return A["w_out"][l, :, CW * n:CW * (n + 1)], CW
            c0, w = PROJ[n]
            return A["w_in"][l, :, c0:c0 + w], w

        def chunk_view(c):
            w = chunk_src(c)[1]
            return ab[order[c] % 2][:, 0:KT * w].rearrange("p (k c) -> p k c", k=KT)

        def chunk_here(eng, c):
            i = order[c]
            eng.wait_ge(s_ab[i % 2], 16 * (i // 2 + 1))

        def expert_src(l, slot, e):
            b = slot % 3
            if b < 2:
                return A["moe_w1" if b == 0 else "moe_w3"][l, e, :, :].rearrange("(k p) f -> p k f", p=P)
            return A["moe_w2"][l, e, :, :].rearrange("(k p) d -> p k d", p=P)

        def slot_view(s):
            if s % 3 < 2:
                return slots[s][:, :].rearrange("p (k f) -> p k f", k=KT)
            return slots[s][:, :].rearrange("p (k d) -> p k d", k=FT)

        block = ctx.enter_context(nc.Block())

        @block.sync
        def _(sp):
            def load_chunk(i):
                src, w = chunk_src(chunks[i])
                if i >= 2:
                    st, l, n = chunks[i - 2]
                    if st == "ada":
                        sp.wait_ge(S["ada_used"], NADA * l + n + 1)
                    elif st == "proj":
                        sp.wait_ge(S["proj"], 14 * l + 2 * n + 2)
                    else:
                        sp.wait_ge(S["wout"], 2 * l + n + 1)
                sp.dma_start(chunk_view(chunks[i]), src.rearrange("(k p) c -> p k c", p=P)).then_inc(s_ab[i % 2], 16)

            def wait_used(s, pairs):
                sp.wait_ge(S[("w1_used", "h13", "yt")[s % 3]], pairs)

            def load_pair0(l, s):
                if l > 0:
                    wait_used(s, NP_ * l)
                if s == 5:
                    sp.wait_ge(S["ada_col"], NADA * min(l + 2, DEPTH))
                sp.dma_start(slot_view(s), expert_src(l, s, s // 3)).then_inc(s_slot[s], 16)

            at_chunk = 0
            for l in range(DEPTH):
                last = max(order[c] for c in chunks if c in plans[l]) + 1
                first_proj = order[("proj", l, 0)]
                pend = list(ORDER)
                if l + 1 < DEPTH:
                    last += 2
                while at_chunk < last:
                    load_chunk(at_chunk)
                    at_chunk += 1
                    if at_chunk >= first_proj + 2 and len(pend) > 1:
                        load_pair0(l, pend.pop(0))
                for s in pend:
                    load_pair0(l, s)
                with sp.Fori(1, NP_) as i:
                    for s in ORDER:
                        wait_used(s, i + NP_ * l)
                        sp.dma_start(slot_view(s), expert_src(l, s, i * 2 + s // 3)).then_inc(s_slot[s], 16)
                sp.wait_ge(S["posm"], l + 1)
                over = sp.value_load(flag[0:1, 0:1], min_val=0, max_val=1)
                O = OV[l]
                with sp.If(over):
                    for s in range(3):
                        wait_used(s, NP_ * (l + 1))
                    with sp.Fori(1, ROUNDS) as r:
                        with sp.Fori(0, E) as e:
                            sp.wait_ge(O["acc"], r + (r - 1) * E + e + 1)
                            for s in range(3):
                                sp.dma_start(slot_view(s), expert_src(l, s, e)).then_inc(O["w"], 16)

        @block.gpsimd
        def _(pool):
            n_chain = [0]

            def link(ins):
                n_chain[0] += 1
                ins.then_inc(S["pool_chain"], 1)
                pool.wait_ge(S["pool_chain"], n_chain[0])

            pool.dma_start(rowsc[0:8, :], A["c_ctx"].rearrange("(k p) -> k p", p=P)).then_inc(S["rows_c_in"], 16)
            pool.dma_start(rowsc[8:16, :], A["c"].rearrange("o (k p) -> (o k) p", p=P)).then_inc(S["rows_c_in"], 16)
            nc.gpsimd.memset(cond[:, :, :], 0.0).then_inc(S["cond0"], 1)
            link(nc.gpsimd.memset(half[:, :], -0.5))
            link(nc.gpsimd.memset(w2gla[:, :], 0.0))
            link(nc.gpsimd.memset(lrT[:, :], 1.0))

            def params(l):
                pool.dma_start(rows[0:48, :], A["ada_b"][l].rearrange("(k p) -> k p", p=P)).then_inc(S["params_in"], 16)
                pool.dma_start(rows[48:56, :], A["norm1_g"][l].rearrange("(k p) -> k p", p=P)).then_inc(S["params_in"], 16)
                pool.dma_start(rows[56:64, :], A["norm2_g"][l].rearrange("(k p) -> k p", p=P)).then_inc(S["params_in"], 16)
                pool.dma_start(rows[64:68, :], A["sgu_b"][l]).then_inc(S["params_in"], 16)
                pool.dma_start(wst[:, :, :], A["sgu_w"][l].rearrange("g p q -> p g q")).then_inc(S["params_in"], 16)
                pool.dma_start(ckc[:, :, :], A["cache_k"][0, l].rearrange("h i t d -> t (h i) d")).then_inc(S["params_in"], 16)
                pool.dma_start(cvc[:, :, :], A["cache_v"][0, l].rearrange("h t d -> t h d")).then_inc(S["params_in"], 16)
                for a in range(2):
                    for b in range(2):
                        pool.dma_start(st0[64 * b:64 * b + 64, a, :, :],
                                       A["state_gla"][0, l, a, b::2].rearrange("h d v -> d h v")).then_inc(S["params_in"], 16)
                    pool.dma_start(w2gla[16 * a:16 * a + 16, 256 * a:256 * a + 256], A["gla_w2"][l, a]).then_inc(S["params_in"], 16)
                pool.dma_start(w2gla[32:33, :], A["gla_b"][l:l + 1].rearrange("o a c -> o (a c)")).then_inc(S["params_in"], 16)
                pool.dma_start(qkg[:, 0, :], A["q_norm_g"][l].partition_broadcast(P)).then_inc(S["params_in"], 16)
                pool.dma_start(qkg[:, 1, :], A["k_norm_g"][l].partition_broadcast(P)).then_inc(S["params_in"], 16)
                pool.dma_start(dg[:, :], A["diff_norm_g"][l].partition_broadcast(P)).then_inc(S["params_in"], 16)
                pool.dma_start(glag[:, :], A["gla_norm_g"][l].partition_broadcast(P)).then_inc(S["params_in"], 16)
                pool.dma_start(dlam[:, :, :], A["diff_lambda"][l].partition_broadcast(P)).then_inc(S["params_in"], 16)
            for l in range(DEPTH):
                if l == 0:
                    params(0)
                    pool.dma_start(rw[:, :, :], A["router_w"].rearrange("(k p) e -> p k e", p=P)).then_inc(S["params_in"], 16)
                    pool.dma_start(rbias[:, :], A["router_bias"].partition_broadcast(P)).then_inc(S["params_in"], 16)
                for st, ll, n in plans[l]:
                    if st == "glaD":
                        pool.wait_ge(S["qkt_gla_c"], 2 * (2 * l + n + 1))
                        nc.gpsimd.memset(attnT, 0.0).then_inc(S["zeroed"], 1)
                    elif st == "glaF":
                        pool.wait_ge(S["og_ms"], 2 * l + n + 1)
                        nc.gpsimd.tensor_tensor(sm(212, 4), sm(208, 4), half[:, :].to_broadcast([P, 4]), ALU.pow).then_inc(S["og_rs"], 1)
                    elif st == "qkt":
                        pool.wait_ge(S["qk_ms"], 2 * l + n + 1)
                        nc.gpsimd.tensor_tensor(sm(QRS, 16), sm(QMS, 16), half[:, :].to_broadcast([P, 16]), ALU.pow).then_inc(S["qk_rs"], 1)
                        if n == 0:
                            pool.wait_ge(S["qk_done"], 2 * l + 1)
                            pool.dma_start(new_k[0, l].rearrange("h i t d -> t (h i) d"),
                                           pr[:, 0, BK:BK + 512].rearrange("p (g d) -> p g d", d=QK)).then_inc(S["kcache_out"], 16)
                    elif st == "pv":
                        pool.wait_ge(S["o_ms"], 2 * l + n + 1)
                        nc.gpsimd.tensor_tensor(sm(228, 4), sm(224, 4), half[:, :].to_broadcast([P, 4]), ALU.pow).then_inc(S["o_rs"], 1)
                        if n == 0:
                            pool.wait_ge(S["ev"], 14 * l + 12)
                            pool.dma_start(new_v[0, l].rearrange("h t d -> t h d"),
                                           pr[:, 0, BV:BV + 512].rearrange("p (h d) -> p h d", d=P)).then_inc(S["vcache_out"], 16)
                            for a in range(2):
                                for b in range(2):
                                    pool.dma_start(new_s[0, l, a, b::2].rearrange("h d v -> d h v"),
                                                   st2[64 * b:64 * b + 64, a, :, :]).then_inc(S["state_out"], 16)
                    elif st == "sgu":
                        pool.wait_ge(S["vms"], l + 1)
                        nc.gpsimd.tensor_tensor(sm(248, 8), sm(240, 8), half[:, :].to_broadcast([P, 8]), ALU.pow).then_inc(S["vrs"], 1)
                    elif st == "route" and l + 1 < DEPTH:
                        pool.wait_ge(S["posm"], l + 1)
                        params(l + 1)
            pool.wait_ge(S["kcache_out"], 16 * DEPTH)
            pool.wait_ge(S["vcache_out"], 16 * DEPTH)
            pool.wait_ge(S["state_out"], 64 * DEPTH)

        NPARAM = 21

        @block.scalar
        def _(act):
            n_chain = [0]

            def link(ins):
                n_chain[0] += 1
                ins.then_inc(S["act_chain"], 1)
                act.wait_ge(S["act_chain"], n_chain[0])

            def params_here(l):
                act.wait_ge(S["params_in"], 16 * (NPARAM - 2) * l + 16 * NPARAM)

            A_ = nc.scalar.activation
            act.dma_start(const[:, :], A["const"]).then_inc(S["const_in"], 16)
            act.dma_start(x_tok[:, 0, :], A["x_prompt"][0]).then_inc(S["x_in"], 16)
            act.dma_start(x_tok[:, 1, :], A["x_sample"][0]).then_inc(S["x_in"], 16)
            act.wait_ge(S["rowsc_t"], 1)
            act.wait_ge(S["cond0"], 1)
            A_(cond[:, :, 0:2].rearrange("p k s -> p s k"), PB[6][:, 128:144].rearrange("p (s k) -> p s k", s=2),
               ACT.Silu).then_inc(S["cond"], 1)
            for j in range(4):
                if j % 2:
                    act.wait_ge(S["x_t"], j + 1)
                    A_(xT[:, 4 * (j % 2):4 * (j % 2) + 4, j // 2, :], PB[j][:, :].rearrange("p (k t) -> p k t", k=4),
                       ACT.Copy).then_inc(S["x_tc"], 1)
            for l in range(DEPTH):
                for st, ll, n in plans[l]:
                    g = 2 * l + n
                    if st == "params":
                        act.wait_ge(S["lam"], 2 * l + 1)
                        A_(lam[:, 2:4], lam[:, 0:2], ACT.Exp).then_inc(S["lam"], 1)
                        act.wait_ge(S["wsT"], l + 1)
                        A_(wsT[:, :, :].rearrange("p g q -> p (g q)"), PB[4][:, :], ACT.Copy).then_inc(S["wsTc"], 1)
                    elif st == "ada":
                        m = NADA * ll + n
                        act.wait_ge(S["ada_used"], m + 1)
                        if m >= 2:
                            act.wait_ge(S["ada_col"], m - 1)
                        A_(adar[m % 2], PB[7][:, :], ACT.Copy).then_inc(S["ada_row"], 1)
                    elif st == "norm":
                        act.wait_ge(S["ss_ready"], g + 1)
                        A_(rsq[:, 0, :], PB[5][:, 0:NS * P], ACT.Sqrt, scale=1.0 / D, bias=EPS).then_inc(S["rstd_ready"], 1)
                        act.wait_ge(S["xn_ready"], g + 1)
                        for k in range(KT):
                            ins = A_(hb[:, k, 1, :], hb[:, k, 1, :], ACT.Identity, bias=mod[:, 24 * n + k, 1:2],
                                     scale=mod[:, 24 * n + 8 + k, 1:2])
                        ins.then_inc(S["ht_act"], 1)
                    elif st == "proj":
                        for s in range(NS):
                            if n in (1, 4, 6) or (n in (0, 2, 3, 5) and s == 1):
                                act.wait_ge(S["proj"], 14 * l + 2 * n + s + 1)
                                if 2 * n + s > 0:
                                    act.wait_ge(S["ev"], 14 * l + 2 * n + s)
                                c0, w = PROJ[n]
                                src = PB[2 * (n % 2) + s][:, 0:w]
                                A_(pr[:, s, c0:c0 + w], src, ACT.Gelu_apprx_tanh if n == 6 else ACT.Copy).then_inc(S["ev"], 1)
                    elif st == "glaA":
                        act.wait_ge(S["lrt"], g + 1)
                        A_(lrT[0:32, :], PB[4][0:32, 0:P], ACT.Copy).then_inc(S["lrtc"], 1)
                    elif st == "glaB":
                        act.wait_ge(S["zz"], g + 1)
                        if n == 1:
                            act.wait_ge(S["og"], 2 * l + 1)
                        link(A_(ki, PB[5][:, :], ACT.Abs))
                        link(A_(ki, ki, ACT.Exp, scale=-1.0))
                        A_(ki, ki, ACT.Ln, bias=1.0).then_inc(S["lng"], 1)
                    elif st == "glaC":
                        act.wait_ge(S["cum"], g + 1)
                        A_(qd, PB[6][:, :], ACT.Exp)
                        A_(ki, PB[6][:, :], ACT.Exp, scale=-1.0)
                        A_(ke, PB[5][:, :], ACT.Exp)
                        A_(dec, PB[4][:, 0:8], ACT.Exp)
                        act.wait_ge(S["ev"], 14 * l + 6)
                        A_(sgtmp, pr[:, n, CR:CR + 256], ACT.Exp, scale=-1.0).then_inc(S["exps"], 1)
                    elif st == "glaD":
                        act.wait_ge(S["qkt_gla"], g + 1)
                        A_(qdT, PB[4][:, :], ACT.Copy).then_inc(S["qkt_gla_c"], 1)
                    elif st == "glaF":
                        act.wait_ge(S["og"], g + 1)
                        A_(ke[:, 0:256], PB[6][:, 0:256], ACT.Square).then_inc(S["og_sq"], 1)
                    elif st == "qkt":
                        act.wait_ge(S["ev"], 14 * l + 10)
                        if n == 1:
                            act.wait_ge(S["sg_done"], 2 * l + 2)
                        A_(atT[n][:, 0:1024], pr[:, n, BQ:BQ + 1024], ACT.Square).then_inc(S["qk_sq"], 1)
                        act.wait_ge(S["qkT"], g + 1)
                        A_(atT[n][:, 0:512], PB[0][:, :], ACT.Copy)
                        if n == 1:
                            A_(atT[1][:, 1024:1536], PB[2][:, :], ACT.Copy)
                        A_(atT[n][:, 512:1024], PB[1][:, :], ACT.Copy).then_inc(S["qkTc"], 1)
                    elif st == "sc":
                        act.wait_ge(S["nmax"], g + 1)
                        if n == 1:
                            act.wait_ge(S["wT"], 2 * l + 1)
                        for m in range(8):
                            if n == 0:
                                src, dst = PB[2 + m // 4][:, P * (m % 4):P * (m % 4) + P], hb[:, m, 0, :]
                            else:
                                src = PB[m // 2][:, 256 * (m % 2):256 * (m % 2) + 256]
                                dst = hb[:, m, :, :].rearrange("p s t -> p (s t)")
                            ins = A_(dst, src, ACT.Exp, bias=sm(SMX + m, 1), scale=QK ** -0.5, accum_out=sm(SSM + m, 1))
                        ins.then_inc(S["pexp"], 1)
                    elif st == "wt":
                        act.wait_ge(S["wT"], g + 1)
                        if n == 0:
                            A_(atT[0][:, 0:512], PB[0][:, :], ACT.Copy).then_inc(S["wTc"], 1)
                        else:
                            A_(pr[:, 1, BQ:BQ + 512], PB[0][:, :], ACT.Copy)
                            A_(pr[:, 1, BQ + 512:BQ + 1024], PB[1][:, :], ACT.Copy).then_inc(S["wTc"], 1)
                    elif st == "pv":
                        act.wait_ge(S["pv"], g + 1)
                        A_(atT[n][:, 512:1024], PB[1 + n][:, :], ACT.Square).then_inc(S["o_sq"], 1)
                    elif st == "catT":
                        for j in range(4):
                            if j % 2:
                                act.wait_ge(S["catT"], 4 * l + j + 1)
                                A_(hb[:, 4 * (j % 2):4 * (j % 2) + 4, j // 2, :], PB[j][:, :].rearrange("p (k t) -> p k t", k=4),
                                   ACT.Copy).then_inc(S["catTc"], 1)
                    elif st == "route":
                        act.wait_ge(S["vcache_out"], 16 * (l + 1))
                        for j in range(4):
                            if j % 2:
                                act.wait_ge(S["htok"], 4 * l + j + 1)
                                A_(htok[:, j // 2, 512 * (j % 2):512 * (j % 2) + 512], PB[j][:, :], ACT.Copy).then_inc(S["htokc"], 1)
                        act.wait_ge(S["logit"], l + 1)
                        A_(sm(256, 32), PB[4][:, 0:32], ACT.Sigmoid).then_inc(S["aff"], 1)
                    elif st == "moe":
                        act.wait_ge(S["gat"], 2 * (9 * l) + 1)
                        A_(hg[:, 0:4, :], PB[0][:, :].rearrange("p (k c) -> p k c", k=4), ACT.Copy).then_inc(S["gat_a"], 1)
                        with act.Fori(0, NP_) as i:
                            v = i + NP_ * l
                            act.wait_ge(S["h13"], v + 1)
                            A_(sg1, PB[2][:, :], ACT.Silu).then_inc(S["silu"], 1)
                            act.wait_ge(S["gat"], (v + l) * 2 + 3)
                            A_(hg[:, 0:4, :], PB[0][:, :].rearrange("p (k c) -> p k c", k=4), ACT.Copy).then_inc(S["gat_a"], 1)
                            act.wait_ge(S["tr"], v + 1)
                            A_(hidT, PB[2][:, :].rearrange("p (f c) -> p f c", f=FT), ACT.Copy).then_inc(S["hidt"], 1)
                            act.wait_ge(S["tr_p"], v + 1)
                            A_(pgT, PB[3][:, 0:256], ACT.Copy).then_inc(S["pgt"], 1)
                            act.wait_ge(S["yt"], v + 1)
                            A_(ytok[:, 0:512], PB[4][:, :], ACT.Copy).then_inc(S["ytok_a"], 1)
                        act.wait_ge(S["posm"], l + 1)
                        over = act.value_load(flag[0:1, 0:1], min_val=0, max_val=1)
                        O = OV[l]
                        with act.If(over):
                            with act.Fori(1, ROUNDS) as r:
                                with act.Fori(0, E) as e:
                                    act.wait_ge(O["h13"], (r - 1) * E + e + 1)
                                    A_(sg1[0:CAP, :], PB[2][0:CAP, :], ACT.Silu).then_inc(O["silu"], 1)
            for j in range(4):
                if j % 2:
                    act.wait_ge(S["fin_t"], j + 1)
                    A_(x_tok[:, j // 2, 512 * (j % 2):512 * (j % 2) + 512], PB[j][:, :], ACT.Copy).then_inc(S["fin_c"], 1)
            act.wait_ge(S["fin_c"], 4)
            act.dma_start(y_p[0], x_tok[:, 0, :]).then_inc(S["y_out"], 16)
            act.dma_start(y_s[0], x_tok[:, 1, :]).then_inc(S["y_out"], 16)
            act.wait_ge(S["y_out"], 32)

        @block.tensor
        def _(pe):
            mm, tp = nc.tensor.matmul, nc.tensor.transpose

            def ada_columns(m):
                pe.wait_ge(S["ada_row"], m + 1)
                for t in range(4):
                    ins = mm(PB[7][:, 2 * t:2 * t + 2], adar[m % 2][:, P * t:P * t + P], const[:, C_SEL:C_SEL + 2],
                             start=True, stop=True)
                ins.then_inc(S["ada_col"], 1)

            pe.wait_ge(S["const_in"], 16)
            pe.wait_ge(S["rows_c_in"], 32)
            tp(PB[6][:, 128:144], rowsc[:, :], ident[0:16, 0:16]).then_inc(S["rowsc_t"], 1)
            pe.wait_ge(S["x_in"], 32)
            for j in range(4):
                for k in range(4):
                    ins = tp(PB[j][:, P * k:P * k + P], x_tok[:, j // 2, (4 * (j % 2) + k) * P:(4 * (j % 2) + k + 1) * P], ident)
                ins.then_inc(S["x_t"], 1)
            for l in range(DEPTH):
                for st, ll, n in plans[l]:
                    g = 2 * l + n
                    if st == "params":
                        pe.wait_ge(S["params_in"], 16 * (NPARAM - 2) * l + 16 * NPARAM)
                        if l > 0:
                            pe.wait_ge(S["acc_end"], l)
                        pe.wait_ge(S["cond"], 1)
                        tp(PB[6][:, 0:NROWS], rows[:, :], ident[0:NROWS, 0:NROWS]).then_inc(S["rows_t"], 1)
                        for h in range(H):
                            ins = tp(PB[4][:, P * h:P * h + P], wst[:, h, :], ident)
                        ins.then_inc(S["wsT"], 1)
                    elif st == "ada":
                        c = (st, ll, n)
                        chunk_here(pe, c)
                        pe.wait_ge(S["cond"], 1)
                        m = NADA * ll + n
                        if n > 0:
                            ada_columns(m - 1)
                        if m > 0:
                            pe.wait_ge(S["ada_colc"], m)
                        w = chunk_view(c)
                        for k in range(KT):
                            j = 32 * (k % 4)
                            ins = mm(PB[7][j:j + 32, :], cond[:, k, :], w[:, k, :], start=(k < 4), stop=(k >= 4))
                        ins.then_inc(S["ada_used"], 1)
                    elif st == "adaout":
                        ada_columns(NADA * (ll + 1) - 1)
                    elif st == "norm":
                        pe.wait_ge(S["sq_ready"], g + 1)
                        for k in range(KT):
                            ins = mm(PB[5][:, 0:NS * P], ones, hb[:, k, :, :].rearrange("p s t -> p (s t)"),
                                     start=(k == 0), stop=(k == KT - 1))
                        ins.then_inc(S["ss_ready"], 1)
                    elif st == "proj":
                        c = (st, l, n)
                        chunk_here(pe, c)
                        if n == 0:
                            pe.wait_ge(S["ht_dve"], 2 * l + 1)
                            pe.wait_ge(S["ht_act"], 2 * l + 1)
                        w = chunk_view(c)
                        wd = PROJ[n][1]
                        if n >= 2:
                            pe.wait_ge(S["ev"], 14 * l + 2 * n - 2)
                        for s in range(NS):
                            for k in range(KT):
                                ins = mm(PB[2 * (n % 2) + s][:, 0:wd], hb[:, k, s, :], w[:, k, :],
                                         start=(k == 0), stop=(k == KT - 1))
                            ins.then_inc(S["proj"], 1)
                    elif st == "glaA":
                        pe.wait_ge(S["ev"], 14 * l + 2)
                        pe.wait_ge(S["wsTc"], l + 1)
                        if n == 1:
                            pe.wait_ge(S["attn_m"], 2 * l + 1)
                        tp(PB[4][0:32, 0:P], pr[:, n, LR:LR + 32], ident).then_inc(S["lrt"], 1)
                    elif st == "glaB":
                        pe.wait_ge(S["lrtc"], g + 1)
                        if n == 1:
                            pe.wait_ge(S["st1"], 2 * l + 1)
                        mm(PB[5][:, :], lrT[:, :], w2gla[:, :], start=True, stop=True).then_inc(S["zz"], 1)
                    elif st == "glaC":
                        pe.wait_ge(S["gg"], g + 1)
                        if n == 1:
                            pe.wait_ge(S["og_done"], 2 * l + 1)
                        for d in range(2):
                            gd = g_sb[:, 256 * d:256 * d + 256]
                            mm(PB[6][:, 256 * d:256 * d + 256], const[:, (C_TRIF, C_TRIB)[d]:][:, 0:P], gd, start=True, stop=True)
                            mm(PB[5][:, 256 * d:256 * d + 256], const[:, (C_REMF, C_REMB)[d]:][:, 0:P], gd, start=True, stop=True)
                            for b in range(2):
                                q = 2 * d + b
                                ins = mm(PB[4][:, 2 * q:2 * q + 2], g_sb[:, P * q:P * q + P],
                                         const[:, C_CHUNK + d:C_CHUNK + d + 2], start=True, stop=True)
                        ins.then_inc(S["cum"], 1)
                    elif st == "glaD":
                        pe.wait_ge(S["qkd"], g + 1)
                        for q in range(4):
                            tp(PB[4][:, P * q:P * q + P], qd[:, P * q:P * q + P], ident)
                        for q in range(4):
                            ins = tp(PB[5][:, P * q:P * q + P], ki[:, P * q:P * q + P], ident)
                        ins.then_inc(S["qkt_gla"], 1)
                    elif st == "glaE":
                        pe.wait_ge(S["qkt_gla_c"], 2 * (g + 1))
                        for d in range(2):
                            for h in range(H):
                                b, q = 64 * (h % 2), P * (2 * d + h // 2)
                                ins = mm(PB[(6, 4)[h % 2]][:, 256 * d + P * (h // 2):256 * d + P * (h // 2) + P], kiT[b:b + 64, q:q + P], qdT[b:b + 64, q:q + P],
                                         start=True, stop=True)
                        ins.then_inc(S["attn"], 1)
                        for r in (0, 64):
                            for step in range(2):
                                d = step ^ (r // 64)
                                for h in range(H):
                                    b, col = 64 * (h % 2), 64 * (4 * step + 2 * d + h // 2)
                                    ins = mm(PB[5][b:b + 64, col:col + 64], ke[r:r + 64, 256 * d + 64 * h:256 * d + 64 * h + 64],
                                             pr[r:r + 64, n, CV + 64 * h:CV + 64 * h + 64], start=True, stop=True)
                            ins.then_inc(S["kv"], 1)
                            if r == 0:
                                pe.wait_ge(S["kv"], 2 * g + 1)
                    elif st == "glaF":
                        pe.wait_ge(S["attn_m"], g + 1)
                        pe.wait_ge(S["st1"], g + 1)
                        first = True
                        for h in range(H):
                            for d in range(2):
                                ins = mm(PB[6][:, 64 * h:64 * h + 64], attnT[:, P * (4 * d + h):P * (4 * d + h) + P],
                                   pr[:, n, CV + 64 * h:CV + 64 * h + 64], start=first, stop=False, skip_group_check=True)
                                first = False
                        for par in range(2):
                            ins.then_inc(S["o_part"], 1)
                            pe.wait_ge(S["o_part"], 2 * g + par + 1)
                            b = 64 * par
                            for h in range(par, H, 2):
                                for d in range(2):
                                    for step in range(n == 0, 2):
                                        r = 64 * (step ^ d)
                                        q = P * (2 * d + h // 2) + r
                                        state = (st0, st1)[step]
                                        ins = mm(PB[6][r:r + 64, 64 * h:64 * h + 64], qdT[b:b + 64, q:q + 64],
                                                 state[b:b + 64, d, h // 2, :], start=False, stop=(h >= 2), skip_group_check=True)
                        ins.then_inc(S["og"], 1)
                    elif st == "qkt":
                        pe.wait_ge(S["qk_done"], g + 1)
                        pe.wait_ge(S["ev"], 14 * (l + 1))
                        if n == 1:
                            pe.wait_ge(S["ob_done"], 2 * l + 1)
                        for h in range(H):
                            tp(PB[0][:, P * h:P * h + P], pr[:, n, BQ + P * h:BQ + P * h + P], ident)
                        if n == 1:
                            for h in range(H):
                                tp(PB[2][:, P * h:P * h + P], ckc[:, 2 * h:2 * h + 2, :].rearrange("p i d -> p (i d)"), ident)
                        for h in range(H):
                            ins = tp(PB[1][:, P * h:P * h + P], pr[:, n, BK + P * h:BK + P * h + P], ident)
                        ins.then_inc(S["qkT"], 1)
                    elif st == "sc":
                        pe.wait_ge(S["qkTc"], g + 1)
                        if n == 1:
                            pe.wait_ge(S["sgu_done"], l + 1)
                        for m in range(8):
                            b, h = 64 * (m // 4), m % 4
                            q = atT[n][b:b + 64, P * h:P * h + P]
                            k = atT[n][b:b + 64, 512 + P * h:512 + P * h + P]
                            if n == 0:
                                ins = mm(PB[2 + m // 4][:, P * (m % 4):P * (m % 4) + P], q, k, start=True, stop=True)
                            else:
                                kc = atT[n][b:b + 64, 1024 + P * h:1024 + P * h + P]
                                mm(PB[m // 2][:, 256 * (m % 2):256 * (m % 2) + P], q, kc, start=True, stop=True)
                                ins = mm(PB[m // 2][:, 256 * (m % 2) + P:256 * (m % 2) + 2 * P], q, k, start=True, stop=True)
                        ins.then_inc(S["sc"], 1)
                    elif st == "wt":
                        pe.wait_ge(S["wmix"], g + 1)
                        for h in range(H):
                            if n == 0:
                                ins = tp(PB[0][:, P * h:P * h + P], hb[:, h, 0, :], ident)
                            else:
                                for j in range(2):
                                    ins = tp(PB[h // 2][:, 256 * (h % 2) + P * j:256 * (h % 2) + P * j + P], hb[:, h, j, :], ident)
                        ins.then_inc(S["wT"], 1)
                    elif st == "pv":
                        pe.wait_ge(S["wTc"], g + 1)
                        for h in range(H):
                            o = PB[1 + n][:, P * h:P * h + P]
                            v = pr[:, n, BV + P * h:BV + P * h + P]
                            if n == 0:
                                ins = mm(o, atT[0][:, P * h:P * h + P], v, start=True, stop=True)
                            else:
                                mm(o, pr[:, 1, BQ + 256 * h:BQ + 256 * h + P], cvc[:, h, :], start=True, stop=False)
                                ins = mm(o, pr[:, 1, BQ + 256 * h + P:BQ + 256 * h + 2 * P], v, start=False, stop=True)
                        ins.then_inc(S["pv"], 1)
                    elif st == "sgu":
                        pe.wait_ge(S["pexp"], 2 * l + 1)
                        pe.wait_ge(S["v_done"], l + 1)
                        for h in range(H):
                            ins = mm(PB[3][:, P * h:P * h + P], wsT[:, h, :], pr[:, :, V0 + 64 * h:V0 + 64 * h + 64],
                                     start=True, stop=True)
                        ins.then_inc(S["sgu_s"], 1)
                    elif st == "catT":
                        pe.wait_ge(S["ob_done"], 2 * l + 2)
                        pe.wait_ge(S["og_done"], 2 * l + 2)
                        for j in range(4):
                            for k in range(4):
                                m = 4 * (j % 2) + k
                                c0 = (U0, U0 + P, BQ, BQ + P, BQ + 2 * P, BQ + 3 * P, CQ, CQ + P)[m]
                                ins = tp(PB[j][:, P * k:P * k + P], pr[:, j // 2, c0:c0 + P], ident)
                            ins.then_inc(S["catT"], 1)
                    elif st == "wout":
                        c = (st, l, n)
                        chunk_here(pe, c)
                        pe.wait_ge(S["catTc"], 4 * (l + 1))
                        w = chunk_view(c)
                        for t in range(4):
                            for m in range(KT):
                                ins = mm(PB[(4, 0)[n] + t // 2][:, 256 * (t % 2):256 * (t % 2) + 256], w[:, m, P * t:P * t + P],
                                         hb[:, m, :, :].rearrange("p s t -> p (s t)"), start=(m == 0), stop=(m == KT - 1))
                        ins.then_inc(S["wout"], 1)
                    elif st == "route":
                        pe.wait_ge(S["ht_dve"], 2 * l + 2)
                        pe.wait_ge(S["ht_act"], 2 * l + 2)
                        pe.wait_ge(S["xadd"], 2 * (l + 1))
                        for s in range(NS):
                            for k in range(KT):
                                ins = mm(PB[4][:, E * s:E * s + E], hb[:, k, s, :], rw[:, k, :], start=(k == 0), stop=(k == KT - 1))
                        ins.then_inc(S["logit"], 1)
                        for j in range(4):
                            for k in range(4):
                                ins = tp(PB[j][:, P * k:P * k + P], hb[:, 4 * (j % 2) + k, j // 2, :], ident)
                            ins.then_inc(S["htok"], 1)
                        pe.wait_ge(S["mask"], l + 1)
                        m = sm(288, 32)
                        mm(PB[4][:, 32:48], const[:, C_STRICT:C_STRICT + P], m[:, 0:16], start=True, stop=True)
                        mm(PB[4][:, 48:64], ones, m[:, 0:16], start=True, stop=False)
                        mm(PB[4][:, 48:64], const[:, C_STRICT:C_STRICT + P], m[:, 16:32], start=False, stop=True)
                        mm(PB[4][:, 64:80], ones, m[:, 0:16], start=True, stop=False)
                        mm(PB[4][:, 64:80], ones, m[:, 16:32], start=False, stop=True).then_inc(S["pos"], 1)
                    elif st == "moe":
                        def gather(b):
                            for k in range(4):
                                for s in range(NS):
                                    ins = mm(PB[b][:, P * k:P * k + P], htok[:, s, P * (4 * b + k):P * (4 * b + k) + P], pm[:, s, :],
                                             start=(s == 0), stop=(s == NS - 1))
                            ins.then_inc(S["gat"], 1)

                        pe.wait_ge(S["htokc"], 4 * (l + 1))
                        pe.wait_ge(S["pmat"], 9 * l + 1)
                        gather(0)
                        gather(1)

                        def scatter(v):
                            pe.wait_ge(S["ytok_a"], v)
                            pe.wait_ge(S["ytok_d"], v)
                            pe.wait_ge(S["pgt"], v)
                            for t in range(KT):
                                b = (6, 7, 0, 1)[t // 2]
                                ins = mm(PB[b][:, 256 * (t % 2):256 * (t % 2) + 256], ytok[:, P * t:P * t + P], pgT, start=True, stop=True)
                                if t % 4 == 3:
                                    ins.then_inc(S["scat"], 1)

                        with pe.Fori(0, NP_) as i:
                            v = i + NP_ * l
                            pe.wait_ge(S["gat_a"], v + l + 1)
                            pe.wait_ge(S["gat_d"], v + l + 1)
                            pe.wait_ge(S["pgt"], v + l + 1)
                            for b in range(2):
                                for a in range(2):
                                    pe.wait_ge(s_slot[3 * a + b], (v + 1) * 16)
                                for k in range(KT):
                                    for a in range(2):
                                        ins = mm(PB[2 + b][CAP * a:CAP * a + CAP, :], hg[:, k, CAP * a:CAP * a + CAP],
                                                 slot_view(3 * a + b)[:, k, :], start=(k == 0), stop=(k == KT - 1))
                                ins.then_inc(S["w1_used" if b == 0 else "h13"], 1)
                            pe.wait_ge(S["pmat"], v + l + 2)
                            pe.wait_ge(S["acc_d"], v * 2 + 3 * l + 1)
                            gather(0)
                            gather(1)
                            pe.wait_ge(S["hid"], v + 1)
                            for f in range(FT):
                                ins = tp(PB[2][:, P * f:P * f + P], hid[:, P * f:P * f + P], ident)
                            ins.then_inc(S["tr"], 1)
                            pe.wait_ge(S["gat_a"], v + l + 2)
                            pe.wait_ge(S["gat_d"], v + l + 2)
                            scatter(v + l + 1)
                            for s in range(NS):
                                ins = tp(PB[3][:, P * s:P * s + P], pg[:, s, :], ident)
                            ins.then_inc(S["tr_p"], 1)
                            pe.wait_ge(S["hidt"], v + 1)
                            for a in range(2):
                                pe.wait_ge(s_slot[3 * a + 2], (v + 1) * 16)
                            for c in range(2):
                                for f in range(FT):
                                    for a in range(2):
                                        ins = mm(PB[4 + c][CAP * a:CAP * a + CAP, :], hidT[:, f, CAP * a:CAP * a + CAP],
                                                 slot_view(3 * a + 2)[:, f, CW * c:CW * c + CW], start=(f == 0), stop=(f == FT - 1))
                            ins.then_inc(S["yt"], 1)
                        pe.wait_ge(S["acc_d"], 2 * NP_ * (l + 1) + 3 * l + 1)
                        scatter((NP_ + 1) * (l + 1))
                        pe.wait_ge(S["posm"], l + 1)
                        over = pe.value_load(flag[0:1, 0:1], min_val=0, max_val=1)
                        O = OV[l]
                        with pe.If(over):
                            with pe.Fori(1, ROUNDS) as r:
                                with pe.Fori(0, E) as e:
                                    q = (r - 1) * E + e
                                    pe.wait_ge(O["p"], q + 1)
                                    for k in range(KT):
                                        for s in range(NS):
                                            ins = mm(PB[0][:, CAP * k:CAP * k + CAP], htok[:, s, P * k:P * k + P], pm[:, s, 0:CAP],
                                                     start=(s == 0), stop=(s == NS - 1))
                                    ins.then_inc(O["gat"], 1)
                                    pe.wait_ge(O["gat_c"], q + 1)
                                    pe.wait_ge(O["w"], (q + 1) * 48)
                                    for b in range(2):
                                        for k in range(KT):
                                            ins = mm(PB[2 + b][0:CAP, :], hg[:, k, 0:CAP], slot_view(b)[:, k, :],
                                                     start=(k == 0), stop=(k == KT - 1))
                                    ins.then_inc(O["h13"], 1)
                                    pe.wait_ge(O["hid"], q + 1)
                                    for f in range(FT):
                                        ins = tp(PB[2][:, P * f:P * f + P], hid[:, P * f:P * f + P], ident)
                                    ins.then_inc(O["tr"], 1)
                                    pe.wait_ge(O["hidt"], q + 1)
                                    for c in range(2):
                                        for f in range(FT):
                                            ins = mm(PB[4 + c][0:CAP, :], hidT[:, f, 0:CAP], slot_view(2)[:, f, CW * c:CW * c + CW],
                                                     start=(f == 0), stop=(f == FT - 1))
                                    ins.then_inc(O["yt"], 1)
                                    for s in range(NS):
                                        ins = tp(PB[3][:, P * s:P * s + P], pg[:, s, :], ident)
                                    ins.then_inc(O["tr_p"], 1)
                                    pe.wait_ge(O["tr_c"], q + 1)
                                    for t in range(KT):
                                        ins = mm(PB[(6, 7, 0, 1)[t // 2]][:, 256 * (t % 2):256 * (t % 2) + 256], ytok[0:CAP, P * t:P * t + P],
                                                 pgT[0:CAP, :], start=True, stop=True)
                                    ins.then_inc(O["scat"], 1)
            pe.wait_ge(S["acc_end"], DEPTH)
            for j in range(4):
                for k in range(4):
                    ins = tp(PB[j][:, P * k:P * k + P], xT[:, 4 * (j % 2) + k, j // 2, :], ident)
                ins.then_inc(S["fin_t"], 1)

        @block.vector
        def _(dve):
            v_ = nc.vector
            n_chain = [0]

            def link(ins):
                n_chain[0] += 1
                ins.then_inc(S["dve_chain"], 1)
                dve.wait_ge(S["dve_chain"], n_chain[0])

            def ada_copy(m):
                dve.wait_ge(S["ada_col"], m + 1)
                if m == NADA:
                    dve.wait_ge(S["mod_ready"], 1)
                c = 4 * (m % NADA)
                v_.tensor_copy(ada[:, c:c + 4, :].rearrange("p c s -> p (c s)"), PB[7][:, 0:8]).then_inc(S["ada_colc"], 1)

            def bc(ap, shape):
                return ap.to_broadcast(shape)

            link(v_.memset(posm[:, :, :], -1.0))
            link(v_.memset(gates[:, :, :], 0.0))
            for j in range(4):
                if j % 2 == 0:
                    dve.wait_ge(S["x_t"], j + 1)
                    v_.tensor_copy(xT[:, 4 * (j % 2):4 * (j % 2) + 4, j // 2, :],
                                   PB[j][:, :].rearrange("p (k t) -> p k t", k=4)).then_inc(S["x_tc"], 1)
            dve.wait_ge(S["x_tc"], 4)
            dve.wait_ge(S["const_in"], 16)
            for l in range(DEPTH):
                lam_init = 0.8 - 0.6 * math.exp(-0.3 * l)
                for st, ll, n in plans[l]:
                    g = 2 * l + n
                    if st == "params":
                        dve.wait_ge(S["params_in"], 16 * (NPARAM - 2) * l + 16 * NPARAM)
                        link(v_.tensor_tensor(sm(320, 128).rearrange("p (a d) -> p a d", a=2), dlam[:, 0::2, :], dlam[:, 1::2, :], ALU.mult))
                        v_.tensor_reduce(lam[:, 0:2], sm(320, 128).rearrange("p (a d) -> p a d", a=2), X, ALU.add).then_inc(S["lam"], 1)
                        dve.wait_ge(S["lam"], 2 * l + 2)
                        link(v_.tensor_tensor(lam[:, 4:5], lam[:, 3:4], lam[:, 2:3], ALU.subtract))
                        link(v_.tensor_scalar(lam[:, 5:6], lam[:, 4:5], -lam_init, None, ALU.add))
                        link(v_.tensor_scalar(dg[:, :], dg[:, :], 1.0 - lam_init, None, ALU.mult))
                        dve.wait_ge(S["rows_t"], l + 1)
                        link(v_.tensor_copy(cols[:, :], PB[6][:, 0:NROWS]))
                    elif st == "ada" and n > 0:
                        ada_copy(NADA * ll + n - 1)
                    elif st == "adaout":
                        ada_copy(NADA * (ll + 1) - 1)
                    elif st == "mod":
                        dve.wait_ge(S["ada_colc"], NADA * (l + 1))
                        link(v_.tensor_tensor(mod[:, :, :], ada[:, :, :],
                                              bc(cols[:, 0:48].unsqueeze(2), [P, 48, 2]), ALU.add))
                        for b in range(2):
                            m = mod[:, 24 * b + 8:24 * b + 16, :]
                            link(v_.tensor_scalar(m, m, 1.0, None, ALU.add))
                            ins = v_.tensor_tensor(m, m, bc(cols[:, 48 + 8 * b:56 + 8 * b].unsqueeze(2), [P, 8, 2]), ALU.mult)
                            if b == 0:
                                link(ins)
                        ins.then_inc(S["mod_ready"], 1)
                        dve.wait_ge(S["mod_ready"], l + 1)
                    elif st == "norm":
                        v_.tensor_tensor(hb[:, :, :, :], xT[:, :, :, :], xT[:, :, :, :], ALU.mult).then_inc(S["sq_ready"], 1)
                        dve.wait_ge(S["rstd_ready"], g + 1)
                        link(v_.reciprocal(rsq[:, 1, :], rsq[:, 0, :]))
                        v_.tensor_tensor(hb[:, :, :, :].rearrange("p k s t -> p k (s t)"), xT[:, :, :, :].rearrange("p k s t -> p k (s t)"),
                                         bc(rsq[:, 1:2, :], [P, KT, 256]), ALU.mult).then_inc(S["xn_ready"], 1)
                        dve.wait_ge(S["xn_ready"], g + 1)
                        for k in range(KT):
                            ins = v_.tensor_scalar(hb[:, k, 0, :], hb[:, k, 0, :], mod[:, 24 * n + 8 + k, 0:1],
                                                   mod[:, 24 * n + k, 0:1], ALU.mult, ALU.add)
                        ins.then_inc(S["ht_dve"], 1)
                    elif st == "proj":
                        if n in (0, 2, 3, 5):
                            dve.wait_ge(S["proj"], 14 * l + 2 * n + 1)
                            if n > 0:
                                dve.wait_ge(S["ev"], 14 * l + 2 * n)
                            c0, w = PROJ[n]
                            v_.tensor_copy(pr[:, 0, c0:c0 + w], PB[2 * (n % 2)][:, 0:w]).then_inc(S["ev"], 1)
                    elif st == "glaB":
                        dve.wait_ge(S["lng"], g + 1)
                        v_.scalar_tensor_tensor(out=g_sb, in0=PB[5][:, :], scalar=0.0, in1=ki, op0=ALU.min,
                                                op1=ALU.subtract).then_inc(S["gg"], 1)
                    elif st == "glaC":
                        dve.wait_ge(S["exps"], g + 1)
                        dve.wait_ge(S["ev"], 14 * l + 6)
                        q = bc(pr[:, n, CQ:CQ + 256].unsqueeze(1), [P, 2, 256])
                        k = bc(pr[:, n, CK:CK + 256].unsqueeze(1), [P, 2, 256])
                        v3 = [t.rearrange("p (a c) -> p a c", a=2) for t in (qd, ki, ke)]
                        v_.scalar_tensor_tensor(out=v3[0], in0=v3[0], scalar=QK ** -0.5, in1=q, op0=ALU.mult, op1=ALU.mult)
                        v_.tensor_tensor(v3[1], v3[1], k, ALU.mult)
                        v_.tensor_tensor(v3[2], v3[2], k, ALU.mult).then_inc(S["qkd"], 1)
                        sgt = pr[:, n, CR:CR + 256]
                        link(v_.tensor_scalar(sgtmp, sgtmp, 1.0, None, ALU.add))
                        link(v_.reciprocal(sgtmp, sgtmp))
                        v_.tensor_tensor(sgt, sgt, sgtmp, ALU.mult).then_inc(S["sg_done"], 1)
                        dve.wait_ge(S["sg_done"], g + 1)
                        s3 = sgt.rearrange("p (h d) -> p h d", h=H)
                        link(v_.tensor_tensor(s3, s3, bc(glag[:, :].unsqueeze(1), [P, H, 64]), ALU.mult))
                    elif st == "glaD":
                        dve.wait_ge(S["qkt_gla"], g + 1)
                        v_.tensor_copy(kiT, PB[5][:, :]).then_inc(S["qkt_gla_c"], 1)
                    elif st == "glaE":
                        dve.wait_ge(S["attn"], g + 1)
                        dve.wait_ge(S["zeroed"], g + 1)
                        for d in range(2):
                            mask = const[:, (C_TRIF, C_TRIB)[d]:][:, 0:P].bitcast(I32)
                            for par in range(2):
                                ins = v_.copy_predicated(attnT[:, 512 * d:512 * d + 512].rearrange("p (h r i) -> p h r i", r=2, i=P)[:, :, par],
                                                         bc(mask.unsqueeze(1), [P, 2, P]),
                                                         PB[(6, 4)[par]][:, 256 * d:256 * d + 256].rearrange("p (h i) -> p h i", h=2))
                        ins.then_inc(S["attn_m"], 1)
                        dve.wait_ge(S["kv"], 2 * g + 2)
                        if n == 0 and l > 0:
                            dve.wait_ge(S["state_out"], 64 * l)
                        kvb = PB[5][:, :].rearrange("p (s a b v) -> p s (a b) v", s=2, a=2, b=2)
                        d3 = dec.rearrange("p (q s) -> p q s", s=2)
                        s0v, s1v, s2v = (t.rearrange("p a b v -> p (a b) v") for t in (st0[:, :, :, :], st1, st2))
                        if n == 0:
                            link(v_.tensor_copy(s1v, kvb[:, 0]))
                            link(v_.tensor_tensor(s2v, s1v, bc(d3[:, :, 1:2], [P, 4, 64]), ALU.mult))
                            v_.tensor_tensor(s2v, s2v, kvb[:, 1], ALU.add).then_inc(S["st1"], 1)
                        else:
                            link(v_.tensor_tensor(s1v, s0v, bc(d3[:, :, 0:1], [P, 4, 64]), ALU.mult))
                            v_.tensor_tensor(s1v, s1v, kvb[:, 0], ALU.add).then_inc(S["st1"], 1)
                    elif st == "glaF":
                        dve.wait_ge(S["og_sq"], g + 1)
                        link(v_.tensor_reduce(sm(204, 4), ke[:, 0:256].rearrange("p (h d) -> p h d", h=H), X, ALU.add))
                        v_.tensor_scalar(sm(208, 4), sm(204, 4), 1.0 / 64, EPS, ALU.mult, ALU.add).then_inc(S["og_ms"], 1)
                        dve.wait_ge(S["og_rs"], g + 1)
                        for h in range(H):
                            ins = v_.scalar_tensor_tensor(out=pr[:, n, CQ + 64 * h:CQ + 64 * h + 64], in0=PB[6][:, 64 * h:64 * h + 64],
                                                          scalar=sm(212 + h, 1), in1=pr[:, n, CR + 64 * h:CR + 64 * h + 64], op0=ALU.mult, op1=ALU.mult)
                        ins.then_inc(S["og_done"], 1)
                    elif st == "qkt":
                        dve.wait_ge(S["qk_sq"], g + 1)
                        qk16 = pr[:, n, BQ:BQ + 1024].rearrange("p (g d) -> p g d", d=64)
                        link(v_.tensor_reduce(sm(SSQ, 16), atT[n][:, 0:1024].rearrange("p (g d) -> p g d", d=64), X, ALU.add))
                        v_.tensor_scalar(sm(QMS, 16), sm(SSQ, 16), 1.0 / 64, EPS, ALU.mult, ALU.add).then_inc(S["qk_ms"], 1)
                        dve.wait_ge(S["qk_rs"], g + 1)
                        link(v_.tensor_tensor(qk16, qk16, bc(sm(QRS, 16).unsqueeze(2), [P, 16, 64]), ALU.mult))
                        qk4 = pr[:, n, BQ:BQ + 1024].rearrange("p (a g d) -> p a g d", a=2, d=64)
                        ins = v_.tensor_tensor(qk4, qk4, bc(qkg[:, :, :].unsqueeze(2), [P, 2, 8, 64]), ALU.mult)
                        if n == 0:
                            ins.then_inc(S["qk_done"], 1)
                        else:
                            link(ins)
                            tmp = atT[1][:, 0:1024]
                            x5 = pr[:, 1, BQ:BQ + 1024].rearrange("p (g h a f) -> p g h a f", g=16, h=2, a=2)
                            t5 = tmp.rearrange("p (g h a f) -> p g h a f", g=16, h=2, a=2)
                            sn = const[:, C_SIN:C_SIN + 64].rearrange("p (h a f) -> p h a f", h=2, a=2)
                            for a in range(2):
                                ins = v_.tensor_tensor(t5[:, :, :, a, :], x5[:, :, :, 1 - a, :],
                                                       bc(sn[:, :, a, :].unsqueeze(1), [P, 16, 2, 16]), ALU.mult)
                            link(ins)
                            link(v_.tensor_tensor(qk16, qk16, bc(const[:, C_COS:C_COS + 64].unsqueeze(1), [P, 16, 64]), ALU.mult))
                            v_.tensor_tensor(pr[:, 1, BQ:BQ + 1024], pr[:, 1, BQ:BQ + 1024], tmp, ALU.add).then_inc(S["qk_done"], 1)
                    elif st == "sc":
                        dve.wait_ge(S["sc"], g + 1)
                        for b in range(2 if n == 0 else 4):
                            w = 4 if n == 0 else 2
                            ins = v_.tensor_reduce(sm(SMX + 8 + w * b, w), PB[(2 if n == 0 else 0) + b][:, :].rearrange("p (m k) -> p m k", m=w),
                                                   X, ALU.max)
                        link(ins)
                        v_.tensor_scalar(sm(SMX, 8), sm(SMX + 8, 8), -(QK ** -0.5), None, ALU.mult).then_inc(S["nmax"], 1)
                        dve.wait_ge(S["pexp"], g + 1)
                        link(v_.reciprocal(sm(SSM + 8, 8), sm(SSM, 8)))
                        r2 = sm(SSM + 12, 4)
                        link(v_.tensor_scalar(r2, r2, lam[:, 5:6], None, ALU.mult))

                        def pw(m):
                            if n == 0:
                                return hb[:, m, 0, :]
                            return hb[:, m, :, :].rearrange("p s t -> p (s t)")
                        for h in range(H):
                            ins = v_.tensor_scalar(pw(h), pw(h), sm(SSM + 8 + h, 1), None, ALU.mult)
                        link(ins)
                        for h in range(H):
                            ins = v_.scalar_tensor_tensor(out=pw(h), in0=pw(4 + h), scalar=sm(SSM + 12 + h, 1), in1=pw(h),
                                                          op0=ALU.mult, op1=ALU.add)
                        ins.then_inc(S["wmix"], 1)
                    elif st == "pv":
                        dve.wait_ge(S["o_sq"], g + 1)
                        link(v_.tensor_reduce(sm(220, 4), atT[n][:, 512:1024].rearrange("p (h d) -> p h d", h=H), X, ALU.add))
                        v_.tensor_scalar(sm(224, 4), sm(220, 4), 1.0 / P, EPS, ALU.mult, ALU.add).then_inc(S["o_ms"], 1)
                        dve.wait_ge(S["o_rs"], g + 1)
                        for h in range(H):
                            ins = v_.scalar_tensor_tensor(out=pr[:, n, BQ + P * h:BQ + P * h + P], in0=PB[1 + n][:, P * h:P * h + P],
                                                          scalar=sm(228 + h, 1), in1=dg[:, :], op0=ALU.mult, op1=ALU.mult)
                        ins.then_inc(S["ob_done"], 1)
                    elif st == "sgu":
                        dve.wait_ge(S["ev"], 14 * (l + 1))
                        v4 = pr[:, :, V0:V0 + 256]
                        tmp = at[:, 0:512].rearrange("p (s c) -> p s c", s=2)
                        link(v_.tensor_tensor(tmp, v4, v4, ALU.mult))
                        link(v_.tensor_reduce(sm(232, 8), tmp.rearrange("p s (g c) -> p (s g) c", c=64), X, ALU.add))
                        v_.tensor_scalar(sm(240, 8), sm(232, 8), 1.0 / 64, EPS, ALU.mult, ALU.add).then_inc(S["vms"], 1)
                        dve.wait_ge(S["vrs"], l + 1)
                        v5 = v4.rearrange("p s (g c) -> p s g c", c=64)
                        v_.tensor_tensor(v5, v5, bc(sm(248, 8).rearrange("p (s g) -> p s g", s=2).unsqueeze(3), [P, 2, 4, 64]),
                                         ALU.mult).then_inc(S["v_done"], 1)
                        dve.wait_ge(S["sgu_s"], l + 1)
                        for h in range(H):
                            u = pr[:, :, U0 + 64 * h:U0 + 64 * h + 64]
                            ins = v_.scalar_tensor_tensor(out=u, in0=PB[3][:, P * h:P * h + P].rearrange("p (s c) -> p s c", s=2),
                                                          scalar=cols[:, 64 + h:65 + h], in1=u, op0=ALU.add, op1=ALU.mult)
                        ins.then_inc(S["sgu_done"], 1)
                    elif st == "catT":
                        for j in range(4):
                            if j % 2 == 0:
                                dve.wait_ge(S["catT"], 4 * l + j + 1)
                                v_.tensor_copy(hb[:, 0:4, j // 2, :], PB[j][:, :].rearrange("p (k t) -> p k t", k=4)).then_inc(S["catTc"], 1)
                    elif st == "wout":
                        dve.wait_ge(S["wout"], 2 * l + n + 1)
                        for t in range(4):
                            for s in range(NS):
                                k = 4 * n + t
                                ins = v_.scalar_tensor_tensor(out=xT[:, k, s, :], in0=PB[(4, 0)[n] + t // 2][:, 256 * (t % 2) + P * s:256 * (t % 2) + P * s + P],
                                                              scalar=mod[:, 16 + k, s:s + 1], in1=xT[:, k, s, :], op0=ALU.mult, op1=ALU.add)
                        ins.then_inc(S["xadd"], 1)
                        dve.wait_ge(S["xadd"], 2 * l + n + 1)
                    elif st == "route":
                        dve.wait_ge(S["vcache_out"], 16 * (l + 1))
                        dve.wait_ge(S["state_out"], 64 * (l + 1))
                        for j in range(4):
                            if j % 2 == 0:
                                dve.wait_ge(S["htok"], 4 * l + j + 1)
                                v_.tensor_copy(htok[:, j // 2, 0:512], PB[j][:, :]).then_inc(S["htokc"], 1)
                        dve.wait_ge(S["aff"], l + 1)
                        aff = sm(256, 32)
                        sel = sm(320, 32)
                        msk = sm(288, 32)
                        tmp, tmp2 = rsq[:, 0, 0:128], rsq[:, 1, 0:128]
                        link(v_.tensor_tensor(sel.rearrange("p (s e) -> p s e", s=2), aff.rearrange("p (s e) -> p s e", s=2),
                                              bc(rbias[:, :].unsqueeze(1), [P, 2, E]), ALU.add))

                        def before(vals, n_, out):
                            i_ = bc(vals.unsqueeze(2), [P, n_, 4, 4])
                            j_ = bc(vals.unsqueeze(3), [P, n_, 4, 4])
                            a = tmp[:, 0:16 * n_].rearrange("p (n j i) -> p n j i", j=4, i=4)
                            b = tmp2[:, 0:16 * n_].rearrange("p (n j i) -> p n j i", j=4, i=4)
                            low = bc(const[:, C_LOWER:C_LOWER + 16].rearrange("p (j i) -> p j i", j=4).unsqueeze(1), [P, n_, 4, 4])
                            v_.tensor_tensor(a, i_, j_, ALU.is_gt)
                            link(v_.tensor_tensor(b, i_, j_, ALU.is_ge))
                            link(v_.tensor_tensor(b, b, low, ALU.mult))
                            link(v_.tensor_tensor(a, a, b, ALU.max))
                            link(v_.tensor_reduce(out, a, X, ALU.add))

                        sel4 = sel.rearrange("p (n e) -> p n e", e=4)
                        rank = sm(352, 32).rearrange("p (n e) -> p n e", e=4)
                        before(sel4, 8, rank)
                        pairs = sm(384, 48).rearrange("p (n c) -> p n c", c=6)
                        v_.tensor_tensor(pairs[:, :, 0:3], sel4[:, :, 0:3], sel4[:, :, 1:4], ALU.add)
                        v_.tensor_tensor(pairs[:, :, 3:5], sel4[:, :, 0:2], sel4[:, :, 2:4], ALU.add)
                        link(v_.tensor_tensor(pairs[:, :, 5:6], sel4[:, :, 0:1], sel4[:, :, 3:4], ALU.add))
                        grp = sm(432, 8)
                        link(v_.tensor_reduce(grp, pairs, X, ALU.max))
                        gr = sm(440, 8)
                        before(grp.rearrange("p (s g) -> p s g", s=2), 2, gr.rearrange("p (s g) -> p s g", s=2))
                        m4 = msk.rearrange("p (n e) -> p n e", e=4)
                        link(v_.tensor_scalar(gr, gr, 0.5, None, ALU.is_lt))
                        link(v_.tensor_scalar(m4, rank, 1.5, None, ALU.is_lt))
                        v_.tensor_tensor(m4, m4, bc(gr.unsqueeze(2), [P, 8, 4]), ALU.mult).then_inc(S["mask"], 1)
                        dve.wait_ge(S["mask"], l + 1)
                        gt = gates[:, :, 0:E]
                        a2, k2 = aff.rearrange("p (s e) -> p s e", s=2), msk.rearrange("p (s e) -> p s e", s=2)
                        link(v_.tensor_tensor(gt, a2, k2, ALU.mult))
                        link(v_.tensor_reduce(sm(320, 2), gt, X, ALU.add))
                        link(v_.reciprocal(sm(322, 2), sm(320, 2)))
                        link(v_.tensor_tensor(gt, gt, bc(sm(322, 2).unsqueeze(2), [P, 2, E]), ALU.mult))
                        dve.wait_ge(S["pos"], l + 1)
                        link(v_.tensor_scalar(posm[:, :, 0:E], PB[4][:, 32:64].rearrange("p (s e) -> p s e", s=2), 1.0, None, ALU.add))
                        link(v_.tensor_tensor(posm[:, :, 0:E], posm[:, :, 0:E], k2, ALU.mult))
                        link(v_.tensor_scalar(posm[:, :, 0:E], posm[:, :, 0:E], -1.0, None, ALU.add))
                        link(v_.tensor_reduce(sm(324, 1), PB[4][:, 64:80], X, ALU.max))
                        link(v_.tensor_scalar(sm(325, 1), sm(324, 1), CAP + 0.5, None, ALU.is_gt))
                        v_.tensor_copy(flag[0:1, 0:1], small[0:1, 325:326]).then_inc(S["posm"], 1)
                        v_.memset(accT, 0.0).then_inc(S["acc_d"], 1)
                        dve.wait_ge(S["acc_d"], (2 * NP_ + 3) * l + 1)
                        v_.memset(pgT, 0.0).then_inc(S["pgt"], 1)
                        v_.memset(ytok[:, 0:512], 0.0).then_inc(S["ytok_a"], 1)
                        v_.memset(ytok[:, 512:1024], 0.0).then_inc(S["ytok_d"], 1)
                    elif st == "moe":
                        iota = const[:, C_IOTA:C_IOTA + CAP]

                        def selectors(e0, done, na=2, io=iota):
                            for s in range(NS):
                                for a in range(na):
                                    ps = posm[:, s, bass.ds(e0 + a, 1)]
                                    gs = gates[:, s, bass.ds(e0 + a, 1)]
                                    v_.tensor_scalar(pm[:, s, CAP * a:CAP * a + CAP], io, ps, None, ALU.is_equal)
                                    ins = v_.tensor_scalar(pg[:, s, CAP * a:CAP * a + CAP], io, ps, gs, ALU.is_equal, ALU.mult)
                            ins.then_inc(done, 1)

                        def slots_of(i, dst, gated):
                            for s in range(NS):
                                for a in range(2):
                                    ps = posm[:, s, bass.ds(i * 2 + a, 1)]
                                    gs = gates[:, s, bass.ds(i * 2 + a, 1)]
                                    o = dst[:, s, CAP * a:CAP * a + CAP]
                                    if gated:
                                        ins = v_.tensor_scalar(o, iota, ps, gs, ALU.is_equal, ALU.mult)
                                    else:
                                        ins = v_.tensor_scalar(o, iota, ps, None, ALU.is_equal)
                            return ins

                        def accumulate(v, b):
                            dve.wait_ge(S["scat"], v * 2 + b + 1)
                            for c in range(2):
                                t = 1024 * b + 512 * c
                                ins = v_.tensor_tensor(accT[:, t:t + 512], accT[:, t:t + 512], PB[(6, 7, 0, 1)[2 * b + c]][:, :], ALU.add)
                            ins.then_inc(S["acc_d"], 1)

                        slots_of(0, pm, False).then_inc(S["pmat"], 1)
                        dve.wait_ge(S["gat"], 2 * (9 * l) + 2)
                        v_.tensor_copy(hg[:, 4:8, :], PB[1][:, :].rearrange("p (k c) -> p k c", k=4)).then_inc(S["gat_d"], 1)
                        with dve.Fori(0, NP_) as i:
                            v = i + NP_ * l
                            slots_of(i + 1, pm, False).then_inc(S["pmat"], 1)
                            slots_of(i, pg, True)
                            dve.wait_ge(S["silu"], v + 1)
                            v_.tensor_tensor(hid, sg1, PB[3][:, :], ALU.mult).then_inc(S["hid"], 1)
                            dve.wait_ge(S["gat"], (v + l) * 2 + 4)
                            v_.tensor_copy(hg[:, 4:8, :], PB[1][:, :].rearrange("p (k c) -> p k c", k=4)).then_inc(S["gat_d"], 1)
                            accumulate(v + l, 0)
                            accumulate(v + l, 1)
                            dve.wait_ge(S["yt"], v + 1)
                            v_.tensor_copy(ytok[:, 512:1024], PB[5][:, :]).then_inc(S["ytok_d"], 1)
                        accumulate((NP_ + 1) * (l + 1) - 1, 0)
                        accumulate((NP_ + 1) * (l + 1) - 1, 1)
                        over = dve.value_load(flag[0:1, 0:1], min_val=0, max_val=1)
                        O = OV[l]
                        with dve.If(over):
                            v_.tensor_copy(iotar, iota).then_inc(O["acc"], 1)
                            dve.wait_ge(O["acc"], 1)
                            with dve.Fori(1, ROUNDS) as r:
                                v_.tensor_scalar(iotar, iotar, float(CAP), None, ALU.add).then_inc(O["acc"], 1)
                                with dve.Fori(0, E) as e:
                                    q = (r - 1) * E + e
                                    dve.wait_ge(O["acc"], r + q + 1)
                                    for s in range(NS):
                                        ps, gs = posm[:, s, bass.ds(e, 1)], gates[:, s, bass.ds(e, 1)]
                                        v_.tensor_scalar(pm[:, s, 0:CAP], iotar, ps, None, ALU.is_equal)
                                        ins = v_.tensor_scalar(pg[:, s, 0:CAP], iotar, ps, gs, ALU.is_equal, ALU.mult)
                                    ins.then_inc(O["p"], 1)
                                    dve.wait_ge(O["gat"], q + 1)
                                    v_.tensor_copy(hg[:, :, 0:CAP], PB[0][:, :].rearrange("p (k c) -> p k c", k=KT)).then_inc(O["gat_c"], 1)
                                    dve.wait_ge(O["silu"], q + 1)
                                    v_.tensor_tensor(hid[0:CAP, :], sg1[0:CAP, :], PB[3][0:CAP, :], ALU.mult).then_inc(O["hid"], 1)
                                    dve.wait_ge(O["tr"], q + 1)
                                    v_.tensor_copy(hidT, PB[2][:, :].rearrange("p (f c) -> p f c", f=FT)).then_inc(O["hidt"], 1)
                                    dve.wait_ge(O["tr_p"], q + 1)
                                    v_.tensor_copy(pgT[0:CAP, :], PB[3][0:CAP, 0:256])
                                    v_.tensor_copy(ytok[0:CAP, 0:512], PB[4][0:CAP, :])
                                    v_.tensor_copy(ytok[0:CAP, 512:1024], PB[5][0:CAP, :]).then_inc(O["tr_c"], 1)
                                    dve.wait_ge(O["scat"], q + 1)
                                    for c in range(4):
                                        ins = v_.tensor_tensor(accT[:, 512 * c:512 * c + 512], accT[:, 512 * c:512 * c + 512],
                                                               PB[(6, 7, 0, 1)[c]][:, :], ALU.add)
                                    ins.then_inc(O["acc"], 1)
                            dve.wait_ge(O["acc"], ROUNDS + (ROUNDS - 1) * E)
                        dve.wait_ge(S["acc_d"], (2 * NP_ + 3) * (l + 1))
                        link(v_.tensor_copy(sm(328, 1), accT[:, 0:1]))
                        a4 = accT.rearrange("p (k s t) -> p k s t", k=KT, s=2)
                        for k in range(KT):
                            for s in range(NS):
                                ins = v_.scalar_tensor_tensor(out=xT[:, k, s, :], in0=a4[:, k, s, :], scalar=mod[:, 40 + k, s:s + 1],
                                                              in1=xT[:, k, s, :], op0=ALU.mult, op1=ALU.add)
                        ins.then_inc(S["acc_end"], 1)
                        dve.wait_ge(S["acc_end"], l + 1)
            for j in range(4):
                if j % 2 == 0:
                    dve.wait_ge(S["fin_t"], j + 1)
                    v_.tensor_copy(x_tok[:, j // 2, 0:512], PB[j][:, :]).then_inc(S["fin_c"], 1)


_INS = ['x_prompt', 'x_sample', 'cache_k', 'cache_v', 'state_gla', 'c', 'c_ctx', 'w_in', 'w_out', 'sgu_w', 'sgu_b',
        'q_norm_g', 'k_norm_g', 'diff_lambda', 'diff_norm_g', 'gla_w2', 'gla_b', 'gla_norm_g', 'norm1_g', 'norm2_g',
        'ada_w', 'ada_b', 'router_w', 'router_bias', 'moe_w1', 'moe_w3', 'moe_w2']
_OUTS = [(1, P, D), (1, P, D), (1, DEPTH, H, 2, P, QK), (1, DEPTH, H, P, P), (1, DEPTH, 2, H, QK, QK)]


def kernel(**inputs):
    import numpy as _np
    import concourse.bacc as _bacc
    from concourse import mybir as _mybir
    from concourse.bass_utils import run_bass_kernel_spmd as _run

    nc = _bacc.Bacc("TRN2", target_bir_lowering=False, num_devices=1)
    arrays, aps = {}, {}
    given = {name: _np.ascontiguousarray(inputs[name]) for name in _INS}
    given["const"] = constants()
    for name, a in given.items():
        arrays[f"in_{name}_dram"] = a
        aps[name] = nc.dram_tensor(f"in_{name}_dram", a.shape, _mybir.dt.from_np(a.dtype), kind="ExternalInput").ap()
    outs = [nc.dram_tensor(f"out_{i}_dram", shape, _mybir.dt.float32, kind="ExternalOutput").ap()
            for i, shape in enumerate(_OUTS)]
    hybrid_step(nc, aps, outs)
    r = _run(nc, [arrays], core_ids=[0])
    return tuple(r.results[0][f"out_{i}_dram"] for i in range(len(_OUTS)))
```

```python
from contextlib import ExitStack
import math

import numpy as np
import concourse.bass as bass
from concourse import mybir

P = 128
NS = 2
D = 1024
KT = D // P
DEPTH = 2
DPROJ = 3104
CW = 512
F = 512
FT = F // P
E = 16
NP_ = E // 2
CAP = 64
ROUNDS = NS * P // CAP
EPS = 1e-6
H = 4
QK = 64
U0, V0, BQ, BK, BV, CQ, CK, CV, CR, LR = 0, 256, 512, 1024, 1536, 2048, 2304, 2560, 2816, 3072
NADA = 6 * D // CW
PROJ = [(LR, 32), (CQ, 512), (CV, 512), (BQ, 512), (BK, 512), (U0, 512), (BV, 512)]
BY_ACT = (1, 4, 5)
ADA_FIRST = (0, NADA // 2, 3 * NADA // 2)
NROWS = 48 + 8 + 8 + 4

F32 = mybir.dt.float32
I32 = mybir.dt.int32
ALU = mybir.AluOpType
ACT = mybir.ActivationFunctionType
X = mybir.AxisListType.X

C_ID, C_ONE, C_TRIF, C_TRIB, C_REMF, C_REMB, C_STRICT = (i * P for i in range(7))
C_CHUNK = 7 * P
C_IOTA = C_CHUNK + 3
C_SEL = C_IOTA + CAP
C_LOWER = C_SEL + 2
C_COS = C_LOWER + 16
C_SIN = C_COS + QK
NCONST = C_SIN + QK


def constants():
    t = np.arange(P)
    a, b = t[:, None], t[None, :]
    same = (a // 64) == (b // 64)
    g = np.float32(1.0 / 16.0)
    c = np.zeros((P, NCONST), np.float32)
    c[:, C_ID:C_ID + P] = a == b
    c[:, C_ONE:C_ONE + P] = 1.0
    c[:, C_TRIF:C_TRIF + P] = ((a <= b) & same) * g
    c[:, C_TRIB:C_TRIB + P] = ((a >= b) & same) * g
    c[:, C_REMF:C_REMF + P] = ((a > b) & same) * g
    c[:, C_REMB:C_REMB + P] = ((a < b) & same) * g
    c[:, C_STRICT:C_STRICT + P] = a < b
    for i, h in enumerate((0, 1, 0)):
        c[:, C_CHUNK + i] = (t // 64 == h) * g
    c[:, C_IOTA:C_IOTA + CAP] = np.arange(CAP)
    for i in range(NS):
        c[:, C_SEL + i] = t % 32 == i
    j, i = np.arange(4)[:, None], np.arange(4)[None, :]
    c[:, C_LOWER:C_LOWER + 16] = (i < j).astype(np.float32).reshape(-1)
    fr = (np.float32(10000.0) ** (-np.arange(16, dtype=np.float32) / np.float32(16))).astype(np.float32)
    for n, pos in enumerate((t // 64, t % 64)):
        ang = pos.astype(np.float32)[:, None] * fr
        c[:, C_COS + 32 * n:C_COS + 32 * n + 32] = np.concatenate([np.cos(ang)] * 2, 1)
        c[:, C_SIN + 32 * n:C_SIN + 32 * n + 32] = np.concatenate([-np.sin(ang), np.sin(ang)], 1)
    return c


def plan(l):
    half = NADA // 2
    ada_mlp = [("ada", l, half + a) for a in range(half)]
    ada_next = [("ada", l + 1, a) for a in range(half)] if l + 1 < DEPTH else []

    def fill(*n):
        out = []
        for _ in range(sum(n)):
            if ada_mlp:
                out.append(ada_mlp.pop(0))
            elif ada_next:
                out.append(ada_next.pop(0))
        return out

    def proj(*halves):
        return [("proj", l, j) for j in halves]

    p = []
    if l == 0:
        p += [("ada", 0, 0), ("ada", 0, 1), ("xin", 0, 0), ("ada", 0, 2), ("params", 0, 0)]
        p += [("ada", 0, a) for a in range(3, half)] + [("adaout", 0, half - 1)]
    else:
        p += [("params", l, 0)]
    p += [("mod", l, 0), ("norm", l, 0)]
    p += [*proj(0, 1, 2, 3), ("glaA", l, 0), *proj(4), ("glaB", l, 0), *proj(5), ("glaC", l, 0), *proj(6), ("glaD", l, 0),
          *proj(7), ("glaE", l, 0), *proj(8), ("glaF", l, 0), ("glaA", l, 1), *proj(9), ("glaB", l, 1), ("qkn", l, 0),
          *proj(10), ("glaC", l, 1), *proj(11), ("glaD", l, 1), ("qkn", l, 1), *proj(12), ("glaE", l, 1), ("sguv", l, 0),
          *proj(13), ("glaF", l, 1)]
    p += [("qkt", l, 0), *fill(1), ("qkt", l, 1), ("sc", l, 0), *fill(1), ("sgu", l, 0), ("sc", l, 1), ("mix", l, 0), *fill(1),
          ("wt", l, 0), *fill(1), ("mix", l, 1), ("pv", l, 0), ("wt", l, 1), ("catT", l, 0), ("pv", l, 1), *fill(2), ("catT", l, 1)]
    assert not ada_mlp
    if l + 1 < DEPTH:
        p += [*fill(1), ("mod", l, 1), ("wout", l, 0), *fill(1), ("wout", l, 1), *fill(1), ("norm", l, 1), *fill(1),
              ("routeA", l, 0), *fill(2), ("adaout", l + 1, half - 1), ("route", l, 0)]
    else:
        p += [("adaout", l, NADA - 1), ("mod", l, 1), ("wout", l, 0), ("wout", l, 1), ("norm", l, 1), ("routeA", l, 0), ("route", l, 0)]
    return p + [("moe", l, 0)]


def hybrid_step(nc, A, outs):
    y_p, y_s, new_k, new_v, new_s = outs
    with ExitStack() as ctx:
        def sb(name, shape, dt=F32):
            return ctx.enter_context(nc.sbuf_tensor(name, shape, dt))

        names = """x_in const_in rows_c_in params_in kcache_out vcache_out state_out y_out
        rows_t rowsc_t cond0 cond ada_row ada_col ada_colc mod_ready ada_used w1_used
        lam sq_ready ss_ready ms_ready rstd_ready xn_ready ht_dve ht_act
        proj ev lrt lrtc zz lng gg cum exps qkd qkt_gla qkt_gla_c attn attn_m zeroed kv o_part st1 og og_sq og_ms og_rs og_done sg_done
        qk_sq qk_ms qk_rs qk_done vms vrs v_done qkT qkTc sc nmax pexp wmix wT wTc pv o_sq o_ms o_rs ob_done
        wsT wsTc sgu_s sgu_done catT catTc wout xadd
        htok htokc logit aff mask pos posm
        x_t x_tc fin_t fin_c
        pmat gat gat_a gat_d h13 silu hid hidt pgt yt tr tr_p ytok_a ytok_d scat acc_d acc_end
        dve_chain act_chain pool_chain flag""".split()
        S = {n: ctx.enter_context(nc.semaphore(n)) for n in names}
        s_ab = [ctx.enter_context(nc.semaphore(f"chunk_in{i}")) for i in range(2)]
        s_slot = [ctx.enter_context(nc.semaphore(f"expert_w_in{i}")) for i in range(6)]
        OV = [{n: ctx.enter_context(nc.semaphore(f"over{l}_{n}")) for n in
               "w p gat gat_c h13 silu hid tr hidt yt tr_p tr_c scat acc".split()} for l in range(DEPTH)]

        const = sb("const", [P, NCONST])
        slots = [sb(f"expert_w{i}", [P, 4096]) for i in range(6)]
        ab = [sb(f"chunk{i}", [P, 4096]) for i in range(2)]
        xT = sb("xT", [P, KT, NS, P])
        hb = sb("hT", [P, KT, NS, P])
        pr = sb("pr", [P, NS, DPROJ])
        gl = sb("gl", [P, 3072])
        at = sb("at", [P, 2560])
        cols = sb("cols", [P, NROWS])
        mod = sb("mod", [P, 48, NS])
        ada = sb("ada", [P, 48, NS])
        wsT = sb("wsT", [P, H, P])
        cvc = sb("cvc", [P, H, P])
        st0 = sb("st0", [P, 2, 2, QK])
        w2gla = sb("w2gla", [33, 512])
        lrT = sb("lrT", [33, P])
        qkg = sb("qkg", [P, 2, QK])
        dg = sb("dg", [P, P])
        rw = sb("rw", [P, KT, E])
        rbias = sb("rbias", [P, E])
        small = sb("small", [P, 448])
        half = sb("half", [P, 1])
        posm = sb("posm", [P, NS, E + 2])
        gates = sb("gates", [P, NS, E + 2])
        flag = sb("flag", [1, 1], I32)
        condm = sb("cond", [P, 32 * KT])
        PB = [ctx.enter_context(nc.psum_tensor(f"bank{i}", [P, 512], F32)) for i in range(8)]

        dlam = at[:, 0:256].rearrange("p (a d) -> p a d", a=4)
        rows, rowsc = at[0:NROWS, 256:384], at[0:16, 384:512]
        wst = at[:, 512:1024].rearrange("p (g q) -> p g q", g=H)
        ckc = at[:, 2048:2560].rearrange("p (g d) -> p g d", d=QK)
        sgtmp = at[:, 1024:1280]
        adar = [slots[5][:, CW * i:CW * i + CW] for i in range(2)]
        cond = condm[:, :].rearrange("p (k c) -> p k c", c=32)
        rsq = gl[:, 0:512].rearrange("p (a t) -> p a t", a=2)

        ident = const[:, C_ID:C_ID + P]
        ones = const[:, C_ONE:C_ONE + P]

        def sm(a, n):
            return small[:, a:a + n]
        lam = sm(0, 8)
        ssum = sm(8, 8)
        SSQ, QMS, QRS, SMX, SSM = 16, 32, 48, 64, 96
        glag = sm(128, QK)

        def glv(a, n):
            return gl[:, a:a + n]
        g_sb, qd, ki, ke, kiT = glv(0, 512), glv(512, 512), glv(1024, 512), glv(1536, 512), glv(2048, 512)
        qdT = g_sb
        attnT = glv(512, 1024)
        st1 = glv(2560, 256).rearrange("p (a b v) -> p a b v", a=2, b=2)
        st2 = glv(2816, 256).rearrange("p (a b v) -> p a b v", a=2, b=2)
        atT = [at[:, 0:1024], at[:, 1024:2560]]
        dec = sm(192, 8)
        p0w = glv(0, 1024).rearrange("p (m t) -> p m t", m=8)
        CATB = (2, 6, 0, 1)
        SCB = (0, 1, 4, 5)

        prf = pr[:, :, :].rearrange("p s c -> p (s c)")
        htok = prf[:, 0:2048].rearrange("p (s d) -> p s d", s=NS)
        accT = prf[:, 2048:4096]
        hg = prf[:, 4096:5120].rearrange("p (k c) -> p k c", k=KT)
        hidT = prf[:, 5120:5632].rearrange("p (f c) -> p f c", f=FT)
        ytok = gl[:, 0:1024]
        pm = gl[:, 1024:1280].rearrange("p (s c) -> p s c", s=NS)
        pg = gl[:, 1280:1536].rearrange("p (s c) -> p s c", s=NS)
        pgT = gl[:, 1536:1792]
        sg1 = gl[:, 1792:2304]
        hid = gl[:, 2304:2816]
        iotar = gl[:, 2816:2880]
        x_tok = prf[:, 0:2048].rearrange("p (s d) -> p s d", s=NS)

        ORDER = (0, 3, 1, 4, 2, 5)

        plans = [plan(l) for l in range(DEPTH)]
        chunks = []
        for l in range(DEPTH):
            for st, ll, n in plans[l]:
                if st == "proj":
                    if n % 2 == 0:
                        chunks.append((st, ll, n // 2))
                elif st in ("ada", "wout"):
                    chunks.append((st, ll, n))
        order = {c: i for i, c in enumerate(chunks)}

        def chunk_src(c):
            st, l, n = c
            if st == "ada":
                return A["ada_w"][l, :, CW * n:CW * (n + 1)], CW
            if st == "wout":
                return A["w_out"][l, :, CW * n:CW * (n + 1)], CW
            c0, w = PROJ[n]
            return A["w_in"][l, :, c0:c0 + w], w

        def chunk_view(c):
            w = chunk_src(c)[1]
            return ab[order[c] % 2][:, 0:KT * w].rearrange("p (k c) -> p k c", k=KT)

        def chunk_here(eng, c):
            i = order[c]
            eng.wait_ge(s_ab[i % 2], 16 * (i // 2 + 1))

        def expert_src(l, slot, e):
            b = slot % 3
            if b < 2:
                return A["moe_w1" if b == 0 else "moe_w3"][l, e, :, :].rearrange("(k p) f -> p k f", p=P)
            return A["moe_w2"][l, e, :, :].rearrange("(k p) d -> p k d", p=P)

        def slot_view(s):
            if s % 3 < 2:
                return slots[s][:, :].rearrange("p (k f) -> p k f", k=KT)
            return slots[s][:, :].rearrange("p (k d) -> p k d", k=FT)

        block = ctx.enter_context(nc.Block())

        @block.sync
        def _(sp):
            def load_chunk(i):
                src, w = chunk_src(chunks[i])
                if i >= 2:
                    st, l, n = chunks[i - 2]
                    if st == "ada":
                        sp.wait_ge(S["ada_used"], NADA * l + n + 1)
                    elif st == "proj":
                        sp.wait_ge(S["proj"], 14 * l + 2 * n + 2)
                    else:
                        sp.wait_ge(S["wout"], 2 * l + n + 1)
                sp.dma_start(chunk_view(chunks[i]), src.rearrange("(k p) c -> p k c", p=P)).then_inc(s_ab[i % 2], 16)

            def wait_used(s, pairs):
                sp.wait_ge(S[("w1_used", "h13", "yt")[s % 3]], pairs)

            def load_pair0(l, s):
                if l > 0:
                    wait_used(s, NP_ * l)
                if s == 5:
                    sp.wait_ge(S["ada_col"], min(NADA * (l + 1) + NADA // 2, NADA * DEPTH))
                sp.dma_start(slot_view(s), expert_src(l, s, s // 3)).then_inc(s_slot[s], 16)

            at_chunk = 0
            for l in range(DEPTH):
                last = max(i for i, c in enumerate(chunks) if c[1] <= l or c in plans[l]) + 1
                pend = list(ORDER)
                if l + 1 < DEPTH:
                    last += 2
                else:
                    while len(pend) > 1:
                        load_pair0(l, pend.pop(0))
                while at_chunk < last:
                    load_chunk(at_chunk)
                    if chunks[at_chunk][0] == "proj" and chunks[at_chunk][2] >= 2 and len(pend) > 1:
                        load_pair0(l, pend.pop(0))
                    at_chunk += 1
                for s in pend:
                    load_pair0(l, s)
                with sp.Fori(1, NP_) as i:
                    for s in ORDER:
                        wait_used(s, i + NP_ * l)
                        sp.dma_start(slot_view(s), expert_src(l, s, i * 2 + s // 3)).then_inc(s_slot[s], 16)
                sp.wait_ge(S["posm"], l + 1)
                over = sp.value_load(flag[0:1, 0:1], min_val=0, max_val=1)
                O = OV[l]
                with sp.If(over):
                    for s in range(3):
                        wait_used(s, NP_ * (l + 1))
                    with sp.Fori(1, ROUNDS) as r:
                        with sp.Fori(0, E) as e:
                            sp.wait_ge(O["acc"], r + (r - 1) * E + e + 1)
                            for s in range(3):
                                sp.dma_start(slot_view(s), expert_src(l, s, e)).then_inc(O["w"], 16)
                    sp.wait_ge(O["acc"], ROUNDS + (ROUNDS - 1) * E)

        @block.gpsimd
        def _(pool):
            n_chain = [0]

            def link(ins):
                n_chain[0] += 1
                ins.then_inc(S["pool_chain"], 1)
                pool.wait_ge(S["pool_chain"], n_chain[0])

            pool.dma_start(rowsc[0:8, :], A["c_ctx"].rearrange("(k p) -> k p", p=P)).then_inc(S["rows_c_in"], 16)
            pool.dma_start(rowsc[8:16, :], A["c"].rearrange("o (k p) -> (o k) p", p=P)).then_inc(S["rows_c_in"], 16)
            nc.gpsimd.memset(cond[:, :, :], 0.0).then_inc(S["cond0"], 1)
            link(nc.gpsimd.memset(half[:, :], -0.5))
            link(nc.gpsimd.memset(w2gla[:, :], 0.0))
            link(nc.gpsimd.memset(lrT[:, :], 1.0))

            def params(l):
                pool.dma_start(rows[0:48, :], A["ada_b"][l].rearrange("(k p) -> k p", p=P)).then_inc(S["params_in"], 16)
                pool.dma_start(rows[48:56, :], A["norm1_g"][l].rearrange("(k p) -> k p", p=P)).then_inc(S["params_in"], 16)
                pool.dma_start(rows[56:64, :], A["norm2_g"][l].rearrange("(k p) -> k p", p=P)).then_inc(S["params_in"], 16)
                pool.dma_start(rows[64:68, :], A["sgu_b"][l]).then_inc(S["params_in"], 16)
                pool.dma_start(wst[:, :, :], A["sgu_w"][l].rearrange("g p q -> p g q")).then_inc(S["params_in"], 16)
                pool.dma_start(ckc[:, :, :], A["cache_k"][0, l].rearrange("h i t d -> t (h i) d")).then_inc(S["params_in"], 16)
                pool.dma_start(cvc[:, :, :], A["cache_v"][0, l].rearrange("h t d -> t h d")).then_inc(S["params_in"], 16)
                for a in range(2):
                    for b in range(2):
                        pool.dma_start(st0[64 * b:64 * b + 64, a, :, :],
                                       A["state_gla"][0, l, a, b::2].rearrange("h d v -> d h v")).then_inc(S["params_in"], 16)
                    pool.dma_start(w2gla[16 * a:16 * a + 16, 256 * a:256 * a + 256], A["gla_w2"][l, a]).then_inc(S["params_in"], 16)
                pool.dma_start(w2gla[32:33, :], A["gla_b"][l:l + 1].rearrange("o a c -> o (a c)")).then_inc(S["params_in"], 16)
                pool.dma_start(qkg[:, 0, :], A["q_norm_g"][l].partition_broadcast(P)).then_inc(S["params_in"], 16)
                pool.dma_start(qkg[:, 1, :], A["k_norm_g"][l].partition_broadcast(P)).then_inc(S["params_in"], 16)
                pool.dma_start(dg[:, :], A["diff_norm_g"][l].partition_broadcast(P)).then_inc(S["params_in"], 16)
                pool.dma_start(glag[:, :], A["gla_norm_g"][l].partition_broadcast(P)).then_inc(S["params_in"], 16)
                pool.dma_start(dlam[:, :, :], A["diff_lambda"][l].partition_broadcast(P)).then_inc(S["params_in"], 16)
            for l in range(DEPTH):
                if l == 0:
                    params(0)
                    pool.dma_start(rw[:, :, :], A["router_w"].rearrange("(k p) e -> p k e", p=P)).then_inc(S["params_in"], 16)
                    pool.dma_start(rbias[:, :], A["router_bias"].partition_broadcast(P)).then_inc(S["params_in"], 16)
                for st, ll, n in plans[l]:
                    if st == "glaD":
                        pool.wait_ge(S["qkt_gla_c"], 2 * (2 * l + n + 1))
                        nc.gpsimd.memset(attnT, 0.0).then_inc(S["zeroed"], 1)
                    elif st == "glaF":
                        pool.wait_ge(S["og_ms"], 2 * l + n + 1)
                        nc.gpsimd.tensor_tensor(sm(212, 4), sm(208, 4), half[:, :].to_broadcast([P, 4]), ALU.pow).then_inc(S["og_rs"], 1)
                    elif st == "pv":
                        pool.wait_ge(S["o_ms"], 2 * l + n + 1)
                        nc.gpsimd.tensor_tensor(sm(228, 4), sm(224, 4), half[:, :].to_broadcast([P, 4]), ALU.pow).then_inc(S["o_rs"], 1)
                    elif st == "qkn":
                        pool.wait_ge(S["qk_ms"], 2 * l + n + 1)
                        nc.gpsimd.tensor_tensor(sm(QRS, 16), sm(QMS, 16), half[:, :].to_broadcast([P, 16]), ALU.pow).then_inc(S["qk_rs"], 1)
                    elif st == "catT":
                        if n == 1:
                            pool.wait_ge(S["qk_done"], 2 * l + 1)
                            pool.dma_start(new_k[0, l].rearrange("h i t d -> t (h i) d"),
                                           pr[:, 0, BK:BK + 512].rearrange("p (g d) -> p g d", d=QK)).then_inc(S["kcache_out"], 16)
                            pool.wait_ge(S["ev"], 14 * (l + 1))
                            pool.dma_start(new_v[0, l].rearrange("h t d -> t h d"),
                                           pr[:, 0, BV:BV + 512].rearrange("p (h d) -> p h d", d=P)).then_inc(S["vcache_out"], 16)
                            for a in range(2):
                                for b in range(2):
                                    pool.dma_start(new_s[0, l, a, b::2].rearrange("h d v -> d h v"),
                                                   st2[64 * b:64 * b + 64, a, :, :]).then_inc(S["state_out"], 16)
                    elif st == "sguv":
                        pool.wait_ge(S["vms"], l + 1)
                        nc.gpsimd.tensor_tensor(sm(248, 8), sm(240, 8), half[:, :].to_broadcast([P, 8]), ALU.pow).then_inc(S["vrs"], 1)
                    elif st == "route" and l + 1 < DEPTH:
                        pool.wait_ge(S["posm"], l + 1)
                        params(l + 1)
            pool.wait_ge(S["kcache_out"], 16 * DEPTH)
            pool.wait_ge(S["vcache_out"], 16 * DEPTH)
            pool.wait_ge(S["state_out"], 64 * DEPTH)

        NPARAM = 21

        @block.scalar
        def _(act):
            n_chain = [0]

            def link(ins):
                n_chain[0] += 1
                ins.then_inc(S["act_chain"], 1)
                act.wait_ge(S["act_chain"], n_chain[0])

            def params_here(l):
                act.wait_ge(S["params_in"], 16 * (NPARAM - 2) * l + 16 * NPARAM)

            A_ = nc.scalar.activation
            act.dma_start(const[:, :], A["const"]).then_inc(S["const_in"], 16)
            act.dma_start(x_tok[:, 0, :], A["x_prompt"][0]).then_inc(S["x_in"], 16)
            act.dma_start(x_tok[:, 1, :], A["x_sample"][0]).then_inc(S["x_in"], 16)
            act.wait_ge(S["rowsc_t"], 1)
            act.wait_ge(S["cond0"], 1)
            A_(cond[:, :, 0:2].rearrange("p k s -> p s k"), PB[6][:, 128:144].rearrange("p (s k) -> p s k", s=2),
               ACT.Silu).then_inc(S["cond"], 1)
            for l in range(DEPTH):
                for st, ll, n in plans[l]:
                    g = 2 * l + n
                    if st == "xin":
                        for j in range(4):
                            if j % 2:
                                act.wait_ge(S["x_t"], j + 1)
                                A_(xT[:, 4 * (j % 2):4 * (j % 2) + 4, j // 2, :], PB[j][:, :].rearrange("p (k t) -> p k t", k=4),
                                   ACT.Copy).then_inc(S["x_tc"], 1)
                    elif st == "params":
                        act.wait_ge(S["lam"], 2 * l + 1)
                        A_(lam[:, 2:4], lam[:, 0:2], ACT.Exp).then_inc(S["lam"], 1)
                        act.wait_ge(S["wsT"], l + 1)
                        A_(wsT[:, :, :].rearrange("p g q -> p (g q)"), PB[4][:, :], ACT.Copy).then_inc(S["wsTc"], 1)
                    elif st == "ada":
                        m = NADA * ll + n
                        act.wait_ge(S["ada_used"], m + 1)
                        if m >= 2:
                            act.wait_ge(S["ada_col"], m - 1)
                        A_(adar[m % 2], PB[7][:, :], ACT.Copy).then_inc(S["ada_row"], 1)
                    elif st == "norm":
                        act.wait_ge(S["ss_ready"], g + 1)
                        A_(rsq[:, 0, :], PB[5][:, 0:NS * P], ACT.Sqrt, scale=1.0 / D, bias=EPS).then_inc(S["rstd_ready"], 1)
                        act.wait_ge(S["xn_ready"], g + 1)
                        for k in range(KT):
                            ins = A_(hb[:, k, 1, :], hb[:, k, 1, :], ACT.Identity, bias=mod[:, 24 * n + k, 1:2],
                                     scale=mod[:, 24 * n + 8 + k, 1:2])
                        ins.then_inc(S["ht_act"], 1)
                    elif st == "proj":
                        c, s = n // 2, n % 2
                        if c in BY_ACT or s == 1:
                            act.wait_ge(S["proj"], 14 * l + n + 1)
                            if n > 0:
                                act.wait_ge(S["ev"], 14 * l + n)
                            c0, w = PROJ[c]
                            A_(pr[:, s, c0:c0 + w], PB[2 * (c % 2) + s][:, 0:w],
                               ACT.Gelu_apprx_tanh if c0 == U0 else ACT.Copy).then_inc(S["ev"], 1)
                    elif st == "glaA":
                        act.wait_ge(S["lrt"], g + 1)
                        A_(lrT[0:32, :], PB[4][0:32, 0:P], ACT.Copy).then_inc(S["lrtc"], 1)
                    elif st == "glaB":
                        act.wait_ge(S["zz"], g + 1)
                        if n == 1:
                            act.wait_ge(S["og"], 2 * l + 1)
                        link(A_(ki, PB[5][:, :], ACT.Abs))
                        link(A_(ki, ki, ACT.Exp, scale=-1.0))
                        A_(ki, ki, ACT.Ln, bias=1.0).then_inc(S["lng"], 1)
                    elif st == "glaC":
                        act.wait_ge(S["cum"], g + 1)
                        A_(qd, PB[6][:, :], ACT.Exp)
                        A_(ki, PB[6][:, :], ACT.Exp, scale=-1.0)
                        A_(ke, PB[5][:, :], ACT.Exp)
                        A_(dec, PB[4][:, 0:8], ACT.Exp)
                        act.wait_ge(S["ev"], 14 * l + 6)
                        A_(sgtmp, pr[:, n, CR:CR + 256], ACT.Exp, scale=-1.0).then_inc(S["exps"], 1)
                    elif st == "glaD":
                        act.wait_ge(S["qkt_gla"], g + 1)
                        A_(qdT, PB[4][:, :], ACT.Copy).then_inc(S["qkt_gla_c"], 1)
                    elif st == "glaF":
                        act.wait_ge(S["og"], g + 1)
                        A_(ke[:, 0:256], PB[6][:, 0:256], ACT.Square).then_inc(S["og_sq"], 1)
                    elif st == "qkn":
                        act.wait_ge(S["ev"], 14 * l + 10)
                        if n == 1:
                            act.wait_ge(S["qk_ms"], 2 * l + 1)
                        A_(atT[0], pr[:, n, BQ:BQ + 1024], ACT.Square).then_inc(S["qk_sq"], 1)
                    elif st == "qkt":
                        if n == 0:
                            act.wait_ge(S["vms"], l + 1)
                        else:
                            act.wait_ge(S["sg_done"], 2 * l + 2)
                        act.wait_ge(S["qkT"], g + 1)
                        A_(atT[n][:, 0:512], PB[4 * n][:, :], ACT.Copy)
                        if n == 1:
                            A_(atT[1][:, 1024:1536], PB[5][:, :], ACT.Copy)
                        A_(atT[n][:, 512:1024], PB[(1, 6)[n]][:, :], ACT.Copy).then_inc(S["qkTc"], 1)
                    elif st == "sc":
                        act.wait_ge(S["nmax"], g + 1)
                        if n == 0:
                            act.wait_ge(S["og_done"], 2 * l + 2)
                        for m in range(8):
                            if n == 0:
                                src, dst = PB[2 + m // 4][:, P * (m % 4):P * (m % 4) + P], p0w[:, m, :]
                            else:
                                src = PB[SCB[m // 2]][:, 256 * (m % 2):256 * (m % 2) + 256]
                                dst = hb[:, m, :, :].rearrange("p s t -> p (s t)")
                            ins = A_(dst, src, ACT.Exp, bias=sm(SMX + 16 * n + m, 1), scale=QK ** -0.5, accum_out=sm(SSM + 16 * n + m, 1))
                        ins.then_inc(S["pexp"], 1)
                    elif st == "wt":
                        act.wait_ge(S["wT"], g + 1)
                        if n == 0:
                            A_(atT[0][:, 0:512], PB[2][:, :], ACT.Copy).then_inc(S["wTc"], 1)
                        else:
                            A_(pr[:, 1, BQ:BQ + 512], PB[0][:, :], ACT.Copy)
                            A_(pr[:, 1, BQ + 512:BQ + 1024], PB[1][:, :], ACT.Copy).then_inc(S["wTc"], 1)
                    elif st == "pv":
                        act.wait_ge(S["pv"], g + 1)
                        A_(atT[n][:, 512:1024], PB[3 + n][:, :], ACT.Square).then_inc(S["o_sq"], 1)
                    elif st == "catT":
                        act.wait_ge(S["catT"], 4 * l + 2 * n + 2)
                        act.wait_ge(S["wT"], 2 * l + 2)
                        A_(hb[:, 4:8, n, :], PB[CATB[2 * n + 1]][:, :].rearrange("p (k t) -> p k t", k=4), ACT.Copy).then_inc(S["catTc"], 1)
                    elif st == "route":
                        act.wait_ge(S["kcache_out"], 16 * (l + 1))
                        act.wait_ge(S["vcache_out"], 16 * (l + 1))
                        for j in range(4):
                            if j % 2:
                                act.wait_ge(S["htok"], 4 * l + j + 1)
                                A_(htok[:, j // 2, 512 * (j % 2):512 * (j % 2) + 512], PB[j][:, :], ACT.Copy).then_inc(S["htokc"], 1)
                        act.wait_ge(S["logit"], l + 1)
                        A_(sm(256, 32), PB[4][:, 0:32], ACT.Sigmoid).then_inc(S["aff"], 1)
                    elif st == "moe":
                        act.wait_ge(S["gat"], 2 * (9 * l) + 1)
                        A_(hg[:, 0:4, :], PB[0][:, :].rearrange("p (k c) -> p k c", k=4), ACT.Copy).then_inc(S["gat_a"], 1)
                        with act.Fori(0, NP_) as i:
                            v = i + NP_ * l
                            act.wait_ge(S["h13"], v + 1)
                            A_(sg1, PB[2][:, :], ACT.Silu).then_inc(S["silu"], 1)
                            act.wait_ge(S["gat"], (v + l) * 2 + 3)
                            A_(hg[:, 0:4, :], PB[0][:, :].rearrange("p (k c) -> p k c", k=4), ACT.Copy).then_inc(S["gat_a"], 1)
                            act.wait_ge(S["tr"], v + 1)
                            A_(hidT, PB[2][:, :].rearrange("p (f c) -> p f c", f=FT), ACT.Copy).then_inc(S["hidt"], 1)
                            act.wait_ge(S["tr_p"], v + 1)
                            A_(pgT, PB[3][:, 0:256], ACT.Copy).then_inc(S["pgt"], 1)
                            act.wait_ge(S["yt"], v + 1)
                            A_(ytok[:, 0:512], PB[4][:, :], ACT.Copy).then_inc(S["ytok_a"], 1)
                        act.wait_ge(S["posm"], l + 1)
                        over = act.value_load(flag[0:1, 0:1], min_val=0, max_val=1)
                        O = OV[l]
                        with act.If(over):
                            with act.Fori(1, ROUNDS) as r:
                                with act.Fori(0, E) as e:
                                    act.wait_ge(O["h13"], (r - 1) * E + e + 1)
                                    A_(sg1[0:CAP, :], PB[2][0:CAP, :], ACT.Silu).then_inc(O["silu"], 1)
            for j in range(4):
                if j % 2:
                    act.wait_ge(S["fin_t"], j + 1)
                    A_(x_tok[:, j // 2, 512 * (j % 2):512 * (j % 2) + 512], PB[j][:, :], ACT.Copy).then_inc(S["fin_c"], 1)
            act.wait_ge(S["fin_c"], 4)
            act.dma_start(y_p[0], x_tok[:, 0, :]).then_inc(S["y_out"], 16)
            act.dma_start(y_s[0], x_tok[:, 1, :]).then_inc(S["y_out"], 16)
            act.wait_ge(S["y_out"], 32)

        @block.tensor
        def _(pe):
            mm, tp = nc.tensor.matmul, nc.tensor.transpose

            def ada_columns(m):
                pe.wait_ge(S["ada_row"], m + 1)
                for t in range(4):
                    ins = mm(PB[7][:, 2 * t:2 * t + 2], adar[m % 2][:, P * t:P * t + P], const[:, C_SEL:C_SEL + 2],
                             start=True, stop=True)
                ins.then_inc(S["ada_col"], 1)

            pe.wait_ge(S["const_in"], 16)
            pe.wait_ge(S["rows_c_in"], 32)
            tp(PB[6][:, 128:144], rowsc[:, :], ident[0:16, 0:16]).then_inc(S["rowsc_t"], 1)
            for l in range(DEPTH):
                for st, ll, n in plans[l]:
                    g = 2 * l + n
                    if st == "xin":
                        pe.wait_ge(S["x_in"], 32)
                        for j in range(4):
                            for k in range(4):
                                ins = tp(PB[j][:, P * k:P * k + P], x_tok[:, j // 2, (4 * (j % 2) + k) * P:(4 * (j % 2) + k + 1) * P], ident)
                            ins.then_inc(S["x_t"], 1)
                    elif st == "params":
                        pe.wait_ge(S["params_in"], 16 * (NPARAM - 2) * l + 16 * NPARAM)
                        if l > 0:
                            pe.wait_ge(S["acc_end"], l)
                        pe.wait_ge(S["cond"], 1)
                        tp(PB[6][:, 0:NROWS], rows[:, :], ident[0:NROWS, 0:NROWS]).then_inc(S["rows_t"], 1)
                        for h in range(H):
                            ins = tp(PB[4][:, P * h:P * h + P], wst[:, h, :], ident)
                        ins.then_inc(S["wsT"], 1)
                    elif st == "ada":
                        c = (st, ll, n)
                        chunk_here(pe, c)
                        pe.wait_ge(S["cond"], 1)
                        m = NADA * ll + n
                        if m not in ADA_FIRST:
                            ada_columns(m - 1)
                        if m > 0:
                            pe.wait_ge(S["ada_colc"], m)
                        w = chunk_view(c)
                        for k in range(KT):
                            j = 32 * (k % 4)
                            ins = mm(PB[7][j:j + 32, :], cond[:, k, :], w[:, k, :], start=(k < 4), stop=(k >= 4))
                        ins.then_inc(S["ada_used"], 1)
                    elif st == "adaout":
                        ada_columns(NADA * ll + n)
                    elif st == "norm":
                        pe.wait_ge(S["sq_ready"], g + 1)
                        for k in range(KT):
                            ins = mm(PB[5][:, 0:NS * P], ones, hb[:, k, :, :].rearrange("p s t -> p (s t)"),
                                     start=(k == 0), stop=(k == KT - 1))
                        ins.then_inc(S["ss_ready"], 1)
                    elif st == "proj":
                        ci, s = n // 2, n % 2
                        c = (st, l, ci)
                        chunk_here(pe, c)
                        if n == 0:
                            pe.wait_ge(S["ht_dve"], 2 * l + 1)
                            pe.wait_ge(S["ht_act"], 2 * l + 1)
                        w = chunk_view(c)
                        if ci >= 2:
                            pe.wait_ge(S["ev"], 14 * l + n - 3)
                        for k in range(KT):
                            ins = mm(PB[2 * (ci % 2) + s][:, 0:PROJ[ci][1]], hb[:, k, s, :], w[:, k, :],
                                     start=(k == 0), stop=(k == KT - 1))
                        ins.then_inc(S["proj"], 1)
                    elif st == "glaA":
                        pe.wait_ge(S["ev"], 14 * l + 2)
                        pe.wait_ge(S["wsTc"], l + 1)
                        if n == 1:
                            pe.wait_ge(S["attn_m"], 2 * l + 1)
                        tp(PB[4][0:32, 0:P], pr[:, n, LR:LR + 32], ident).then_inc(S["lrt"], 1)
                    elif st == "glaB":
                        pe.wait_ge(S["lrtc"], g + 1)
                        if n == 1:
                            pe.wait_ge(S["st1"], 2 * l + 1)
                        mm(PB[5][:, :], lrT[:, :], w2gla[:, :], start=True, stop=True).then_inc(S["zz"], 1)
                    elif st == "glaC":
                        pe.wait_ge(S["gg"], g + 1)
                        if n == 1:
                            pe.wait_ge(S["og_done"], 2 * l + 1)
                        for d in range(2):
                            gd = g_sb[:, 256 * d:256 * d + 256]
                            mm(PB[6][:, 256 * d:256 * d + 256], const[:, (C_TRIF, C_TRIB)[d]:][:, 0:P], gd, start=True, stop=True)
                            mm(PB[5][:, 256 * d:256 * d + 256], const[:, (C_REMF, C_REMB)[d]:][:, 0:P], gd, start=True, stop=True)
                            for b in range(2):
                                q = 2 * d + b
                                ins = mm(PB[4][:, 2 * q:2 * q + 2], g_sb[:, P * q:P * q + P],
                                         const[:, C_CHUNK + d:C_CHUNK + d + 2], start=True, stop=True)
                        ins.then_inc(S["cum"], 1)
                    elif st == "glaD":
                        pe.wait_ge(S["qkd"], g + 1)
                        for q in range(4):
                            tp(PB[4][:, P * q:P * q + P], qd[:, P * q:P * q + P], ident)
                        for q in range(4):
                            ins = tp(PB[5][:, P * q:P * q + P], ki[:, P * q:P * q + P], ident)
                        ins.then_inc(S["qkt_gla"], 1)
                    elif st == "glaE":
                        pe.wait_ge(S["qkt_gla_c"], 2 * (g + 1))
                        for d in range(2):
                            for h in range(H):
                                b, q = 64 * (h % 2), P * (2 * d + h // 2)
                                ins = mm(PB[(6, 4)[h % 2]][:, 256 * d + P * (h // 2):256 * d + P * (h // 2) + P], kiT[b:b + 64, q:q + P], qdT[b:b + 64, q:q + P],
                                         start=True, stop=True)
                        ins.then_inc(S["attn"], 1)
                        for r in (0, 64):
                            for step in range(2):
                                d = step ^ (r // 64)
                                for h in range(H):
                                    b, col = 64 * (h % 2), 64 * (4 * step + 2 * d + h // 2)
                                    ins = mm(PB[5][b:b + 64, col:col + 64], ke[r:r + 64, 256 * d + 64 * h:256 * d + 64 * h + 64],
                                             pr[r:r + 64, n, CV + 64 * h:CV + 64 * h + 64], start=True, stop=True)
                            ins.then_inc(S["kv"], 1)
                            if r == 0:
                                pe.wait_ge(S["kv"], 2 * g + 1)
                    elif st == "glaF":
                        pe.wait_ge(S["attn_m"], g + 1)
                        pe.wait_ge(S["st1"], g + 1)
                        first = True
                        for h in range(H):
                            for d in range(2):
                                ins = mm(PB[6][:, 64 * h:64 * h + 64], attnT[:, P * (4 * d + h):P * (4 * d + h) + P],
                                   pr[:, n, CV + 64 * h:CV + 64 * h + 64], start=first, stop=False, skip_group_check=True)
                                first = False
                        for par in range(2):
                            ins.then_inc(S["o_part"], 1)
                            pe.wait_ge(S["o_part"], 2 * g + par + 1)
                            b = 64 * par
                            for h in range(par, H, 2):
                                for d in range(2):
                                    for step in range(n == 0, 2):
                                        r = 64 * (step ^ d)
                                        q = P * (2 * d + h // 2) + r
                                        state = (st0, st1)[step]
                                        ins = mm(PB[6][r:r + 64, 64 * h:64 * h + 64], qdT[b:b + 64, q:q + 64],
                                                 state[b:b + 64, d, h // 2, :], start=False, stop=(h >= 2), skip_group_check=True)
                        ins.then_inc(S["og"], 1)
                    elif st == "qkt":
                        pe.wait_ge(S["qk_done"], g + 1)
                        pe.wait_ge(S["ev"], 14 * (l + 1))
                        if n == 1:
                            pe.wait_ge(S["og_done"], 2 * l + 2)
                        for h in range(H):
                            tp(PB[4 * n][:, P * h:P * h + P], pr[:, n, BQ + P * h:BQ + P * h + P], ident)
                        if n == 1:
                            for h in range(H):
                                tp(PB[5][:, P * h:P * h + P], ckc[:, 2 * h:2 * h + 2, :].rearrange("p i d -> p (i d)"), ident)
                        for h in range(H):
                            ins = tp(PB[(1, 6)[n]][:, P * h:P * h + P], pr[:, n, BK + P * h:BK + P * h + P], ident)
                        ins.then_inc(S["qkT"], 1)
                    elif st == "sc":
                        pe.wait_ge(S["qkTc"], g + 1)
                        for m in range(8):
                            b, h = 64 * (m // 4), m % 4
                            q = atT[n][b:b + 64, P * h:P * h + P]
                            k = atT[n][b:b + 64, 512 + P * h:512 + P * h + P]
                            if n == 0:
                                ins = mm(PB[2 + m // 4][:, P * (m % 4):P * (m % 4) + P], q, k, start=True, stop=True)
                            else:
                                kc = atT[n][b:b + 64, 1024 + P * h:1024 + P * h + P]
                                mm(PB[SCB[m // 2]][:, 256 * (m % 2):256 * (m % 2) + P], q, kc, start=True, stop=True)
                                ins = mm(PB[SCB[m // 2]][:, 256 * (m % 2) + P:256 * (m % 2) + 2 * P], q, k, start=True, stop=True)
                        ins.then_inc(S["sc"], 1)
                    elif st == "wt":
                        pe.wait_ge(S["wmix"], g + 1)
                        for h in range(H):
                            if n == 0:
                                ins = tp(PB[2][:, P * h:P * h + P], p0w[:, h, :], ident)
                            else:
                                for j in range(2):
                                    ins = tp(PB[h // 2][:, 256 * (h % 2) + P * j:256 * (h % 2) + P * j + P], hb[:, h, j, :], ident)
                        ins.then_inc(S["wT"], 1)
                    elif st == "pv":
                        pe.wait_ge(S["wTc"], g + 1)
                        for h in range(H):
                            o = PB[3 + n][:, P * h:P * h + P]
                            v = pr[:, n, BV + P * h:BV + P * h + P]
                            if n == 0:
                                ins = mm(o, atT[0][:, P * h:P * h + P], v, start=True, stop=True)
                            else:
                                mm(o, pr[:, 1, BQ + 256 * h:BQ + 256 * h + P], cvc[:, h, :], start=True, stop=False)
                                ins = mm(o, pr[:, 1, BQ + 256 * h + P:BQ + 256 * h + 2 * P], v, start=False, stop=True)
                        ins.then_inc(S["pv"], 1)
                    elif st == "sgu":
                        pe.wait_ge(S["qkTc"], 2 * l + 2)
                        pe.wait_ge(S["v_done"], l + 1)
                        for h in range(H):
                            ins = mm(PB[6][:, P * h:P * h + P], wsT[:, h, :], pr[:, :, V0 + 64 * h:V0 + 64 * h + 64],
                                     start=True, stop=True)
                        ins.then_inc(S["sgu_s"], 1)
                    elif st == "catT":
                        pe.wait_ge(S["ob_done"], 2 * l + n + 1)
                        pe.wait_ge(S["og_done"], 2 * l + n + 1)
                        pe.wait_ge(S["sgu_done"], l + 1)
                        for j in (2 * n, 2 * n + 1):
                            for k in range(4):
                                m = 4 * (j % 2) + k
                                c0 = (U0, U0 + P, BQ, BQ + P, BQ + 2 * P, BQ + 3 * P, CQ, CQ + P)[m]
                                ins = tp(PB[CATB[j]][:, P * k:P * k + P], pr[:, n, c0:c0 + P], ident)
                            ins.then_inc(S["catT"], 1)
                    elif st == "wout":
                        c = (st, l, n)
                        chunk_here(pe, c)
                        pe.wait_ge(S["catTc"], 4 * (l + 1))
                        w = chunk_view(c)
                        for t in range(4):
                            for m in range(KT):
                                ins = mm(PB[(4, 0)[n] + t // 2][:, 256 * (t % 2):256 * (t % 2) + 256], w[:, m, P * t:P * t + P],
                                         hb[:, m, :, :].rearrange("p s t -> p (s t)"), start=(m == 0), stop=(m == KT - 1))
                        ins.then_inc(S["wout"], 1)
                    elif st == "routeA":
                        pe.wait_ge(S["ht_dve"], 2 * l + 2)
                        pe.wait_ge(S["ht_act"], 2 * l + 2)
                        pe.wait_ge(S["xadd"], 2 * (l + 1))
                        for s in range(NS):
                            for k in range(KT):
                                ins = mm(PB[4][:, E * s:E * s + E], hb[:, k, s, :], rw[:, k, :], start=(k == 0), stop=(k == KT - 1))
                        ins.then_inc(S["logit"], 1)
                        for j in range(4):
                            for k in range(4):
                                ins = tp(PB[j][:, P * k:P * k + P], hb[:, 4 * (j % 2) + k, j // 2, :], ident)
                            ins.then_inc(S["htok"], 1)
                    elif st == "route":
                        pe.wait_ge(S["mask"], l + 1)
                        m = sm(288, 32)
                        mm(PB[4][:, 32:48], const[:, C_STRICT:C_STRICT + P], m[:, 0:16], start=True, stop=True)
                        mm(PB[4][:, 48:64], ones, m[:, 0:16], start=True, stop=False)
                        mm(PB[4][:, 48:64], const[:, C_STRICT:C_STRICT + P], m[:, 16:32], start=False, stop=True)
                        mm(PB[4][:, 64:80], ones, m[:, 0:16], start=True, stop=False)
                        mm(PB[4][:, 64:80], ones, m[:, 16:32], start=False, stop=True).then_inc(S["pos"], 1)
                    elif st == "moe":
                        def gather(b):
                            for k in range(4):
                                for s in range(NS):
                                    ins = mm(PB[b][:, P * k:P * k + P], htok[:, s, P * (4 * b + k):P * (4 * b + k) + P], pm[:, s, :],
                                             start=(s == 0), stop=(s == NS - 1))
                            ins.then_inc(S["gat"], 1)

                        pe.wait_ge(S["htokc"], 4 * (l + 1))
                        pe.wait_ge(S["pmat"], 9 * l + 1)
                        gather(0)
                        gather(1)

                        def scatter(v):
                            pe.wait_ge(S["ytok_a"], v)
                            pe.wait_ge(S["ytok_d"], v)
                            pe.wait_ge(S["pgt"], v)
                            for t in range(KT):
                                b = (6, 7, 0, 1)[t // 2]
                                ins = mm(PB[b][:, 256 * (t % 2):256 * (t % 2) + 256], ytok[:, P * t:P * t + P], pgT, start=True, stop=True)
                                if t % 4 == 3:
                                    ins.then_inc(S["scat"], 1)

                        with pe.Fori(0, NP_) as i:
                            v = i + NP_ * l
                            pe.wait_ge(S["gat_a"], v + l + 1)
                            pe.wait_ge(S["gat_d"], v + l + 1)
                            pe.wait_ge(S["pgt"], v + l + 1)
                            for b in range(2):
                                for a in range(2):
                                    pe.wait_ge(s_slot[3 * a + b], (v + 1) * 16)
                                for k in range(KT):
                                    for a in range(2):
                                        ins = mm(PB[2 + b][CAP * a:CAP * a + CAP, :], hg[:, k, CAP * a:CAP * a + CAP],
                                                 slot_view(3 * a + b)[:, k, :], start=(k == 0), stop=(k == KT - 1))
                                ins.then_inc(S["w1_used" if b == 0 else "h13"], 1)
                            pe.wait_ge(S["pmat"], v + l + 2)
                            pe.wait_ge(S["acc_d"], v * 2 + 3 * l + 1)
                            gather(0)
                            gather(1)
                            pe.wait_ge(S["hid"], v + 1)
                            for f in range(FT):
                                ins = tp(PB[2][:, P * f:P * f + P], hid[:, P * f:P * f + P], ident)
                            ins.then_inc(S["tr"], 1)
                            pe.wait_ge(S["gat_a"], v + l + 2)
                            pe.wait_ge(S["gat_d"], v + l + 2)
                            scatter(v + l + 1)
                            for s in range(NS):
                                ins = tp(PB[3][:, P * s:P * s + P], pg[:, s, :], ident)
                            ins.then_inc(S["tr_p"], 1)
                            pe.wait_ge(S["hidt"], v + 1)
                            for a in range(2):
                                pe.wait_ge(s_slot[3 * a + 2], (v + 1) * 16)
                            for c in range(2):
                                for f in range(FT):
                                    for a in range(2):
                                        ins = mm(PB[4 + c][CAP * a:CAP * a + CAP, :], hidT[:, f, CAP * a:CAP * a + CAP],
                                                 slot_view(3 * a + 2)[:, f, CW * c:CW * c + CW], start=(f == 0), stop=(f == FT - 1))
                            ins.then_inc(S["yt"], 1)
                        pe.wait_ge(S["acc_d"], 2 * NP_ * (l + 1) + 3 * l + 1)
                        scatter((NP_ + 1) * (l + 1))
                        pe.wait_ge(S["posm"], l + 1)
                        over = pe.value_load(flag[0:1, 0:1], min_val=0, max_val=1)
                        O = OV[l]
                        with pe.If(over):
                            with pe.Fori(1, ROUNDS) as r:
                                with pe.Fori(0, E) as e:
                                    q = (r - 1) * E + e
                                    pe.wait_ge(O["p"], q + 1)
                                    for k in range(KT):
                                        for s in range(NS):
                                            ins = mm(PB[0][:, CAP * k:CAP * k + CAP], htok[:, s, P * k:P * k + P], pm[:, s, 0:CAP],
                                                     start=(s == 0), stop=(s == NS - 1))
                                    ins.then_inc(O["gat"], 1)
                                    pe.wait_ge(O["gat_c"], q + 1)
                                    pe.wait_ge(O["w"], (q + 1) * 48)
                                    for b in range(2):
                                        for k in range(KT):
                                            ins = mm(PB[2 + b][0:CAP, :], hg[:, k, 0:CAP], slot_view(b)[:, k, :],
                                                     start=(k == 0), stop=(k == KT - 1))
                                    ins.then_inc(O["h13"], 1)
                                    pe.wait_ge(O["hid"], q + 1)
                                    for f in range(FT):
                                        ins = tp(PB[2][:, P * f:P * f + P], hid[:, P * f:P * f + P], ident)
                                    ins.then_inc(O["tr"], 1)
                                    pe.wait_ge(O["hidt"], q + 1)
                                    for c in range(2):
                                        for f in range(FT):
                                            ins = mm(PB[4 + c][0:CAP, :], hidT[:, f, 0:CAP], slot_view(2)[:, f, CW * c:CW * c + CW],
                                                     start=(f == 0), stop=(f == FT - 1))
                                    ins.then_inc(O["yt"], 1)
                                    for s in range(NS):
                                        ins = tp(PB[3][:, P * s:P * s + P], pg[:, s, :], ident)
                                    ins.then_inc(O["tr_p"], 1)
                                    pe.wait_ge(O["tr_c"], q + 1)
                                    for t in range(KT):
                                        ins = mm(PB[(6, 7, 0, 1)[t // 2]][:, 256 * (t % 2):256 * (t % 2) + 256], ytok[0:CAP, P * t:P * t + P],
                                                 pgT[0:CAP, :], start=True, stop=True)
                                    ins.then_inc(O["scat"], 1)
            pe.wait_ge(S["acc_end"], DEPTH)
            for j in range(4):
                for k in range(4):
                    ins = tp(PB[j][:, P * k:P * k + P], xT[:, 4 * (j % 2) + k, j // 2, :], ident)
                ins.then_inc(S["fin_t"], 1)

        @block.vector
        def _(dve):
            v_ = nc.vector
            n_chain = [0]

            def link(ins):
                n_chain[0] += 1
                ins.then_inc(S["dve_chain"], 1)
                dve.wait_ge(S["dve_chain"], n_chain[0])

            def ada_copy(m):
                dve.wait_ge(S["ada_col"], m + 1)
                c = 4 * (m % NADA)
                v_.tensor_copy(ada[:, c:c + 4, :].rearrange("p c s -> p (c s)"), PB[7][:, 0:8]).then_inc(S["ada_colc"], 1)

            def bc(ap, shape):
                return ap.to_broadcast(shape)

            link(v_.memset(posm[:, :, :], -1.0))
            link(v_.memset(gates[:, :, :], 0.0))
            dve.wait_ge(S["const_in"], 16)
            for l in range(DEPTH):
                lam_init = 0.8 - 0.6 * math.exp(-0.3 * l)
                for st, ll, n in plans[l]:
                    g = 2 * l + n
                    if st == "xin":
                        for j in range(4):
                            if j % 2 == 0:
                                dve.wait_ge(S["x_t"], j + 1)
                                v_.tensor_copy(xT[:, 4 * (j % 2):4 * (j % 2) + 4, j // 2, :],
                                               PB[j][:, :].rearrange("p (k t) -> p k t", k=4)).then_inc(S["x_tc"], 1)
                        dve.wait_ge(S["x_tc"], 4)
                    elif st == "params":
                        dve.wait_ge(S["params_in"], 16 * (NPARAM - 2) * l + 16 * NPARAM)
                        link(v_.tensor_tensor(sm(320, 128).rearrange("p (a d) -> p a d", a=2), dlam[:, 0::2, :], dlam[:, 1::2, :], ALU.mult))
                        v_.tensor_reduce(lam[:, 0:2], sm(320, 128).rearrange("p (a d) -> p a d", a=2), X, ALU.add).then_inc(S["lam"], 1)
                        dve.wait_ge(S["lam"], 2 * l + 2)
                        link(v_.tensor_tensor(lam[:, 4:5], lam[:, 3:4], lam[:, 2:3], ALU.subtract))
                        link(v_.tensor_scalar(lam[:, 5:6], lam[:, 4:5], -lam_init, None, ALU.add))
                        link(v_.tensor_scalar(dg[:, :], dg[:, :], 1.0 - lam_init, None, ALU.mult))
                        dve.wait_ge(S["rows_t"], l + 1)
                        link(v_.tensor_copy(cols[:, :], PB[6][:, 0:NROWS]))
                    elif st == "ada":
                        if NADA * ll + n not in ADA_FIRST:
                            ada_copy(NADA * ll + n - 1)
                    elif st == "adaout":
                        ada_copy(NADA * ll + n)
                    elif st == "mod":
                        dve.wait_ge(S["ada_colc"], NADA * l + NADA // 2 * (n + 1))
                        link(v_.tensor_tensor(mod[:, 24 * n:24 * n + 24, :], ada[:, 24 * n:24 * n + 24, :],
                                              bc(cols[:, 24 * n:24 * n + 24].unsqueeze(2), [P, 24, 2]), ALU.add))
                        m = mod[:, 24 * n + 8:24 * n + 16, :]
                        link(v_.tensor_scalar(m, m, 1.0, None, ALU.add))
                        v_.tensor_tensor(m, m, bc(cols[:, 48 + 8 * n:56 + 8 * n].unsqueeze(2), [P, 8, 2]), ALU.mult).then_inc(S["mod_ready"], 1)
                        dve.wait_ge(S["mod_ready"], g + 1)
                    elif st == "norm":
                        v_.tensor_tensor(hb[:, :, :, :], xT[:, :, :, :], xT[:, :, :, :], ALU.mult).then_inc(S["sq_ready"], 1)
                        dve.wait_ge(S["rstd_ready"], g + 1)
                        link(v_.reciprocal(rsq[:, 1, :], rsq[:, 0, :]))
                        v_.tensor_tensor(hb[:, :, :, :].rearrange("p k s t -> p k (s t)"), xT[:, :, :, :].rearrange("p k s t -> p k (s t)"),
                                         bc(rsq[:, 1:2, :], [P, KT, 256]), ALU.mult).then_inc(S["xn_ready"], 1)
                        dve.wait_ge(S["xn_ready"], g + 1)
                        for k in range(KT):
                            ins = v_.tensor_scalar(hb[:, k, 0, :], hb[:, k, 0, :], mod[:, 24 * n + 8 + k, 0:1],
                                                   mod[:, 24 * n + k, 0:1], ALU.mult, ALU.add)
                        ins.then_inc(S["ht_dve"], 1)
                    elif st == "proj":
                        c = n // 2
                        if c not in BY_ACT and n % 2 == 0:
                            dve.wait_ge(S["proj"], 14 * l + n + 1)
                            if n > 0:
                                dve.wait_ge(S["ev"], 14 * l + n)
                            c0, w = PROJ[c]
                            v_.tensor_copy(pr[:, 0, c0:c0 + w], PB[2 * (c % 2)][:, 0:w]).then_inc(S["ev"], 1)
                    elif st == "glaB":
                        dve.wait_ge(S["lng"], g + 1)
                        v_.scalar_tensor_tensor(out=g_sb, in0=PB[5][:, :], scalar=0.0, in1=ki, op0=ALU.min,
                                                op1=ALU.subtract).then_inc(S["gg"], 1)
                    elif st == "glaC":
                        dve.wait_ge(S["exps"], g + 1)
                        dve.wait_ge(S["ev"], 14 * l + 6)
                        q = bc(pr[:, n, CQ:CQ + 256].unsqueeze(1), [P, 2, 256])
                        k = bc(pr[:, n, CK:CK + 256].unsqueeze(1), [P, 2, 256])
                        v3 = [t.rearrange("p (a c) -> p a c", a=2) for t in (qd, ki, ke)]
                        v_.scalar_tensor_tensor(out=v3[0], in0=v3[0], scalar=QK ** -0.5, in1=q, op0=ALU.mult, op1=ALU.mult)
                        v_.tensor_tensor(v3[1], v3[1], k, ALU.mult)
                        v_.tensor_tensor(v3[2], v3[2], k, ALU.mult).then_inc(S["qkd"], 1)
                        sgt = pr[:, n, CR:CR + 256]
                        link(v_.tensor_scalar(sgtmp, sgtmp, 1.0, None, ALU.add))
                        link(v_.reciprocal(sgtmp, sgtmp))
                        v_.tensor_tensor(sgt, sgt, sgtmp, ALU.mult).then_inc(S["sg_done"], 1)
                        dve.wait_ge(S["sg_done"], g + 1)
                        s3 = sgt.rearrange("p (h d) -> p h d", h=H)
                        link(v_.tensor_tensor(s3, s3, bc(glag[:, :].unsqueeze(1), [P, H, 64]), ALU.mult))
                    elif st == "glaD":
                        dve.wait_ge(S["qkt_gla"], g + 1)
                        v_.tensor_copy(kiT, PB[5][:, :]).then_inc(S["qkt_gla_c"], 1)
                    elif st == "glaE":
                        dve.wait_ge(S["attn"], g + 1)
                        dve.wait_ge(S["zeroed"], g + 1)
                        for d in range(2):
                            mask = const[:, (C_TRIF, C_TRIB)[d]:][:, 0:P].bitcast(I32)
                            for par in range(2):
                                ins = v_.copy_predicated(attnT[:, 512 * d:512 * d + 512].rearrange("p (h r i) -> p h r i", r=2, i=P)[:, :, par],
                                                         bc(mask.unsqueeze(1), [P, 2, P]),
                                                         PB[(6, 4)[par]][:, 256 * d:256 * d + 256].rearrange("p (h i) -> p h i", h=2))
                        ins.then_inc(S["attn_m"], 1)
                        dve.wait_ge(S["kv"], 2 * g + 2)
                        if n == 0 and l > 0:
                            dve.wait_ge(S["state_out"], 64 * l)
                        kvb = PB[5][:, :].rearrange("p (s a b v) -> p s (a b) v", s=2, a=2, b=2)
                        d3 = dec.rearrange("p (q s) -> p q s", s=2)
                        s0v, s1v, s2v = (t.rearrange("p a b v -> p (a b) v") for t in (st0[:, :, :, :], st1, st2))
                        if n == 0:
                            link(v_.tensor_copy(s1v, kvb[:, 0]))
                            link(v_.tensor_tensor(s2v, s1v, bc(d3[:, :, 1:2], [P, 4, 64]), ALU.mult))
                            v_.tensor_tensor(s2v, s2v, kvb[:, 1], ALU.add).then_inc(S["st1"], 1)
                        else:
                            link(v_.tensor_tensor(s1v, s0v, bc(d3[:, :, 0:1], [P, 4, 64]), ALU.mult))
                            v_.tensor_tensor(s1v, s1v, kvb[:, 0], ALU.add).then_inc(S["st1"], 1)
                    elif st == "glaF":
                        dve.wait_ge(S["og_sq"], g + 1)
                        link(v_.tensor_reduce(sm(204, 4), ke[:, 0:256].rearrange("p (h d) -> p h d", h=H), X, ALU.add))
                        v_.tensor_scalar(sm(208, 4), sm(204, 4), 1.0 / 64, EPS, ALU.mult, ALU.add).then_inc(S["og_ms"], 1)
                        dve.wait_ge(S["og_rs"], g + 1)
                        for h in range(H):
                            ins = v_.scalar_tensor_tensor(out=pr[:, n, CQ + 64 * h:CQ + 64 * h + 64], in0=PB[6][:, 64 * h:64 * h + 64],
                                                          scalar=sm(212 + h, 1), in1=pr[:, n, CR + 64 * h:CR + 64 * h + 64], op0=ALU.mult, op1=ALU.mult)
                        ins.then_inc(S["og_done"], 1)
                    elif st == "qkn":
                        dve.wait_ge(S["qk_sq"], g + 1)
                        qk16 = pr[:, n, BQ:BQ + 1024].rearrange("p (g d) -> p g d", d=64)
                        link(v_.tensor_reduce(sm(SSQ, 16), atT[0].rearrange("p (g d) -> p g d", d=64), X, ALU.add))
                        v_.tensor_scalar(sm(QMS, 16), sm(SSQ, 16), 1.0 / 64, EPS, ALU.mult, ALU.add).then_inc(S["qk_ms"], 1)
                        dve.wait_ge(S["qk_rs"], g + 1)
                        link(v_.tensor_tensor(qk16, qk16, bc(sm(QRS, 16).unsqueeze(2), [P, 16, 64]), ALU.mult))
                        qk4 = pr[:, n, BQ:BQ + 1024].rearrange("p (a g d) -> p a g d", a=2, d=64)
                        ins = v_.tensor_tensor(qk4, qk4, bc(qkg[:, :, :].unsqueeze(2), [P, 2, 8, 64]), ALU.mult)
                        if n == 0:
                            ins.then_inc(S["qk_done"], 1)
                        else:
                            link(ins)
                            tmp = atT[0]
                            x5 = pr[:, 1, BQ:BQ + 1024].rearrange("p (g h a f) -> p g h a f", g=16, h=2, a=2)
                            t5 = tmp.rearrange("p (g h a f) -> p g h a f", g=16, h=2, a=2)
                            sn = const[:, C_SIN:C_SIN + 64].rearrange("p (h a f) -> p h a f", h=2, a=2)
                            for a in range(2):
                                ins = v_.tensor_tensor(t5[:, :, :, a, :], x5[:, :, :, 1 - a, :],
                                                       bc(sn[:, :, a, :].unsqueeze(1), [P, 16, 2, 16]), ALU.mult)
                            link(ins)
                            link(v_.tensor_tensor(qk16, qk16, bc(const[:, C_COS:C_COS + 64].unsqueeze(1), [P, 16, 64]), ALU.mult))
                            v_.tensor_tensor(pr[:, 1, BQ:BQ + 1024], pr[:, 1, BQ:BQ + 1024], tmp, ALU.add).then_inc(S["qk_done"], 1)
                    elif st == "sc":
                        dve.wait_ge(S["sc"], g + 1)
                        for b in range(2 if n == 0 else 4):
                            w = 4 if n == 0 else 2
                            ins = v_.tensor_reduce(sm(SMX + 16 * n + 8 + w * b, w), PB[(2 + b if n == 0 else SCB[b])][:, :].rearrange("p (m k) -> p m k", m=w),
                                                   X, ALU.max)
                        link(ins)
                        v_.tensor_scalar(sm(SMX + 16 * n, 8), sm(SMX + 16 * n + 8, 8), -(QK ** -0.5), None, ALU.mult).then_inc(S["nmax"], 1)
                    elif st == "mix":
                        dve.wait_ge(S["pexp"], g + 1)
                        sums = SSM + 16 * n
                        link(v_.reciprocal(sm(sums + 8, 8), sm(sums, 8)))
                        r2 = sm(sums + 12, 4)
                        link(v_.tensor_scalar(r2, r2, lam[:, 5:6], None, ALU.mult))

                        def pw(m):
                            if n == 0:
                                return p0w[:, m, :]
                            return hb[:, m, :, :].rearrange("p s t -> p (s t)")
                        for h in range(H):
                            ins = v_.tensor_scalar(pw(h), pw(h), sm(sums + 8 + h, 1), None, ALU.mult)
                        link(ins)
                        for h in range(H):
                            ins = v_.scalar_tensor_tensor(out=pw(h), in0=pw(4 + h), scalar=sm(sums + 12 + h, 1), in1=pw(h),
                                                          op0=ALU.mult, op1=ALU.add)
                        ins.then_inc(S["wmix"], 1)
                    elif st == "pv":
                        dve.wait_ge(S["o_sq"], g + 1)
                        link(v_.tensor_reduce(sm(220, 4), atT[n][:, 512:1024].rearrange("p (h d) -> p h d", h=H), X, ALU.add))
                        v_.tensor_scalar(sm(224, 4), sm(220, 4), 1.0 / P, EPS, ALU.mult, ALU.add).then_inc(S["o_ms"], 1)
                        dve.wait_ge(S["o_rs"], g + 1)
                        for h in range(H):
                            ins = v_.scalar_tensor_tensor(out=pr[:, n, BQ + P * h:BQ + P * h + P], in0=PB[3 + n][:, P * h:P * h + P],
                                                          scalar=sm(228 + h, 1), in1=dg[:, :], op0=ALU.mult, op1=ALU.mult)
                        ins.then_inc(S["ob_done"], 1)
                    elif st == "sguv":
                        dve.wait_ge(S["ev"], 14 * l + 12)
                        v4 = pr[:, :, V0:V0 + 256]
                        tmp = at[:, 0:512].rearrange("p (s c) -> p s c", s=2)
                        link(v_.tensor_tensor(tmp, v4, v4, ALU.mult))
                        link(v_.tensor_reduce(sm(232, 8), tmp.rearrange("p s (g c) -> p (s g) c", c=64), X, ALU.add))
                        v_.tensor_scalar(sm(240, 8), sm(232, 8), 1.0 / 64, EPS, ALU.mult, ALU.add).then_inc(S["vms"], 1)
                        dve.wait_ge(S["vrs"], l + 1)
                        v5 = v4.rearrange("p s (g c) -> p s g c", c=64)
                        v_.tensor_tensor(v5, v5, bc(sm(248, 8).rearrange("p (s g) -> p s g", s=2).unsqueeze(3), [P, 2, 4, 64]),
                                         ALU.mult).then_inc(S["v_done"], 1)
                    elif st == "sgu":
                        dve.wait_ge(S["sgu_s"], l + 1)
                        for h in range(H):
                            u = pr[:, :, U0 + 64 * h:U0 + 64 * h + 64]
                            ins = v_.scalar_tensor_tensor(out=u, in0=PB[6][:, P * h:P * h + P].rearrange("p (s c) -> p s c", s=2),
                                                          scalar=cols[:, 64 + h:65 + h], in1=u, op0=ALU.add, op1=ALU.mult)
                        ins.then_inc(S["sgu_done"], 1)
                    elif st == "catT":
                        dve.wait_ge(S["catT"], 4 * l + 2 * n + 1)
                        dve.wait_ge(S["wT"], 2 * l + 2)
                        v_.tensor_copy(hb[:, 0:4, n, :], PB[CATB[2 * n]][:, :].rearrange("p (k t) -> p k t", k=4)).then_inc(S["catTc"], 1)
                    elif st == "wout":
                        dve.wait_ge(S["wout"], 2 * l + n + 1)
                        for t in range(4):
                            for s in range(NS):
                                k = 4 * n + t
                                ins = v_.scalar_tensor_tensor(out=xT[:, k, s, :], in0=PB[(4, 0)[n] + t // 2][:, 256 * (t % 2) + P * s:256 * (t % 2) + P * s + P],
                                                              scalar=mod[:, 16 + k, s:s + 1], in1=xT[:, k, s, :], op0=ALU.mult, op1=ALU.add)
                        ins.then_inc(S["xadd"], 1)
                        dve.wait_ge(S["xadd"], 2 * l + n + 1)
                    elif st == "route":
                        dve.wait_ge(S["kcache_out"], 16 * (l + 1))
                        dve.wait_ge(S["vcache_out"], 16 * (l + 1))
                        dve.wait_ge(S["state_out"], 64 * (l + 1))
                        for j in range(4):
                            if j % 2 == 0:
                                dve.wait_ge(S["htok"], 4 * l + j + 1)
                                v_.tensor_copy(htok[:, j // 2, 0:512], PB[j][:, :]).then_inc(S["htokc"], 1)
                        dve.wait_ge(S["aff"], l + 1)
                        aff = sm(256, 32)
                        sel = sm(320, 32)
                        msk = sm(288, 32)
                        tmp, tmp2 = rsq[:, 0, 0:128], rsq[:, 1, 0:128]
                        link(v_.tensor_tensor(sel.rearrange("p (s e) -> p s e", s=2), aff.rearrange("p (s e) -> p s e", s=2),
                                              bc(rbias[:, :].unsqueeze(1), [P, 2, E]), ALU.add))

                        def before(vals, n_, out):
                            i_ = bc(vals.unsqueeze(2), [P, n_, 4, 4])
                            j_ = bc(vals.unsqueeze(3), [P, n_, 4, 4])
                            a = tmp[:, 0:16 * n_].rearrange("p (n j i) -> p n j i", j=4, i=4)
                            b = tmp2[:, 0:16 * n_].rearrange("p (n j i) -> p n j i", j=4, i=4)
                            low = bc(const[:, C_LOWER:C_LOWER + 16].rearrange("p (j i) -> p j i", j=4).unsqueeze(1), [P, n_, 4, 4])
                            v_.tensor_tensor(a, i_, j_, ALU.is_gt)
                            link(v_.tensor_tensor(b, i_, j_, ALU.is_ge))
                            link(v_.tensor_tensor(b, b, low, ALU.mult))
                            link(v_.tensor_tensor(a, a, b, ALU.max))
                            link(v_.tensor_reduce(out, a, X, ALU.add))

                        sel4 = sel.rearrange("p (n e) -> p n e", e=4)
                        rank = sm(352, 32).rearrange("p (n e) -> p n e", e=4)
                        before(sel4, 8, rank)
                        pairs = sm(384, 48).rearrange("p (n c) -> p n c", c=6)
                        v_.tensor_tensor(pairs[:, :, 0:3], sel4[:, :, 0:3], sel4[:, :, 1:4], ALU.add)
                        v_.tensor_tensor(pairs[:, :, 3:5], sel4[:, :, 0:2], sel4[:, :, 2:4], ALU.add)
                        link(v_.tensor_tensor(pairs[:, :, 5:6], sel4[:, :, 0:1], sel4[:, :, 3:4], ALU.add))
                        grp = sm(432, 8)
                        link(v_.tensor_reduce(grp, pairs, X, ALU.max))
                        gr = sm(440, 8)
                        before(grp.rearrange("p (s g) -> p s g", s=2), 2, gr.rearrange("p (s g) -> p s g", s=2))
                        m4 = msk.rearrange("p (n e) -> p n e", e=4)
                        link(v_.tensor_scalar(gr, gr, 0.5, None, ALU.is_lt))
                        link(v_.tensor_scalar(m4, rank, 1.5, None, ALU.is_lt))
                        v_.tensor_tensor(m4, m4, bc(gr.unsqueeze(2), [P, 8, 4]), ALU.mult).then_inc(S["mask"], 1)
                        dve.wait_ge(S["mask"], l + 1)
                        gt = gates[:, :, 0:E]
                        a2, k2 = aff.rearrange("p (s e) -> p s e", s=2), msk.rearrange("p (s e) -> p s e", s=2)
                        link(v_.tensor_tensor(gt, a2, k2, ALU.mult))
                        link(v_.tensor_reduce(sm(320, 2), gt, X, ALU.add))
                        link(v_.reciprocal(sm(322, 2), sm(320, 2)))
                        link(v_.tensor_tensor(gt, gt, bc(sm(322, 2).unsqueeze(2), [P, 2, E]), ALU.mult))
                        dve.wait_ge(S["pos"], l + 1)
                        link(v_.tensor_scalar(posm[:, :, 0:E], PB[4][:, 32:64].rearrange("p (s e) -> p s e", s=2), 1.0, None, ALU.add))
                        link(v_.tensor_tensor(posm[:, :, 0:E], posm[:, :, 0:E], k2, ALU.mult))
                        link(v_.tensor_scalar(posm[:, :, 0:E], posm[:, :, 0:E], -1.0, None, ALU.add))
                        link(v_.tensor_reduce(sm(324, 1), PB[4][:, 64:80], X, ALU.max))
                        link(v_.tensor_scalar(sm(325, 1), sm(324, 1), CAP + 0.5, None, ALU.is_gt))
                        v_.tensor_copy(flag[0:1, 0:1], small[0:1, 325:326]).then_inc(S["posm"], 1)
                        v_.memset(accT, 0.0).then_inc(S["acc_d"], 1)
                        dve.wait_ge(S["acc_d"], (2 * NP_ + 3) * l + 1)
                        v_.memset(pgT, 0.0).then_inc(S["pgt"], 1)
                        v_.memset(ytok[:, 0:512], 0.0).then_inc(S["ytok_a"], 1)
                        v_.memset(ytok[:, 512:1024], 0.0).then_inc(S["ytok_d"], 1)
                    elif st == "moe":
                        iota = const[:, C_IOTA:C_IOTA + CAP]

                        def selectors(e0, done, na=2, io=iota):
                            for s in range(NS):
                                for a in range(na):
                                    ps = posm[:, s, bass.ds(e0 + a, 1)]
                                    gs = gates[:, s, bass.ds(e0 + a, 1)]
                                    v_.tensor_scalar(pm[:, s, CAP * a:CAP * a + CAP], io, ps, None, ALU.is_equal)
                                    ins = v_.tensor_scalar(pg[:, s, CAP * a:CAP * a + CAP], io, ps, gs, ALU.is_equal, ALU.mult)
                            ins.then_inc(done, 1)

                        def slots_of(i, dst, gated):
                            for s in range(NS):
                                for a in range(2):
                                    ps = posm[:, s, bass.ds(i * 2 + a, 1)]
                                    gs = gates[:, s, bass.ds(i * 2 + a, 1)]
                                    o = dst[:, s, CAP * a:CAP * a + CAP]
                                    if gated:
                                        ins = v_.tensor_scalar(o, iota, ps, gs, ALU.is_equal, ALU.mult)
                                    else:
                                        ins = v_.tensor_scalar(o, iota, ps, None, ALU.is_equal)
                            return ins

                        def accumulate(v, b):
                            dve.wait_ge(S["scat"], v * 2 + b + 1)
                            for c in range(2):
                                t = 1024 * b + 512 * c
                                ins = v_.tensor_tensor(accT[:, t:t + 512], accT[:, t:t + 512], PB[(6, 7, 0, 1)[2 * b + c]][:, :], ALU.add)
                            ins.then_inc(S["acc_d"], 1)

                        slots_of(0, pm, False).then_inc(S["pmat"], 1)
                        dve.wait_ge(S["gat"], 2 * (9 * l) + 2)
                        v_.tensor_copy(hg[:, 4:8, :], PB[1][:, :].rearrange("p (k c) -> p k c", k=4)).then_inc(S["gat_d"], 1)
                        with dve.Fori(0, NP_) as i:
                            v = i + NP_ * l
                            slots_of(i + 1, pm, False).then_inc(S["pmat"], 1)
                            slots_of(i, pg, True)
                            dve.wait_ge(S["silu"], v + 1)
                            v_.tensor_tensor(hid, sg1, PB[3][:, :], ALU.mult).then_inc(S["hid"], 1)
                            dve.wait_ge(S["gat"], (v + l) * 2 + 4)
                            v_.tensor_copy(hg[:, 4:8, :], PB[1][:, :].rearrange("p (k c) -> p k c", k=4)).then_inc(S["gat_d"], 1)
                            accumulate(v + l, 0)
                            accumulate(v + l, 1)
                            dve.wait_ge(S["yt"], v + 1)
                            v_.tensor_copy(ytok[:, 512:1024], PB[5][:, :]).then_inc(S["ytok_d"], 1)
                        accumulate((NP_ + 1) * (l + 1) - 1, 0)
                        accumulate((NP_ + 1) * (l + 1) - 1, 1)
                        over = dve.value_load(flag[0:1, 0:1], min_val=0, max_val=1)
                        O = OV[l]
                        with dve.If(over):
                            v_.tensor_copy(iotar, iota).then_inc(O["acc"], 1)
                            dve.wait_ge(O["acc"], 1)
                            with dve.Fori(1, ROUNDS) as r:
                                v_.tensor_scalar(iotar, iotar, float(CAP), None, ALU.add).then_inc(O["acc"], 1)
                                with dve.Fori(0, E) as e:
                                    q = (r - 1) * E + e
                                    dve.wait_ge(O["acc"], r + q + 1)
                                    for s in range(NS):
                                        ps, gs = posm[:, s, bass.ds(e, 1)], gates[:, s, bass.ds(e, 1)]
                                        v_.tensor_scalar(pm[:, s, 0:CAP], iotar, ps, None, ALU.is_equal)
                                        ins = v_.tensor_scalar(pg[:, s, 0:CAP], iotar, ps, gs, ALU.is_equal, ALU.mult)
                                    ins.then_inc(O["p"], 1)
                                    dve.wait_ge(O["gat"], q + 1)
                                    v_.tensor_copy(hg[:, :, 0:CAP], PB[0][:, :].rearrange("p (k c) -> p k c", k=KT)).then_inc(O["gat_c"], 1)
                                    dve.wait_ge(O["silu"], q + 1)
                                    v_.tensor_tensor(hid[0:CAP, :], sg1[0:CAP, :], PB[3][0:CAP, :], ALU.mult).then_inc(O["hid"], 1)
                                    dve.wait_ge(O["tr"], q + 1)
                                    v_.tensor_copy(hidT, PB[2][:, :].rearrange("p (f c) -> p f c", f=FT)).then_inc(O["hidt"], 1)
                                    dve.wait_ge(O["tr_p"], q + 1)
                                    v_.tensor_copy(pgT[0:CAP, :], PB[3][0:CAP, 0:256])
                                    v_.tensor_copy(ytok[0:CAP, 0:512], PB[4][0:CAP, :])
                                    v_.tensor_copy(ytok[0:CAP, 512:1024], PB[5][0:CAP, :]).then_inc(O["tr_c"], 1)
                                    dve.wait_ge(O["scat"], q + 1)
                                    for c in range(4):
                                        ins = v_.tensor_tensor(accT[:, 512 * c:512 * c + 512], accT[:, 512 * c:512 * c + 512],
                                                               PB[(6, 7, 0, 1)[c]][:, :], ALU.add)
                                    ins.then_inc(O["acc"], 1)
                            dve.wait_ge(O["acc"], ROUNDS + (ROUNDS - 1) * E)
                        dve.wait_ge(S["acc_d"], (2 * NP_ + 3) * (l + 1))
                        link(v_.tensor_copy(sm(328, 1), accT[:, 0:1]))
                        a4 = accT.rearrange("p (k s t) -> p k s t", k=KT, s=2)
                        for k in range(KT):
                            for s in range(NS):
                                ins = v_.scalar_tensor_tensor(out=xT[:, k, s, :], in0=a4[:, k, s, :], scalar=mod[:, 40 + k, s:s + 1],
                                                              in1=xT[:, k, s, :], op0=ALU.mult, op1=ALU.add)
                        ins.then_inc(S["acc_end"], 1)
                        dve.wait_ge(S["acc_end"], l + 1)
            for j in range(4):
                if j % 2 == 0:
                    dve.wait_ge(S["fin_t"], j + 1)
                    v_.tensor_copy(x_tok[:, j // 2, 0:512], PB[j][:, :]).then_inc(S["fin_c"], 1)


_INS = ['x_prompt', 'x_sample', 'cache_k', 'cache_v', 'state_gla', 'c', 'c_ctx', 'w_in', 'w_out', 'sgu_w', 'sgu_b',
        'q_norm_g', 'k_norm_g', 'diff_lambda', 'diff_norm_g', 'gla_w2', 'gla_b', 'gla_norm_g', 'norm1_g', 'norm2_g',
        'ada_w', 'ada_b', 'router_w', 'router_bias', 'moe_w1', 'moe_w3', 'moe_w2']
_OUTS = [(1, P, D), (1, P, D), (1, DEPTH, H, 2, P, QK), (1, DEPTH, H, P, P), (1, DEPTH, 2, H, QK, QK)]


def kernel(**inputs):
    import numpy as _np
    import concourse.bacc as _bacc
    from concourse import mybir as _mybir
    from concourse.bass_utils import run_bass_kernel_spmd as _run

    nc = _bacc.Bacc("TRN2", target_bir_lowering=False, num_devices=1)
    arrays, aps = {}, {}
    given = {name: _np.ascontiguousarray(inputs[name]) for name in _INS}
    given["const"] = constants()
    for name, a in given.items():
        arrays[f"in_{name}_dram"] = a
        aps[name] = nc.dram_tensor(f"in_{name}_dram", a.shape, _mybir.dt.from_np(a.dtype), kind="ExternalInput").ap()
    outs = [nc.dram_tensor(f"out_{i}_dram", shape, _mybir.dt.float32, kind="ExternalOutput").ap()
            for i, shape in enumerate(_OUTS)]
    hybrid_step(nc, aps, outs)
    r = _run(nc, [arrays], core_ids=[0])
    return tuple(r.results[0][f"out_{i}_dram"] for i in range(len(_OUTS)))
```

```python
from contextlib import ExitStack
import math

import numpy as np
import concourse.bass as bass
from concourse import mybir

P = 128
NS = 2
D = 1024
KT = D // P
DEPTH = 2
DPROJ = 3104
CW = 512
F = 512
FT = F // P
E = 16
NP_ = E // 2
CAP = 64
ROUNDS = NS * P // CAP
EPS = 1e-6
H = 4
QK = 64
U0, V0, BQ, BK, BV, CQ, CK, CV, CR, LR = 0, 256, 512, 1024, 1536, 2048, 2304, 2560, 2816, 3072
NADA = 6 * D // CW
PROJ = [(LR, 32), (CQ, 512), (CV, 512), (BQ, 512), (BK, 512), (U0, 512), (BV, 512)]
BY_ACT = (1, 4, 5)
ADA_FIRST = (0, NADA // 2, 3 * NADA // 2)
NROWS = 48 + 8 + 8 + 4

F32 = mybir.dt.float32
I32 = mybir.dt.int32
ALU = mybir.AluOpType
ACT = mybir.ActivationFunctionType
X = mybir.AxisListType.X

C_ID, C_ONE, C_TRIF, C_TRIB, C_REMF, C_REMB, C_STRICT = (i * P for i in range(7))
C_CHUNK = 7 * P
C_IOTA = C_CHUNK + 3
C_SEL = C_IOTA + CAP
C_LOWER = C_SEL + 2
C_COS = C_LOWER + 16
C_SIN = C_COS + QK
NCONST = C_SIN + QK


def constants():
    t = np.arange(P)
    a, b = t[:, None], t[None, :]
    same = (a // 64) == (b // 64)
    g = np.float32(1.0 / 16.0)
    c = np.zeros((P, NCONST), np.float32)
    c[:, C_ID:C_ID + P] = a == b
    c[:, C_ONE:C_ONE + P] = 1.0
    c[:, C_TRIF:C_TRIF + P] = ((a <= b) & same) * g
    c[:, C_TRIB:C_TRIB + P] = ((a >= b) & same) * g
    c[:, C_REMF:C_REMF + P] = ((a > b) & same) * g
    c[:, C_REMB:C_REMB + P] = ((a < b) & same) * g
    c[:, C_STRICT:C_STRICT + P] = a < b
    for i, h in enumerate((0, 1, 0)):
        c[:, C_CHUNK + i] = (t // 64 == h) * g
    c[:, C_IOTA:C_IOTA + CAP] = np.arange(CAP)
    for i in range(NS):
        c[:, C_SEL + i] = t % 32 == i
    j, i = np.arange(4)[:, None], np.arange(4)[None, :]
    c[:, C_LOWER:C_LOWER + 16] = (i < j).astype(np.float32).reshape(-1)
    fr = (np.float32(10000.0) ** (-np.arange(16, dtype=np.float32) / np.float32(16))).astype(np.float32)
    for n, pos in enumerate((t // 64, t % 64)):
        ang = pos.astype(np.float32)[:, None] * fr
        c[:, C_COS + 32 * n:C_COS + 32 * n + 32] = np.concatenate([np.cos(ang)] * 2, 1)
        c[:, C_SIN + 32 * n:C_SIN + 32 * n + 32] = np.concatenate([-np.sin(ang), np.sin(ang)], 1)
    return c


def plan(l):
    half = NADA // 2
    ada_mlp = [("ada", l, half + a) for a in range(half)]
    ada_next = [("ada", l + 1, a) for a in range(half)] if l + 1 < DEPTH else []

    def fill(*n):
        out = []
        for _ in range(sum(n)):
            if ada_mlp:
                out.append(ada_mlp.pop(0))
            elif ada_next:
                out.append(ada_next.pop(0))
        return out

    def proj(*halves):
        return [("proj", l, j) for j in halves]

    p = []
    if l == 0:
        p += [("ada", 0, 0), ("ada", 0, 1), ("xin", 0, 0), ("ada", 0, 2), ("sqa", 0, 0), ("sq", 0, 0), ("ada", 0, 3), ("pcols", 0, 0),
              ("xn", 0, 0), ("ada", 0, 4), ("ada", 0, 5), ("adaout", 0, half - 1), ("mod", 0, 0), ("norm", 0, 0)]
    else:
        p += [("pcols", l, 0), ("sq", l, 0), ("mod", l, 0), ("xn", l, 0), ("norm", l, 0)]
    p += [*proj(0, 2), ("lam", l, 0), *proj(3), *proj(4), ("glaB", l, 0), *proj(5), ("glaC", l, 0), *proj(6), ("glaD", l, 0),
          *proj(7), ("glaE", l, 0), *proj(8), ("glaF", l, 0), *proj(9), ("glaB", l, 1), ("qkn", l, 0),
          *proj(10), ("glaC", l, 1), *proj(11), ("glaD", l, 1), ("qkn", l, 1), *proj(12), ("glaE", l, 1), ("sguv", l, 0),
          *proj(13), ("glaF", l, 1)]
    p += [("qkt", l, 0), *fill(1), ("qkt", l, 1), ("sc", l, 0), ("sgu", l, 0), ("sc", l, 1), *fill(1), ("mix", l, 0),
          ("wt", l, 0), *fill(1), ("mix", l, 1), ("pv", l, 0), ("wt", l, 1), *fill(1), ("catT", l, 0), ("pv", l, 1), *fill(1), ("catT", l, 1), *fill(1)]
    assert not ada_mlp
    if l + 1 < DEPTH:
        p += [*fill(1), ("mod", l, 1), ("wout", l, 0), *fill(1), ("sqa", l, 1), ("wout", l, 1), *fill(1), ("sq", l, 1), *fill(2),
              ("xn", l, 1), ("norm", l, 1),
              ("routeA", l, 0), *fill(1), ("adaout", l + 1, half - 1), ("route", l, 0)]
    else:
        p += [("adaout", l, NADA - 1), ("mod", l, 1), ("wout", l, 0), ("sqa", l, 1), ("wout", l, 1), ("sq", l, 1),
              ("xn", l, 1), ("norm", l, 1), ("routeA", l, 0), ("route", l, 0)]
    return p + [("moe", l, 0)]


def hybrid_step(nc, A, outs):
    y_p, y_s, new_k, new_v, new_s = outs
    with ExitStack() as ctx:
        def sb(name, shape, dt=F32):
            return ctx.enter_context(nc.sbuf_tensor(name, shape, dt))

        names = """x_in const_in rows_c_in params_in kcache_out vcache_out state_out y_out
        rows_t rowsc_t cond0 cond lr_one ada_row ada_col ada_colc mod_ready ada_used w1_used
        lam sq_ready ss_ready ms_ready rstd_ready xn_ready ht_dve ht_act
        proj ev zz lng gg cum exps qkd qkt_gla qkt_gla_c attn attn_m zeroed kv o_part st1 og og_sq og_ms og_rs og_done sg_done
        qk_sq qk_ms qk_rs qk_done vms vrs v_done qkT qkTc sc nmax pexp wmix wT wTc pv o_sq o_ms o_rs ob_done
        wsT wsTc sgu_s sgu_done catT catTc wout xadd
        htok htokc logit aff mask pos posm
        x_t x_tc fin_t fin_c fin_a
        pmat gat gat_a gat_d h13 silu hid hidt pgt yt tr tr_p ytok_a ytok_d scat acc_d acc_end
        dve_chain act_chain pool_chain flag""".split()
        S = {n: ctx.enter_context(nc.semaphore(n)) for n in names}
        s_ab = [ctx.enter_context(nc.semaphore(f"chunk_in{i}")) for i in range(3)]
        s_slot = [ctx.enter_context(nc.semaphore(f"expert_w_in{i}")) for i in range(6)]
        s_odd = [ctx.enter_context(nc.semaphore(f"odd_pair_w1_in{a}")) for a in range(2)]
        OV = [{n: ctx.enter_context(nc.semaphore(f"over{l}_{n}")) for n in
               "w p gat gat_c h13 silu hid tr hidt yt tr_p tr_c scat acc".split()} for l in range(DEPTH)]

        const = sb("const", [P, NCONST])
        slots = [sb(f"expert_w{i}", [P, 4096]) for i in range(6)]
        ab = [sb(f"chunk{i}", [P, 4096]) for i in range(2)]
        xT = sb("xT", [P, KT, NS, P])
        hb = sb("hT", [P, KT, NS, P])
        pr = sb("pr", [P, NS, DPROJ])
        gl = sb("gl", [P, 3072])
        at = sb("at", [P, 2560])
        cols = sb("cols", [P, NROWS])
        mod = sb("mod", [P, 48, NS])
        ada = sb("ada", [P, 48, NS])
        wsT = sb("wsT", [P, H, P])
        cvc = sb("cvc", [P, H, P])
        st0 = sb("st0", [P, 2, 2, QK])
        w2gla = sb("w2gla", [33, 512])
        qkg = sb("qkg", [P, 2, QK])
        dg = sb("dg", [P, P])
        rw = sb("rw", [P, KT, E])
        rbias = sb("rbias", [P, E])
        small = sb("small", [P, 448])
        half = sb("half", [P, 1])
        posm = sb("posm", [P, NS, E + 2])
        gates = sb("gates", [P, NS, E + 2])
        flag = sb("flag", [1, 1], I32)
        condm = sb("cond", [P, 32 * KT])
        PB = [ctx.enter_context(nc.psum_tensor(f"bank{i}", [P, 512], F32)) for i in range(8)]

        dlam = at[:, 0:256].rearrange("p (a d) -> p a d", a=4)
        rows, rowsc = at[0:NROWS, 256:384], at[0:16, 384:512]
        wst = at[:, 512:1024].rearrange("p (g q) -> p g q", g=H)
        ckc = at[:, 2048:2560].rearrange("p (g d) -> p g d", d=QK)
        sgtmp = at[:, 1024:1280]
        lrT = at[0:33, 1280:1536]
        adar = [slots[5][:, CW * i:CW * i + CW] for i in range(2)]
        cond = condm[:, :].rearrange("p (k c) -> p k c", c=32)
        rsq = gl[:, 0:512].rearrange("p (a t) -> p a t", a=2)

        ident = const[:, C_ID:C_ID + P]
        ones = const[:, C_ONE:C_ONE + P]

        def sm(a, n):
            return small[:, a:a + n]
        lam = sm(0, 8)
        ssum = sm(8, 8)
        SSQ, QMS, QRS, SMX, SSM = 16, 32, 48, 64, 96
        glag = sm(128, QK)

        def glv(a, n):
            return gl[:, a:a + n]
        g_sb, qd, ki, ke, kiT = glv(0, 512), glv(512, 512), glv(1024, 512), glv(1536, 512), glv(2048, 512)
        qdT = g_sb
        attnT = glv(512, 1024)
        st1 = glv(2560, 256).rearrange("p (a b v) -> p a b v", a=2, b=2)
        st2 = glv(2816, 256).rearrange("p (a b v) -> p a b v", a=2, b=2)
        atT = [at[:, 0:1024], at[:, 1024:2560]]
        dec = sm(192, 8)
        p0w = glv(0, 1024).rearrange("p (m t) -> p m t", m=8)
        CATB = (2, 6, 0, 1)
        SCB = (0, 1, 4, 5)

        prf = pr[:, :, :].rearrange("p s c -> p (s c)")
        htok = prf[:, 0:2048].rearrange("p (s d) -> p s d", s=NS)
        accT = prf[:, 2048:4096]
        sqr = accT.rearrange("p (k c) -> p k c", k=KT)
        hg = prf[:, 4096:5120].rearrange("p (k c) -> p k c", k=KT)
        hidT = prf[:, 5120:5632].rearrange("p (f c) -> p f c", f=FT)
        ytok = gl[:, 0:1024]
        pm = gl[:, 1024:1280].rearrange("p (s c) -> p s c", s=NS)
        pg = gl[:, 1280:1536].rearrange("p (s c) -> p s c", s=NS)
        pgT = gl[:, 1536:1792]
        sg1 = gl[:, 1792:2304]
        hid = gl[:, 2304:2816]
        iotar = gl[:, 2816:2880]
        x_tok = prf[:, 0:2048].rearrange("p (s d) -> p s d", s=NS)

        ORDER = (0, 3, 1, 4, 2, 5)

        plans = [plan(l) for l in range(DEPTH)]
        chunks = []
        for l in range(DEPTH):
            for st, ll, n in plans[l]:
                if st == "proj":
                    if n % 2 == 0:
                        chunks.append((st, ll, n // 2))
                elif st in ("ada", "wout"):
                    chunks.append((st, ll, n))
        order = {c: i for i, c in enumerate(chunks)}
        held = [[], [], []]
        place = []
        for i, c in enumerate(chunks):
            early = c[0] == "proj" and c[1] > 0 and c[2] < 2
            b = min(range(2 if early else 3), key=lambda b: held[b][-1] if held[b] else b - 3)
            place.append((b, len(held[b])))
            held[b].append(i)
        chunk_mem = ab + [slots[2]]
        first_of = [order[("ada", 0, 0)], order[("proj", 1, 0)]]

        def chunk_src(c):
            st, l, n = c
            if st == "ada":
                return A["ada_w"][l, :, CW * n:CW * (n + 1)], CW
            if st == "wout":
                return A["w_out"][l, :, CW * n:CW * (n + 1)], CW
            c0, w = PROJ[n]
            return A["w_in"][l, :, c0:c0 + w], w

        def chunk_view(c):
            w = chunk_src(c)[1]
            return chunk_mem[place[order[c]][0]][:, 0:KT * w].rearrange("p (k c) -> p k c", k=KT)

        def chunk_here(eng, c):
            b, before = place[order[c]]
            eng.wait_ge(s_ab[b], 16 * (before + 1))

        def expert_src(l, slot, e):
            b = slot % 3
            if b < 2:
                return A["moe_w1" if b == 0 else "moe_w3"][l, e, :, :].rearrange("(k p) f -> p k f", p=P)
            return A["moe_w2"][l, e, :, :].rearrange("(k p) d -> p k d", p=P)

        def w1_view(a, odd):
            return ab[a][:, :].rearrange("p (k f) -> p k f", k=KT) if odd else slot_view(3 * a)

        def slot_view(s):
            if s % 3 < 2:
                return slots[s][:, :].rearrange("p (k f) -> p k f", k=KT)
            return slots[s][:, :].rearrange("p (k d) -> p k d", k=FT)

        block = ctx.enter_context(nc.Block())

        @block.sync
        def _(sp):
            def wait_chunk_used(i):
                st, l, n = chunks[i]
                if st == "ada":
                    sp.wait_ge(S["ada_used"], NADA * l + n + 1)
                elif st == "proj":
                    sp.wait_ge(S["proj"], 14 * l + 2 * n + 2)
                else:
                    sp.wait_ge(S["wout"], 2 * l + n + 1)

            def load_chunk(i):
                src, w = chunk_src(chunks[i])
                b, before = place[i]
                if before > 0:
                    wait_chunk_used(held[b][before - 1])
                if i >= first_of[1] > held[b][before - 1]:
                    wait_used(0 if b < 2 else 2, NP_)
                sp.dma_start(chunk_view(chunks[i]), src.rearrange("(k p) c -> p k c", p=P)).then_inc(s_ab[b], 16)

            def wait_used(s, pairs):
                sp.wait_ge(S[("w1_used", "h13", "yt")[s % 3]], pairs)

            def load_w1(l, pair, odd, experts=(0, 1)):
                for a in experts:
                    sp.dma_start(w1_view(a, odd), expert_src(l, 3 * a, pair * 2 + a)).then_inc(s_odd[a] if odd else s_slot[3 * a], 16)

            def load_pair0(l, s):
                if l > 0:
                    wait_used(s, NP_ * l)
                if s == 2:
                    wait_chunk_used([i for i in held[2] if l + 1 == DEPTH or i < first_of[l + 1]][-1])
                if s == 5:
                    sp.wait_ge(S["ada_col"], min(NADA * (l + 1) + NADA // 2, NADA * DEPTH))
                sp.dma_start(slot_view(s), expert_src(l, s, s // 3)).then_inc(s_slot[s], 16)

            sp.dma_start(rowsc[0:8, :], A["c_ctx"].rearrange("(k p) -> k p", p=P)).then_inc(S["rows_c_in"], 16)
            sp.dma_start(rowsc[8:16, :], A["c"].rearrange("o (k p) -> (o k) p", p=P)).then_inc(S["rows_c_in"], 16)
            at_chunk = 0
            for l in range(DEPTH):
                last = first_of[l + 1] if l + 1 < DEPTH else len(chunks)
                pend = list(ORDER)
                while at_chunk < last:
                    load_chunk(at_chunk)
                    st, cl, n = chunks[at_chunk]
                    if l == 0 and st == "proj" and n >= 2 and len(pend) > 2:
                        load_pair0(l, pend.pop(0))
                    if l > 0 and (st, n) == ("proj", 1):
                        while len(pend) > 2:
                            load_pair0(l, pend.pop(0))
                    at_chunk += 1
                in_layer = [[i for i in held[b] if l + 1 == DEPTH or i < first_of[l + 1]][-1] for b in range(3)]
                for b in sorted(range(3), key=lambda b: in_layer[b]):
                    if b == 2:
                        for s in pend:
                            load_pair0(l, s)
                    else:
                        wait_chunk_used(in_layer[b])
                        load_w1(l, 1, True, (b,))

                def refill(i, odd, more=True):
                    v = i + NP_ * l
                    if more:
                        sp.wait_ge(S["w1_used"], v + 1)
                        load_w1(l, i + 2, odd)
                    for b in (1, 2):
                        for s in (b, 3 + b):
                            wait_used(s, v + 1)
                            sp.dma_start(slot_view(s), expert_src(l, s, (i + 1) * 2 + s // 3)).then_inc(s_slot[s], 16)

                with sp.Fori(0, NP_ // 2 - 1) as j:
                    refill(j * 2, False)
                    refill(j * 2 + 1, True)
                refill(NP_ - 2, False, more=False)
                sp.wait_ge(S["posm"], l + 1)
                over = sp.value_load(flag[0:1, 0:1], min_val=0, max_val=1)
                O = OV[l]
                with sp.If(over):
                    for s in range(3):
                        wait_used(s, NP_ * (l + 1))
                    with sp.Fori(1, ROUNDS) as r:
                        with sp.Fori(0, E) as e:
                            sp.wait_ge(O["acc"], r + (r - 1) * E + e + 1)
                            for s in range(3):
                                sp.dma_start(slot_view(s), expert_src(l, s, e)).then_inc(O["w"], 16)
                    sp.wait_ge(O["acc"], ROUNDS + (ROUNDS - 1) * E)

        @block.gpsimd
        def _(pool):
            n_chain = [0]

            def link(ins):
                n_chain[0] += 1
                ins.then_inc(S["pool_chain"], 1)
                pool.wait_ge(S["pool_chain"], n_chain[0])

            nc.gpsimd.memset(cond[:, :, :], 0.0).then_inc(S["cond0"], 1)
            link(nc.gpsimd.memset(half[:, :], -0.5))
            link(nc.gpsimd.memset(w2gla[:, :], 0.0))

            def params(l):
                nc.gpsimd.memset(lrT, 1.0).then_inc(S["lr_one"], 1)
                pool.dma_start(rows[0:48, :], A["ada_b"][l].rearrange("(k p) -> k p", p=P)).then_inc(S["params_in"], 16)
                pool.dma_start(rows[48:56, :], A["norm1_g"][l].rearrange("(k p) -> k p", p=P)).then_inc(S["params_in"], 16)
                pool.dma_start(rows[56:64, :], A["norm2_g"][l].rearrange("(k p) -> k p", p=P)).then_inc(S["params_in"], 16)
                pool.dma_start(rows[64:68, :], A["sgu_b"][l]).then_inc(S["params_in"], 16)
                pool.dma_start(wst[:, :, :], A["sgu_w"][l].rearrange("g p q -> p g q")).then_inc(S["params_in"], 16)
                pool.dma_start(ckc[:, :, :], A["cache_k"][0, l].rearrange("h i t d -> t (h i) d")).then_inc(S["params_in"], 16)
                pool.dma_start(cvc[:, :, :], A["cache_v"][0, l].rearrange("h t d -> t h d")).then_inc(S["params_in"], 16)
                for a in range(2):
                    for b in range(2):
                        pool.dma_start(st0[64 * b:64 * b + 64, a, :, :],
                                       A["state_gla"][0, l, a, b::2].rearrange("h d v -> d h v")).then_inc(S["params_in"], 16)
                    pool.dma_start(w2gla[16 * a:16 * a + 16, 256 * a:256 * a + 256], A["gla_w2"][l, a]).then_inc(S["params_in"], 16)
                pool.dma_start(w2gla[32:33, :], A["gla_b"][l:l + 1].rearrange("o a c -> o (a c)")).then_inc(S["params_in"], 16)
                pool.dma_start(qkg[:, 0, :], A["q_norm_g"][l].partition_broadcast(P)).then_inc(S["params_in"], 16)
                pool.dma_start(qkg[:, 1, :], A["k_norm_g"][l].partition_broadcast(P)).then_inc(S["params_in"], 16)
                pool.dma_start(dg[:, :], A["diff_norm_g"][l].partition_broadcast(P)).then_inc(S["params_in"], 16)
                pool.dma_start(glag[:, :], A["gla_norm_g"][l].partition_broadcast(P)).then_inc(S["params_in"], 16)
                pool.dma_start(dlam[:, :, :], A["diff_lambda"][l].partition_broadcast(P)).then_inc(S["params_in"], 16)
            for l in range(DEPTH):
                if l == 0:
                    params(0)
                    pool.dma_start(rw[:, :, :], A["router_w"].rearrange("(k p) e -> p k e", p=P)).then_inc(S["params_in"], 16)
                    pool.dma_start(rbias[:, :], A["router_bias"].partition_broadcast(P)).then_inc(S["params_in"], 16)
                for st, ll, n in plans[l]:
                    if st == "glaD":
                        pool.wait_ge(S["qkt_gla_c"], 2 * (2 * l + n + 1))
                        nc.gpsimd.memset(attnT, 0.0).then_inc(S["zeroed"], 1)
                    elif st == "glaF":
                        pool.wait_ge(S["og_ms"], 2 * l + n + 1)
                        nc.gpsimd.tensor_tensor(sm(212, 4), sm(208, 4), half[:, :].to_broadcast([P, 4]), ALU.pow).then_inc(S["og_rs"], 1)
                    elif st == "pv":
                        pool.wait_ge(S["o_ms"], 2 * l + n + 1)
                        nc.gpsimd.tensor_tensor(sm(228, 4), sm(224, 4), half[:, :].to_broadcast([P, 4]), ALU.pow).then_inc(S["o_rs"], 1)
                    elif st == "qkn":
                        pool.wait_ge(S["qk_ms"], 2 * l + n + 1)
                        nc.gpsimd.tensor_tensor(sm(QRS, 16), sm(QMS, 16), half[:, :].to_broadcast([P, 16]), ALU.pow).then_inc(S["qk_rs"], 1)
                    elif st == "catT":
                        if n == 1:
                            pool.wait_ge(S["qk_done"], 2 * l + 1)
                            pool.dma_start(new_k[0, l].rearrange("h i t d -> t (h i) d"),
                                           pr[:, 0, BK:BK + 512].rearrange("p (g d) -> p g d", d=QK)).then_inc(S["kcache_out"], 16)
                            pool.wait_ge(S["ev"], 14 * (l + 1))
                            pool.dma_start(new_v[0, l].rearrange("h t d -> t h d"),
                                           pr[:, 0, BV:BV + 512].rearrange("p (h d) -> p h d", d=P)).then_inc(S["vcache_out"], 16)
                            for a in range(2):
                                for b in range(2):
                                    pool.dma_start(new_s[0, l, a, b::2].rearrange("h d v -> d h v"),
                                                   st2[64 * b:64 * b + 64, a, :, :]).then_inc(S["state_out"], 16)
                    elif st == "sguv":
                        pool.wait_ge(S["vms"], l + 1)
                        nc.gpsimd.tensor_tensor(sm(248, 8), sm(240, 8), half[:, :].to_broadcast([P, 8]), ALU.pow).then_inc(S["vrs"], 1)
                    elif st == "routeA":
                        pool.wait_ge(S["ss_ready"], 2 * l + 2)
                        nc.gpsimd.memset(accT, 0.0).then_inc(S["acc_d"], 1)
                    elif st == "route" and l + 1 < DEPTH:
                        pool.wait_ge(S["posm"], l + 1)
                        params(l + 1)
            pool.wait_ge(S["kcache_out"], 16 * DEPTH)
            pool.wait_ge(S["vcache_out"], 16 * DEPTH)
            pool.wait_ge(S["state_out"], 64 * DEPTH)

        NPARAM = 21

        @block.scalar
        def _(act):
            n_chain = [0]

            def link(ins):
                n_chain[0] += 1
                ins.then_inc(S["act_chain"], 1)
                act.wait_ge(S["act_chain"], n_chain[0])

            def params_here(l):
                act.wait_ge(S["params_in"], 16 * (NPARAM - 2) * l + 16 * NPARAM)

            A_ = nc.scalar.activation

            def ada_copy(m):
                c = 4 * (m % NADA)
                act.wait_ge(S["ada_col"], m + 1)
                if m >= NADA:
                    act.wait_ge(S["mod_ready"], m // (NADA // 2) - 1)
                A_(ada[:, c:c + 4, :].rearrange("p c s -> p (c s)"), PB[7][:, 0:8], ACT.Copy).then_inc(S["ada_colc"], 1)

            act.dma_start(const[:, :], A["const"]).then_inc(S["const_in"], 16)
            act.dma_start(x_tok[:, 0, :], A["x_prompt"][0]).then_inc(S["x_in"], 16)
            act.dma_start(x_tok[:, 1, :], A["x_sample"][0]).then_inc(S["x_in"], 16)
            act.wait_ge(S["rowsc_t"], 1)
            act.wait_ge(S["cond0"], 1)
            A_(cond[:, :, 0:2].rearrange("p k s -> p s k"), PB[6][:, 128:144].rearrange("p (s k) -> p s k", s=2),
               ACT.Silu).then_inc(S["cond"], 1)
            for l in range(DEPTH):
                for st, ll, n in plans[l]:
                    g = 2 * l + n
                    if st == "xin":
                        for j in range(4):
                            if j % 2:
                                act.wait_ge(S["x_t"], j + 1)
                                A_(xT[:, 4 * (j % 2):4 * (j % 2) + 4, j // 2, :], PB[j][:, :].rearrange("p (k t) -> p k t", k=4),
                                   ACT.Copy).then_inc(S["x_tc"], 1)
                    elif st == "lam":
                        act.wait_ge(S["lam"], 2 * l + 1)
                        A_(lam[:, 2:4], lam[:, 0:2], ACT.Exp).then_inc(S["lam"], 1)
                    elif st == "pcols":
                        act.wait_ge(S["wsT"], l + 1)
                        A_(wsT[:, :, :].rearrange("p g q -> p (g q)"), PB[4][:, :], ACT.Copy).then_inc(S["wsTc"], 1)
                    elif st == "ada":
                        m = NADA * ll + n
                        if m not in ADA_FIRST and m >= ADA_FIRST[1]:
                            ada_copy(m - 1)
                        act.wait_ge(S["ada_used"], m + 1)
                        if m >= 2:
                            act.wait_ge(S["ada_col"], m - 1)
                        A_(adar[m % 2], PB[7][:, :], ACT.Copy).then_inc(S["ada_row"], 1)
                    elif st == "adaout" and NADA * ll + n >= ADA_FIRST[1]:
                        ada_copy(NADA * ll + n)
                    elif st == "sq":
                        act.wait_ge(S["ss_ready"], g + 1)
                        A_(rsq[:, 0, :], PB[5][:, 0:NS * P], ACT.Sqrt, scale=1.0 / D, bias=EPS).then_inc(S["rstd_ready"], 1)
                    elif st == "norm":
                        act.wait_ge(S["mod_ready"], g + 1)
                        for k in range(KT):
                            if k % 4 == 0:
                                act.wait_ge(S["xn_ready"], 2 * g + k // 4 + 1)
                            ins = A_(hb[:, k, 1, :], hb[:, k, 1, :], ACT.Identity, bias=mod[:, 24 * n + k, 1:2],
                                     scale=mod[:, 24 * n + 8 + k, 1:2])
                        ins.then_inc(S["ht_act"], 1)
                    elif st == "proj":
                        c, s = n // 2, n % 2
                        if n == 0:
                            act.wait_ge(S["proj"], 14 * l + 2)
                            act.wait_ge(S["lr_one"], l + 1)
                            A_(lrT[0:32, :], PB[0][0:32, 0:NS * P], ACT.Copy).then_inc(S["ev"], 2)
                        elif c in BY_ACT or s == 1:
                            act.wait_ge(S["proj"], 14 * l + n + 1)
                            if n > 0:
                                act.wait_ge(S["ev"], 14 * l + n)
                            c0, w = PROJ[c]
                            A_(pr[:, s, c0:c0 + w], PB[2 * (c % 2) + s][:, 0:w],
                               ACT.Gelu_apprx_tanh if c0 == U0 else ACT.Copy).then_inc(S["ev"], 1)
                    elif st == "glaB":
                        act.wait_ge(S["zz"], g + 1)
                        if n == 1:
                            act.wait_ge(S["og"], 2 * l + 1)
                        link(A_(ki, PB[5][:, :], ACT.Abs))
                        link(A_(ki, ki, ACT.Exp, scale=-1.0))
                        A_(ki, ki, ACT.Ln, bias=1.0).then_inc(S["lng"], 1)
                    elif st == "glaC":
                        act.wait_ge(S["cum"], g + 1)
                        A_(qd, PB[6][:, :], ACT.Exp)
                        A_(ki, PB[6][:, :], ACT.Exp, scale=-1.0)
                        A_(ke, PB[5][:, :], ACT.Exp)
                        A_(dec, PB[4][:, 0:8], ACT.Exp)
                        act.wait_ge(S["ev"], 14 * l + 6)
                        A_(sgtmp, pr[:, n, CR:CR + 256], ACT.Exp, scale=-1.0).then_inc(S["exps"], 1)
                    elif st == "glaD":
                        act.wait_ge(S["qkt_gla"], g + 1)
                        A_(qdT, PB[4][:, :], ACT.Copy).then_inc(S["qkt_gla_c"], 1)
                    elif st == "glaF":
                        act.wait_ge(S["og"], g + 1)
                        A_(ke[:, 0:256], PB[6][:, 0:256], ACT.Square).then_inc(S["og_sq"], 1)
                    elif st == "qkn":
                        act.wait_ge(S["ev"], 14 * l + 10)
                        if n == 1:
                            act.wait_ge(S["qk_ms"], 2 * l + 1)
                        A_(atT[0], pr[:, n, BQ:BQ + 1024], ACT.Square).then_inc(S["qk_sq"], 1)
                    elif st == "qkt":
                        if n == 0:
                            act.wait_ge(S["vms"], l + 1)
                        else:
                            act.wait_ge(S["sg_done"], 2 * l + 2)
                        act.wait_ge(S["qkT"], g + 1)
                        A_(atT[n][:, 0:512], PB[4 * n][:, :], ACT.Copy)
                        if n == 1:
                            A_(atT[1][:, 1024:1536], PB[5][:, :], ACT.Copy)
                        A_(atT[n][:, 512:1024], PB[(1, 6)[n]][:, :], ACT.Copy).then_inc(S["qkTc"], 1)
                    elif st == "sc":
                        act.wait_ge(S["nmax"], g + 1)
                        if n == 0:
                            act.wait_ge(S["og_done"], 2 * l + 2)
                        for m in range(8):
                            if n == 0:
                                src, dst = PB[2 + m // 4][:, P * (m % 4):P * (m % 4) + P], p0w[:, m, :]
                            else:
                                src = PB[SCB[m // 2]][:, 256 * (m % 2):256 * (m % 2) + 256]
                                dst = hb[:, m, :, :].rearrange("p s t -> p (s t)")
                            ins = A_(dst, src, ACT.Exp, bias=sm(SMX + 16 * n + m, 1), scale=QK ** -0.5, accum_out=sm(SSM + 16 * n + m, 1))
                        ins.then_inc(S["pexp"], 1)
                    elif st == "wt":
                        act.wait_ge(S["wT"], g + 1)
                        if n == 0:
                            A_(atT[0][:, 0:512], PB[2][:, :], ACT.Copy).then_inc(S["wTc"], 1)
                        else:
                            A_(pr[:, 1, BQ:BQ + 512], PB[0][:, :], ACT.Copy)
                            A_(pr[:, 1, BQ + 512:BQ + 1024], PB[1][:, :], ACT.Copy).then_inc(S["wTc"], 1)
                    elif st == "pv":
                        act.wait_ge(S["pv"], g + 1)
                        A_(atT[n][:, 512:1024], PB[3 + n][:, :], ACT.Square).then_inc(S["o_sq"], 1)
                    elif st == "catT":
                        act.wait_ge(S["catT"], 4 * l + 2 * n + 2)
                        act.wait_ge(S["wT"], 2 * l + 2)
                        A_(hb[:, 4:8, n, :], PB[CATB[2 * n + 1]][:, :].rearrange("p (k t) -> p k t", k=4), ACT.Copy).then_inc(S["catTc"], 1)
                    elif st == "routeA":
                        act.wait_ge(S["logit"], l + 1)
                        A_(sm(256, 32), PB[4][:, 0:32], ACT.Sigmoid).then_inc(S["aff"], 1)
                        act.wait_ge(S["kcache_out"], 16 * (l + 1))
                        act.wait_ge(S["vcache_out"], 16 * (l + 1))
                        for j in range(4):
                            act.wait_ge(S["htok"], 4 * l + j + 1)
                            A_(htok[:, j // 2, 512 * (j % 2):512 * (j % 2) + 512], PB[j][:, :], ACT.Copy).then_inc(S["htokc"], 1)
                    elif st == "moe":
                        act.wait_ge(S["gat"], 2 * NP_ * l + 1)
                        A_(hg[:, 0:4, :], PB[0][:, :].rearrange("p (k c) -> p k c", k=4), ACT.Copy).then_inc(S["gat_a"], 1)

                        def pair(i, last):
                            v = i + NP_ * l
                            act.wait_ge(S["h13"], v + 1)
                            A_(sg1, PB[2][:, :], ACT.Silu).then_inc(S["silu"], 1)
                            if not last:
                                act.wait_ge(S["gat"], v * 2 + 3)
                                A_(hg[:, 0:4, :], PB[0][:, :].rearrange("p (k c) -> p k c", k=4), ACT.Copy).then_inc(S["gat_a"], 1)
                            act.wait_ge(S["tr"], v + 1)
                            A_(hidT, PB[2][:, :].rearrange("p (f c) -> p f c", f=FT), ACT.Copy).then_inc(S["hidt"], 1)
                            act.wait_ge(S["tr_p"], v + 1)
                            A_(pgT, PB[3][:, 0:256], ACT.Copy).then_inc(S["pgt"], 1)
                            act.wait_ge(S["yt"], v + 1)
                            A_(ytok[:, 0:512], PB[4][:, :], ACT.Copy).then_inc(S["ytok_a"], 1)

                        with act.Fori(0, NP_ - 1) as i:
                            pair(i, False)
                        pair(NP_ - 1, True)
                        act.wait_ge(S["posm"], l + 1)
                        over = act.value_load(flag[0:1, 0:1], min_val=0, max_val=1)
                        O = OV[l]
                        with act.If(over):
                            with act.Fori(1, ROUNDS) as r:
                                with act.Fori(0, E) as e:
                                    act.wait_ge(O["h13"], (r - 1) * E + e + 1)
                                    A_(sg1[0:CAP, :], PB[2][0:CAP, :], ACT.Silu).then_inc(O["silu"], 1)
            act.wait_ge(S["fin_c"], 2)
            for y, s in ((y_p, 0), (y_s, 1)):
                act.dma_start(y[0, :, 0:512], x_tok[:, s, 0:512]).then_inc(S["y_out"], 16)
            for y, s in ((y_p, 0), (y_s, 1)):
                act.wait_ge(S["fin_t"], 3 + s)
                A_(x_tok[:, s, 512:1024], PB[2 * s + 1][:, :], ACT.Copy).then_inc(S["fin_a"], 1)
                act.wait_ge(S["fin_a"], 1 + s)
                act.dma_start(y[0, :, 512:1024], x_tok[:, s, 512:1024]).then_inc(S["y_out"], 16)
            act.wait_ge(S["y_out"], 64)

        @block.tensor
        def _(pe):
            mm, tp = nc.tensor.matmul, nc.tensor.transpose

            def ada_columns(m):
                pe.wait_ge(S["ada_row"], m + 1)
                for t in range(4):
                    ins = mm(PB[7][:, 2 * t:2 * t + 2], adar[m % 2][:, P * t:P * t + P], const[:, C_SEL:C_SEL + 2],
                             start=True, stop=True)
                ins.then_inc(S["ada_col"], 1)

            pe.wait_ge(S["const_in"], 16)
            pe.wait_ge(S["rows_c_in"], 32)
            tp(PB[6][:, 128:144], rowsc[:, :], ident[0:16, 0:16]).then_inc(S["rowsc_t"], 1)
            for l in range(DEPTH):
                for st, ll, n in plans[l]:
                    g = 2 * l + n
                    if st == "xin":
                        pe.wait_ge(S["x_in"], 32)
                        for j in range(4):
                            for k in range(4):
                                ins = tp(PB[j][:, P * k:P * k + P], x_tok[:, j // 2, (4 * (j % 2) + k) * P:(4 * (j % 2) + k + 1) * P], ident)
                            ins.then_inc(S["x_t"], 1)
                    elif st == "pcols":
                        pe.wait_ge(S["params_in"], 16 * (NPARAM - 2) * l + 16 * NPARAM)
                        if l > 0:
                            pe.wait_ge(S["acc_end"], 2 * l - 1)
                        pe.wait_ge(S["cond"], 1)
                        tp(PB[6][:, 0:NROWS], rows[:, :], ident[0:NROWS, 0:NROWS]).then_inc(S["rows_t"], 1)
                        for h in range(H):
                            ins = tp(PB[4][:, P * h:P * h + P], wst[:, h, :], ident)
                        ins.then_inc(S["wsT"], 1)
                    elif st == "ada":
                        c = (st, ll, n)
                        chunk_here(pe, c)
                        pe.wait_ge(S["cond"], 1)
                        m = NADA * ll + n
                        if m not in ADA_FIRST:
                            ada_columns(m - 1)
                        if m > 0:
                            pe.wait_ge(S["ada_colc"], m)
                        w = chunk_view(c)
                        for k in range(KT):
                            j = 32 * (k % 4)
                            ins = mm(PB[7][j:j + 32, :], cond[:, k, :], w[:, k, :], start=(k < 4), stop=(k >= 4))
                        ins.then_inc(S["ada_used"], 1)
                    elif st == "adaout":
                        ada_columns(NADA * ll + n)
                    elif st == "sq":
                        for k in range(KT):
                            if k % 4 == 0:
                                pe.wait_ge(S["sq_ready"], 2 * g + k // 4 + 1)
                            ins = mm(PB[5][:, 0:NS * P], ones, sqr[:, k, :], start=(k == 0), stop=(k == KT - 1))
                        ins.then_inc(S["ss_ready"], 1)
                    elif st == "proj":
                        ci, s = n // 2, n % 2
                        c = (st, l, ci)
                        chunk_here(pe, c)
                        w = chunk_view(c)
                        if n == 0:
                            pe.wait_ge(S["ht_dve"], 2 * l + 1)
                            pe.wait_ge(S["ht_act"], 2 * l + 1)
                            for k in range(KT):
                                ins = mm(PB[0][0:32, 0:NS * P], w[:, k, :], hb[:, k, :, :].rearrange("p s t -> p (s t)"),
                                         start=(k == 0), stop=(k == KT - 1))
                            ins.then_inc(S["proj"], 2)
                            continue
                        if ci >= 2:
                            pe.wait_ge(S["ev"], 14 * l + n - 3)
                        for k in range(KT):
                            ins = mm(PB[2 * (ci % 2) + s][:, 0:PROJ[ci][1]], hb[:, k, s, :], w[:, k, :],
                                     start=(k == 0), stop=(k == KT - 1))
                        ins.then_inc(S["proj"], 1)
                    elif st == "glaB":
                        pe.wait_ge(S["ev"], 14 * l + 2)
                        if n == 1:
                            pe.wait_ge(S["st1"], 2 * l + 1)
                        mm(PB[5][:, :], lrT[:, P * n:P * n + P], w2gla[:, :], start=True, stop=True).then_inc(S["zz"], 1)
                    elif st == "glaC":
                        pe.wait_ge(S["gg"], g + 1)
                        if n == 1:
                            pe.wait_ge(S["og_done"], 2 * l + 1)
                        for d in range(2):
                            gd = g_sb[:, 256 * d:256 * d + 256]
                            mm(PB[6][:, 256 * d:256 * d + 256], const[:, (C_TRIF, C_TRIB)[d]:][:, 0:P], gd, start=True, stop=True)
                            mm(PB[5][:, 256 * d:256 * d + 256], const[:, (C_REMF, C_REMB)[d]:][:, 0:P], gd, start=True, stop=True)
                            for b in range(2):
                                q = 2 * d + b
                                ins = mm(PB[4][:, 2 * q:2 * q + 2], g_sb[:, P * q:P * q + P],
                                         const[:, C_CHUNK + d:C_CHUNK + d + 2], start=True, stop=True)
                        ins.then_inc(S["cum"], 1)
                    elif st == "glaD":
                        pe.wait_ge(S["qkd"], g + 1)
                        for q in range(4):
                            tp(PB[4][:, P * q:P * q + P], qd[:, P * q:P * q + P], ident)
                        for q in range(4):
                            ins = tp(PB[5][:, P * q:P * q + P], ki[:, P * q:P * q + P], ident)
                        ins.then_inc(S["qkt_gla"], 1)
                    elif st == "glaE":
                        pe.wait_ge(S["qkt_gla_c"], 2 * (g + 1))
                        for d in range(2):
                            for h in range(H):
                                b, q = 64 * (h % 2), P * (2 * d + h // 2)
                                ins = mm(PB[(6, 4)[h % 2]][:, 256 * d + P * (h // 2):256 * d + P * (h // 2) + P], kiT[b:b + 64, q:q + P], qdT[b:b + 64, q:q + P],
                                         start=True, stop=True)
                        ins.then_inc(S["attn"], 1)
                        for r in (0, 64):
                            for step in range(2):
                                d = step ^ (r // 64)
                                for h in range(H):
                                    b, col = 64 * (h % 2), 64 * (4 * step + 2 * d + h // 2)
                                    ins = mm(PB[5][b:b + 64, col:col + 64], ke[r:r + 64, 256 * d + 64 * h:256 * d + 64 * h + 64],
                                             pr[r:r + 64, n, CV + 64 * h:CV + 64 * h + 64], start=True, stop=True)
                            ins.then_inc(S["kv"], 1)
                            if r == 0:
                                pe.wait_ge(S["kv"], 2 * g + 1)
                    elif st == "glaF":
                        pe.wait_ge(S["attn_m"], g + 1)
                        pe.wait_ge(S["st1"], g + 1)
                        first = True
                        for h in range(H):
                            for d in range(2):
                                ins = mm(PB[6][:, 64 * h:64 * h + 64], attnT[:, P * (4 * d + h):P * (4 * d + h) + P],
                                   pr[:, n, CV + 64 * h:CV + 64 * h + 64], start=first, stop=False, skip_group_check=True)
                                first = False
                        for par in range(2):
                            ins.then_inc(S["o_part"], 1)
                            pe.wait_ge(S["o_part"], 2 * g + par + 1)
                            b = 64 * par
                            for h in range(par, H, 2):
                                for d in range(2):
                                    for step in range(n == 0, 2):
                                        r = 64 * (step ^ d)
                                        q = P * (2 * d + h // 2) + r
                                        state = (st0, st1)[step]
                                        ins = mm(PB[6][r:r + 64, 64 * h:64 * h + 64], qdT[b:b + 64, q:q + 64],
                                                 state[b:b + 64, d, h // 2, :], start=False, stop=(h >= 2), skip_group_check=True)
                        ins.then_inc(S["og"], 1)
                    elif st == "qkt":
                        pe.wait_ge(S["qk_done"], g + 1)
                        pe.wait_ge(S["ev"], 14 * (l + 1))
                        if n == 1:
                            pe.wait_ge(S["og_done"], 2 * l + 2)
                        for h in range(H):
                            tp(PB[4 * n][:, P * h:P * h + P], pr[:, n, BQ + P * h:BQ + P * h + P], ident)
                        if n == 1:
                            for h in range(H):
                                tp(PB[5][:, P * h:P * h + P], ckc[:, 2 * h:2 * h + 2, :].rearrange("p i d -> p (i d)"), ident)
                        for h in range(H):
                            ins = tp(PB[(1, 6)[n]][:, P * h:P * h + P], pr[:, n, BK + P * h:BK + P * h + P], ident)
                        ins.then_inc(S["qkT"], 1)
                    elif st == "sc":
                        pe.wait_ge(S["qkTc"], g + 1)
                        for m in range(8):
                            b, h = 64 * (m // 4), m % 4
                            q = atT[n][b:b + 64, P * h:P * h + P]
                            k = atT[n][b:b + 64, 512 + P * h:512 + P * h + P]
                            if n == 0:
                                ins = mm(PB[2 + m // 4][:, P * (m % 4):P * (m % 4) + P], q, k, start=True, stop=True)
                            else:
                                kc = atT[n][b:b + 64, 1024 + P * h:1024 + P * h + P]
                                mm(PB[SCB[m // 2]][:, 256 * (m % 2):256 * (m % 2) + P], q, kc, start=True, stop=True)
                                ins = mm(PB[SCB[m // 2]][:, 256 * (m % 2) + P:256 * (m % 2) + 2 * P], q, k, start=True, stop=True)
                        ins.then_inc(S["sc"], 1)
                    elif st == "wt":
                        pe.wait_ge(S["wmix"], g + 1)
                        for h in range(H):
                            if n == 0:
                                ins = tp(PB[2][:, P * h:P * h + P], p0w[:, h, :], ident)
                            else:
                                for j in range(2):
                                    ins = tp(PB[h // 2][:, 256 * (h % 2) + P * j:256 * (h % 2) + P * j + P], hb[:, h, j, :], ident)
                        ins.then_inc(S["wT"], 1)
                    elif st == "pv":
                        pe.wait_ge(S["wTc"], g + 1)
                        for h in range(H):
                            o = PB[3 + n][:, P * h:P * h + P]
                            v = pr[:, n, BV + P * h:BV + P * h + P]
                            if n == 0:
                                ins = mm(o, atT[0][:, P * h:P * h + P], v, start=True, stop=True)
                            else:
                                mm(o, pr[:, 1, BQ + 256 * h:BQ + 256 * h + P], cvc[:, h, :], start=True, stop=False)
                                ins = mm(o, pr[:, 1, BQ + 256 * h + P:BQ + 256 * h + 2 * P], v, start=False, stop=True)
                        ins.then_inc(S["pv"], 1)
                    elif st == "sgu":
                        pe.wait_ge(S["qkTc"], 2 * l + 2)
                        pe.wait_ge(S["v_done"], l + 1)
                        for h in range(H):
                            ins = mm(PB[6][:, P * h:P * h + P], wsT[:, h, :], pr[:, :, V0 + 64 * h:V0 + 64 * h + 64],
                                     start=True, stop=True)
                        ins.then_inc(S["sgu_s"], 1)
                    elif st == "catT":
                        pe.wait_ge(S["ob_done"], 2 * l + n + 1)
                        pe.wait_ge(S["og_done"], 2 * l + n + 1)
                        pe.wait_ge(S["sgu_done"], l + 1)
                        for j in (2 * n, 2 * n + 1):
                            for k in range(4):
                                m = 4 * (j % 2) + k
                                c0 = (U0, U0 + P, BQ, BQ + P, BQ + 2 * P, BQ + 3 * P, CQ, CQ + P)[m]
                                ins = tp(PB[CATB[j]][:, P * k:P * k + P], pr[:, n, c0:c0 + P], ident)
                            ins.then_inc(S["catT"], 1)
                    elif st == "wout":
                        c = (st, l, n)
                        chunk_here(pe, c)
                        pe.wait_ge(S["catTc"], 4 * (l + 1))
                        w = chunk_view(c)
                        for t in range(4):
                            for m in range(KT):
                                ins = mm(PB[(4, 0)[n] + t // 2][:, 256 * (t % 2):256 * (t % 2) + 256], w[:, m, P * t:P * t + P],
                                         hb[:, m, :, :].rearrange("p s t -> p (s t)"), start=(m == 0), stop=(m == KT - 1))
                        ins.then_inc(S["wout"], 1)
                    elif st == "routeA":
                        pe.wait_ge(S["ht_dve"], 2 * l + 2)
                        pe.wait_ge(S["ht_act"], 2 * l + 2)
                        pe.wait_ge(S["xadd"], 2 * (l + 1))
                        for s in range(NS):
                            for k in range(KT):
                                ins = mm(PB[4][:, E * s:E * s + E], hb[:, k, s, :], rw[:, k, :], start=(k == 0), stop=(k == KT - 1))
                        ins.then_inc(S["logit"], 1)
                        for j in range(4):
                            for k in range(4):
                                ins = tp(PB[j][:, P * k:P * k + P], hb[:, 4 * (j % 2) + k, j // 2, :], ident)
                            ins.then_inc(S["htok"], 1)
                    elif st == "route":
                        pe.wait_ge(S["mask"], l + 1)
                        m = sm(288, 32)
                        mm(PB[4][:, 32:48], const[:, C_STRICT:C_STRICT + P], m[:, 0:16], start=True, stop=True)
                        mm(PB[4][:, 48:64], ones, m[:, 0:16], start=True, stop=False)
                        mm(PB[4][:, 48:64], const[:, C_STRICT:C_STRICT + P], m[:, 16:32], start=False, stop=True)
                        mm(PB[4][:, 64:80], ones, m[:, 0:16], start=True, stop=False)
                        mm(PB[4][:, 64:80], ones, m[:, 16:32], start=False, stop=True).then_inc(S["pos"], 1)
                    elif st == "moe":
                        def gather(b):
                            for k in range(4):
                                for s in range(NS):
                                    ins = mm(PB[b][:, P * k:P * k + P], htok[:, s, P * (4 * b + k):P * (4 * b + k) + P], pm[:, s, :],
                                             start=(s == 0), stop=(s == NS - 1))
                            ins.then_inc(S["gat"], 1)

                        pe.wait_ge(S["htokc"], 4 * (l + 1))
                        pe.wait_ge(S["pmat"], NP_ * l + 1)
                        gather(0)
                        gather(1)

                        def scatter(v):
                            pe.wait_ge(S["ytok_a"], v)
                            pe.wait_ge(S["ytok_d"], v)
                            pe.wait_ge(S["pgt"], v)
                            for t in range(KT):
                                b = (6, 7, 0, 1)[t // 2]
                                ins = mm(PB[b][:, 256 * (t % 2):256 * (t % 2) + 256], ytok[:, P * t:P * t + P], pgT, start=True, stop=True)
                                if t % 4 == 3:
                                    ins.then_inc(S["scat"], 1)

                        def pair(i, odd, uses, last=False):
                            v = i + NP_ * l
                            pe.wait_ge(S["gat_a"], v + 1)
                            pe.wait_ge(S["pgt"], v + l + 1)
                            for b in range(2):
                                for a in range(2):
                                    if b == 0:
                                        pe.wait_ge(s_odd[a] if odd else s_slot[3 * a], uses * 16)
                                    else:
                                        pe.wait_ge(s_slot[3 * a + b], (v + 1) * 16)
                                w = [w1_view(a, odd) if b == 0 else slot_view(3 * a + b) for a in range(2)]
                                for k in range(KT):
                                    if b == 0 and k == 4:
                                        pe.wait_ge(S["gat_d"], v + 1)
                                    for a in range(2):
                                        ins = mm(PB[2 + b][CAP * a:CAP * a + CAP, :], hg[:, k, CAP * a:CAP * a + CAP],
                                                 w[a][:, k, :], start=(k == 0), stop=(k == KT - 1))
                                ins.then_inc(S["w1_used" if b == 0 else "h13"], 1)
                            pe.wait_ge(S["acc_d"], v * 2 + 3 * l + 1)
                            if not last:
                                pe.wait_ge(S["pmat"], v + 2)
                                gather(0)
                                gather(1)
                            pe.wait_ge(S["hid"], v + 1)
                            for f in range(FT):
                                ins = tp(PB[2][:, P * f:P * f + P], hid[:, P * f:P * f + P], ident)
                            ins.then_inc(S["tr"], 1)
                            if not last:
                                pe.wait_ge(S["gat_a"], v + 2)
                                pe.wait_ge(S["gat_d"], v + 2)
                            scatter(v + l + 1)
                            for s in range(NS):
                                ins = tp(PB[3][:, P * s:P * s + P], pg[:, s, :], ident)
                            ins.then_inc(S["tr_p"], 1)
                            pe.wait_ge(S["hidt"], v + 1)
                            for a in range(2):
                                pe.wait_ge(s_slot[3 * a + 2], (v + 1) * 16)
                            for c in range(2):
                                for f in range(FT):
                                    for a in range(2):
                                        ins = mm(PB[4 + c][CAP * a:CAP * a + CAP, :], hidT[:, f, CAP * a:CAP * a + CAP],
                                                 slot_view(3 * a + 2)[:, f, CW * c:CW * c + CW], start=(f == 0), stop=(f == FT - 1))
                            ins.then_inc(S["yt"], 1)

                        with pe.Fori(0, NP_ // 2 - 1) as j:
                            pair(j * 2, False, j + NP_ // 2 * l + 1)
                            pair(j * 2 + 1, True, j + NP_ // 2 * l + 1)
                        pair(NP_ - 2, False, NP_ // 2 * (l + 1))
                        pair(NP_ - 1, True, NP_ // 2 * (l + 1), last=True)
                        pe.wait_ge(S["acc_d"], 2 * NP_ * (l + 1) + 3 * l + 1)
                        scatter((NP_ + 1) * (l + 1))
                        pe.wait_ge(S["posm"], l + 1)
                        over = pe.value_load(flag[0:1, 0:1], min_val=0, max_val=1)
                        O = OV[l]
                        with pe.If(over):
                            with pe.Fori(1, ROUNDS) as r:
                                with pe.Fori(0, E) as e:
                                    q = (r - 1) * E + e
                                    pe.wait_ge(O["p"], q + 1)
                                    for k in range(KT):
                                        for s in range(NS):
                                            ins = mm(PB[0][:, CAP * k:CAP * k + CAP], htok[:, s, P * k:P * k + P], pm[:, s, 0:CAP],
                                                     start=(s == 0), stop=(s == NS - 1))
                                    ins.then_inc(O["gat"], 1)
                                    pe.wait_ge(O["gat_c"], q + 1)
                                    pe.wait_ge(O["w"], (q + 1) * 48)
                                    for b in range(2):
                                        for k in range(KT):
                                            ins = mm(PB[2 + b][0:CAP, :], hg[:, k, 0:CAP], slot_view(b)[:, k, :],
                                                     start=(k == 0), stop=(k == KT - 1))
                                    ins.then_inc(O["h13"], 1)
                                    pe.wait_ge(O["hid"], q + 1)
                                    for f in range(FT):
                                        ins = tp(PB[2][:, P * f:P * f + P], hid[:, P * f:P * f + P], ident)
                                    ins.then_inc(O["tr"], 1)
                                    pe.wait_ge(O["hidt"], q + 1)
                                    for c in range(2):
                                        for f in range(FT):
                                            ins = mm(PB[4 + c][0:CAP, :], hidT[:, f, 0:CAP], slot_view(2)[:, f, CW * c:CW * c + CW],
                                                     start=(f == 0), stop=(f == FT - 1))
                                    ins.then_inc(O["yt"], 1)
                                    for s in range(NS):
                                        ins = tp(PB[3][:, P * s:P * s + P], pg[:, s, :], ident)
                                    ins.then_inc(O["tr_p"], 1)
                                    pe.wait_ge(O["tr_c"], q + 1)
                                    for t in range(KT):
                                        ins = mm(PB[(6, 7, 0, 1)[t // 2]][:, 256 * (t % 2):256 * (t % 2) + 256], ytok[0:CAP, P * t:P * t + P],
                                                 pgT[0:CAP, :], start=True, stop=True)
                                    ins.then_inc(O["scat"], 1)
            for n, j in enumerate((0, 2, 1, 3)):
                pe.wait_ge(S["acc_end"], 2 * DEPTH - 1 + n // 2)
                for k in range(4):
                    ins = tp(PB[j][:, P * k:P * k + P], xT[:, 4 * (j % 2) + k, j // 2, :], ident)
                ins.then_inc(S["fin_t"], 1)

        @block.vector
        def _(dve):
            v_ = nc.vector
            n_chain = [0]

            def link(ins):
                n_chain[0] += 1
                ins.then_inc(S["dve_chain"], 1)
                dve.wait_ge(S["dve_chain"], n_chain[0])

            def ada_copy(m):
                dve.wait_ge(S["ada_col"], m + 1)
                c = 4 * (m % NADA)
                v_.tensor_copy(ada[:, c:c + 4, :].rearrange("p c s -> p (c s)"), PB[7][:, 0:8]).then_inc(S["ada_colc"], 1)

            def bc(ap, shape):
                return ap.to_broadcast(shape)

            def squares(k):
                xk = xT[:, k:k + 4, :, :].rearrange("p k s t -> p k (s t)")
                v_.tensor_tensor(sqr[:, k:k + 4, :], xk, xk, ALU.mult).then_inc(S["sq_ready"], 1)

            link(v_.memset(posm[:, :, :], -1.0))
            link(v_.memset(gates[:, :, :], 0.0))
            dve.wait_ge(S["const_in"], 16)
            for l in range(DEPTH):
                lam_init = 0.8 - 0.6 * math.exp(-0.3 * l)
                for st, ll, n in plans[l]:
                    g = 2 * l + n
                    if st == "xin":
                        for j in range(4):
                            if j % 2 == 0:
                                dve.wait_ge(S["x_t"], j + 1)
                                v_.tensor_copy(xT[:, 4 * (j % 2):4 * (j % 2) + 4, j // 2, :],
                                               PB[j][:, :].rearrange("p (k t) -> p k t", k=4)).then_inc(S["x_tc"], 1)
                        dve.wait_ge(S["x_tc"], 4)
                    elif st == "lam":
                        dve.wait_ge(S["params_in"], 16 * (NPARAM - 2) * l + 16 * NPARAM)
                        link(v_.tensor_tensor(sm(320, 128).rearrange("p (a d) -> p a d", a=2), dlam[:, 0::2, :], dlam[:, 1::2, :], ALU.mult))
                        v_.tensor_reduce(lam[:, 0:2], sm(320, 128).rearrange("p (a d) -> p a d", a=2), X, ALU.add).then_inc(S["lam"], 1)
                        dve.wait_ge(S["lam"], 2 * l + 2)
                        link(v_.tensor_tensor(lam[:, 4:5], lam[:, 3:4], lam[:, 2:3], ALU.subtract))
                        link(v_.tensor_scalar(lam[:, 5:6], lam[:, 4:5], -lam_init, None, ALU.add))
                        link(v_.tensor_scalar(dg[:, :], dg[:, :], 1.0 - lam_init, None, ALU.mult))
                    elif st == "ada":
                        m = NADA * ll + n
                        if m not in ADA_FIRST and m < ADA_FIRST[1]:
                            ada_copy(m - 1)
                    elif st == "adaout":
                        if NADA * ll + n < ADA_FIRST[1]:
                            ada_copy(NADA * ll + n)
                    elif st == "mod":
                        if n == 0:
                            dve.wait_ge(S["rows_t"], l + 1)
                            link(v_.tensor_copy(cols[:, :], PB[6][:, 0:NROWS]))
                        dve.wait_ge(S["ada_colc"], NADA * l + NADA // 2 * (n + 1))
                        link(v_.tensor_tensor(mod[:, 24 * n:24 * n + 24, :], ada[:, 24 * n:24 * n + 24, :],
                                              bc(cols[:, 24 * n:24 * n + 24].unsqueeze(2), [P, 24, 2]), ALU.add))
                        m = mod[:, 24 * n + 8:24 * n + 16, :]
                        link(v_.tensor_scalar(m, m, 1.0, None, ALU.add))
                        v_.tensor_tensor(m, m, bc(cols[:, 48 + 8 * n:56 + 8 * n].unsqueeze(2), [P, 8, 2]), ALU.mult).then_inc(S["mod_ready"], 1)
                        dve.wait_ge(S["mod_ready"], g + 1)
                    elif st in ("sqa", "sq"):
                        squares(0 if st == "sqa" else 4)
                    elif st == "xn":
                        dve.wait_ge(S["rstd_ready"], g + 1)
                        link(v_.reciprocal(rsq[:, 1, :], rsq[:, 0, :]))
                        for k in (0, 4):
                            v_.tensor_tensor(hb[:, k:k + 4, :, :].rearrange("p k s t -> p k (s t)"),
                                             xT[:, k:k + 4, :, :].rearrange("p k s t -> p k (s t)"),
                                             bc(rsq[:, 1:2, :], [P, 4, 256]), ALU.mult).then_inc(S["xn_ready"], 1)
                    elif st == "norm":
                        dve.wait_ge(S["xn_ready"], 2 * g + 2)
                        for k in range(KT):
                            ins = v_.tensor_scalar(hb[:, k, 0, :], hb[:, k, 0, :], mod[:, 24 * n + 8 + k, 0:1],
                                                   mod[:, 24 * n + k, 0:1], ALU.mult, ALU.add)
                        ins.then_inc(S["ht_dve"], 1)
                    elif st == "proj":
                        c = n // 2
                        if n > 0 and c not in BY_ACT and n % 2 == 0:
                            dve.wait_ge(S["proj"], 14 * l + n + 1)
                            if n > 0:
                                dve.wait_ge(S["ev"], 14 * l + n)
                            c0, w = PROJ[c]
                            v_.tensor_copy(pr[:, 0, c0:c0 + w], PB[2 * (c % 2)][:, 0:w]).then_inc(S["ev"], 1)
                    elif st == "glaB":
                        dve.wait_ge(S["lng"], g + 1)
                        v_.scalar_tensor_tensor(out=g_sb, in0=PB[5][:, :], scalar=0.0, in1=ki, op0=ALU.min,
                                                op1=ALU.subtract).then_inc(S["gg"], 1)
                    elif st == "glaC":
                        dve.wait_ge(S["exps"], g + 1)
                        dve.wait_ge(S["ev"], 14 * l + 6)
                        q = bc(pr[:, n, CQ:CQ + 256].unsqueeze(1), [P, 2, 256])
                        k = bc(pr[:, n, CK:CK + 256].unsqueeze(1), [P, 2, 256])
                        v3 = [t.rearrange("p (a c) -> p a c", a=2) for t in (qd, ki, ke)]
                        v_.scalar_tensor_tensor(out=v3[0], in0=v3[0], scalar=QK ** -0.5, in1=q, op0=ALU.mult, op1=ALU.mult)
                        v_.tensor_tensor(v3[1], v3[1], k, ALU.mult)
                        v_.tensor_tensor(v3[2], v3[2], k, ALU.mult).then_inc(S["qkd"], 1)
                        sgt = pr[:, n, CR:CR + 256]
                        link(v_.tensor_scalar(sgtmp, sgtmp, 1.0, None, ALU.add))
                        link(v_.reciprocal(sgtmp, sgtmp))
                        v_.tensor_tensor(sgt, sgt, sgtmp, ALU.mult).then_inc(S["sg_done"], 1)
                        dve.wait_ge(S["sg_done"], g + 1)
                        s3 = sgt.rearrange("p (h d) -> p h d", h=H)
                        link(v_.tensor_tensor(s3, s3, bc(glag[:, :].unsqueeze(1), [P, H, 64]), ALU.mult))
                    elif st == "glaD":
                        dve.wait_ge(S["qkt_gla"], g + 1)
                        v_.tensor_copy(kiT, PB[5][:, :]).then_inc(S["qkt_gla_c"], 1)
                    elif st == "glaE":
                        dve.wait_ge(S["attn"], g + 1)
                        dve.wait_ge(S["zeroed"], g + 1)
                        for d in range(2):
                            mask = const[:, (C_TRIF, C_TRIB)[d]:][:, 0:P].bitcast(I32)
                            for par in range(2):
                                ins = v_.copy_predicated(attnT[:, 512 * d:512 * d + 512].rearrange("p (h r i) -> p h r i", r=2, i=P)[:, :, par],
                                                         bc(mask.unsqueeze(1), [P, 2, P]),
                                                         PB[(6, 4)[par]][:, 256 * d:256 * d + 256].rearrange("p (h i) -> p h i", h=2))
                        ins.then_inc(S["attn_m"], 1)
                        dve.wait_ge(S["kv"], 2 * g + 2)
                        if n == 0 and l > 0:
                            dve.wait_ge(S["state_out"], 64 * l)
                        kvb = PB[5][:, :].rearrange("p (s a b v) -> p s (a b) v", s=2, a=2, b=2)
                        d3 = dec.rearrange("p (q s) -> p q s", s=2)
                        s0v, s1v, s2v = (t.rearrange("p a b v -> p (a b) v") for t in (st0[:, :, :, :], st1, st2))
                        if n == 0:
                            link(v_.tensor_copy(s1v, kvb[:, 0]))
                            link(v_.tensor_tensor(s2v, s1v, bc(d3[:, :, 1:2], [P, 4, 64]), ALU.mult))
                            v_.tensor_tensor(s2v, s2v, kvb[:, 1], ALU.add).then_inc(S["st1"], 1)
                        else:
                            link(v_.tensor_tensor(s1v, s0v, bc(d3[:, :, 0:1], [P, 4, 64]), ALU.mult))
                            v_.tensor_tensor(s1v, s1v, kvb[:, 0], ALU.add).then_inc(S["st1"], 1)
                    elif st == "glaF":
                        dve.wait_ge(S["og_sq"], g + 1)
                        link(v_.tensor_reduce(sm(204, 4), ke[:, 0:256].rearrange("p (h d) -> p h d", h=H), X, ALU.add))
                        v_.tensor_scalar(sm(208, 4), sm(204, 4), 1.0 / 64, EPS, ALU.mult, ALU.add).then_inc(S["og_ms"], 1)
                        dve.wait_ge(S["og_rs"], g + 1)
                        for h in range(H):
                            ins = v_.scalar_tensor_tensor(out=pr[:, n, CQ + 64 * h:CQ + 64 * h + 64], in0=PB[6][:, 64 * h:64 * h + 64],
                                                          scalar=sm(212 + h, 1), in1=pr[:, n, CR + 64 * h:CR + 64 * h + 64], op0=ALU.mult, op1=ALU.mult)
                        ins.then_inc(S["og_done"], 1)
                    elif st == "qkn":
                        dve.wait_ge(S["qk_sq"], g + 1)
                        qk16 = pr[:, n, BQ:BQ + 1024].rearrange("p (g d) -> p g d", d=64)
                        link(v_.tensor_reduce(sm(SSQ, 16), atT[0].rearrange("p (g d) -> p g d", d=64), X, ALU.add))
                        v_.tensor_scalar(sm(QMS, 16), sm(SSQ, 16), 1.0 / 64, EPS, ALU.mult, ALU.add).then_inc(S["qk_ms"], 1)
                        dve.wait_ge(S["qk_rs"], g + 1)
                        link(v_.tensor_tensor(qk16, qk16, bc(sm(QRS, 16).unsqueeze(2), [P, 16, 64]), ALU.mult))
                        qk4 = pr[:, n, BQ:BQ + 1024].rearrange("p (a g d) -> p a g d", a=2, d=64)
                        ins = v_.tensor_tensor(qk4, qk4, bc(qkg[:, :, :].unsqueeze(2), [P, 2, 8, 64]), ALU.mult)
                        if n == 0:
                            ins.then_inc(S["qk_done"], 1)
                        else:
                            link(ins)
                            tmp = atT[0]
                            x5 = pr[:, 1, BQ:BQ + 1024].rearrange("p (g h a f) -> p g h a f", g=16, h=2, a=2)
                            t5 = tmp.rearrange("p (g h a f) -> p g h a f", g=16, h=2, a=2)
                            sn = const[:, C_SIN:C_SIN + 64].rearrange("p (h a f) -> p h a f", h=2, a=2)
                            for a in range(2):
                                ins = v_.tensor_tensor(t5[:, :, :, a, :], x5[:, :, :, 1 - a, :],
                                                       bc(sn[:, :, a, :].unsqueeze(1), [P, 16, 2, 16]), ALU.mult)
                            link(ins)
                            link(v_.tensor_tensor(qk16, qk16, bc(const[:, C_COS:C_COS + 64].unsqueeze(1), [P, 16, 64]), ALU.mult))
                            v_.tensor_tensor(pr[:, 1, BQ:BQ + 1024], pr[:, 1, BQ:BQ + 1024], tmp, ALU.add).then_inc(S["qk_done"], 1)
                    elif st == "sc":
                        dve.wait_ge(S["sc"], g + 1)
                        for b in range(2 if n == 0 else 4):
                            w = 4 if n == 0 else 2
                            ins = v_.tensor_reduce(sm(SMX + 16 * n + 8 + w * b, w), PB[(2 + b if n == 0 else SCB[b])][:, :].rearrange("p (m k) -> p m k", m=w),
                                                   X, ALU.max)
                        link(ins)
                        v_.tensor_scalar(sm(SMX + 16 * n, 8), sm(SMX + 16 * n + 8, 8), -(QK ** -0.5), None, ALU.mult).then_inc(S["nmax"], 1)
                    elif st == "mix":
                        dve.wait_ge(S["pexp"], g + 1)
                        sums = SSM + 16 * n
                        link(v_.reciprocal(sm(sums + 8, 8), sm(sums, 8)))
                        r2 = sm(sums + 12, 4)
                        link(v_.tensor_scalar(r2, r2, lam[:, 5:6], None, ALU.mult))

                        def pw(m):
                            if n == 0:
                                return p0w[:, m, :]
                            return hb[:, m, :, :].rearrange("p s t -> p (s t)")
                        for h in range(H):
                            ins = v_.tensor_scalar(pw(h), pw(h), sm(sums + 8 + h, 1), None, ALU.mult)
                        link(ins)
                        for h in range(H):
                            ins = v_.scalar_tensor_tensor(out=pw(h), in0=pw(4 + h), scalar=sm(sums + 12 + h, 1), in1=pw(h),
                                                          op0=ALU.mult, op1=ALU.add)
                        ins.then_inc(S["wmix"], 1)
                    elif st == "pv":
                        dve.wait_ge(S["o_sq"], g + 1)
                        link(v_.tensor_reduce(sm(220, 4), atT[n][:, 512:1024].rearrange("p (h d) -> p h d", h=H), X, ALU.add))
                        v_.tensor_scalar(sm(224, 4), sm(220, 4), 1.0 / P, EPS, ALU.mult, ALU.add).then_inc(S["o_ms"], 1)
                        dve.wait_ge(S["o_rs"], g + 1)
                        for h in range(H):
                            ins = v_.scalar_tensor_tensor(out=pr[:, n, BQ + P * h:BQ + P * h + P], in0=PB[3 + n][:, P * h:P * h + P],
                                                          scalar=sm(228 + h, 1), in1=dg[:, :], op0=ALU.mult, op1=ALU.mult)
                        ins.then_inc(S["ob_done"], 1)
                    elif st == "sguv":
                        dve.wait_ge(S["ev"], 14 * l + 12)
                        v4 = pr[:, :, V0:V0 + 256]
                        tmp = at[:, 0:512].rearrange("p (s c) -> p s c", s=2)
                        link(v_.tensor_tensor(tmp, v4, v4, ALU.mult))
                        link(v_.tensor_reduce(sm(232, 8), tmp.rearrange("p s (g c) -> p (s g) c", c=64), X, ALU.add))
                        v_.tensor_scalar(sm(240, 8), sm(232, 8), 1.0 / 64, EPS, ALU.mult, ALU.add).then_inc(S["vms"], 1)
                        dve.wait_ge(S["vrs"], l + 1)
                        v5 = v4.rearrange("p s (g c) -> p s g c", c=64)
                        v_.tensor_tensor(v5, v5, bc(sm(248, 8).rearrange("p (s g) -> p s g", s=2).unsqueeze(3), [P, 2, 4, 64]),
                                         ALU.mult).then_inc(S["v_done"], 1)
                    elif st == "sgu":
                        dve.wait_ge(S["sgu_s"], l + 1)
                        for h in range(H):
                            u = pr[:, :, U0 + 64 * h:U0 + 64 * h + 64]
                            ins = v_.scalar_tensor_tensor(out=u, in0=PB[6][:, P * h:P * h + P].rearrange("p (s c) -> p s c", s=2),
                                                          scalar=cols[:, 64 + h:65 + h], in1=u, op0=ALU.add, op1=ALU.mult)
                        ins.then_inc(S["sgu_done"], 1)
                    elif st == "catT":
                        dve.wait_ge(S["catT"], 4 * l + 2 * n + 1)
                        dve.wait_ge(S["wT"], 2 * l + 2)
                        v_.tensor_copy(hb[:, 0:4, n, :], PB[CATB[2 * n]][:, :].rearrange("p (k t) -> p k t", k=4)).then_inc(S["catTc"], 1)
                    elif st == "wout":
                        dve.wait_ge(S["wout"], 2 * l + n + 1)
                        for t in range(4):
                            for s in range(NS):
                                k = 4 * n + t
                                ins = v_.scalar_tensor_tensor(out=xT[:, k, s, :], in0=PB[(4, 0)[n] + t // 2][:, 256 * (t % 2) + P * s:256 * (t % 2) + P * s + P],
                                                              scalar=mod[:, 16 + k, s:s + 1], in1=xT[:, k, s, :], op0=ALU.mult, op1=ALU.add)
                        ins.then_inc(S["xadd"], 1)
                        dve.wait_ge(S["xadd"], 2 * l + n + 1)
                    elif st == "routeA":
                        dve.wait_ge(S["kcache_out"], 16 * (l + 1))
                        dve.wait_ge(S["vcache_out"], 16 * (l + 1))
                        dve.wait_ge(S["state_out"], 64 * (l + 1))
                        dve.wait_ge(S["aff"], l + 1)
                        aff = sm(256, 32)
                        sel = sm(320, 32)
                        msk = sm(288, 32)
                        tmp, tmp2 = rsq[:, 0, 0:128], rsq[:, 1, 0:128]
                        link(v_.tensor_tensor(sel.rearrange("p (s e) -> p s e", s=2), aff.rearrange("p (s e) -> p s e", s=2),
                                              bc(rbias[:, :].unsqueeze(1), [P, 2, E]), ALU.add))

                        def before(vals, n_, out):
                            i_ = bc(vals.unsqueeze(2), [P, n_, 4, 4])
                            j_ = bc(vals.unsqueeze(3), [P, n_, 4, 4])
                            a = tmp[:, 0:16 * n_].rearrange("p (n j i) -> p n j i", j=4, i=4)
                            b = tmp2[:, 0:16 * n_].rearrange("p (n j i) -> p n j i", j=4, i=4)
                            low = bc(const[:, C_LOWER:C_LOWER + 16].rearrange("p (j i) -> p j i", j=4).unsqueeze(1), [P, n_, 4, 4])
                            v_.tensor_tensor(a, i_, j_, ALU.is_gt)
                            link(v_.tensor_tensor(b, i_, j_, ALU.is_ge))
                            link(v_.tensor_tensor(b, b, low, ALU.mult))
                            link(v_.tensor_tensor(a, a, b, ALU.max))
                            link(v_.tensor_reduce(out, a, X, ALU.add))

                        sel4 = sel.rearrange("p (n e) -> p n e", e=4)
                        rank = sm(352, 32).rearrange("p (n e) -> p n e", e=4)
                        before(sel4, 8, rank)
                        pairs = sm(384, 48).rearrange("p (n c) -> p n c", c=6)
                        v_.tensor_tensor(pairs[:, :, 0:3], sel4[:, :, 0:3], sel4[:, :, 1:4], ALU.add)
                        v_.tensor_tensor(pairs[:, :, 3:5], sel4[:, :, 0:2], sel4[:, :, 2:4], ALU.add)
                        link(v_.tensor_tensor(pairs[:, :, 5:6], sel4[:, :, 0:1], sel4[:, :, 3:4], ALU.add))
                        grp = sm(432, 8)
                        link(v_.tensor_reduce(grp, pairs, X, ALU.max))
                        gr = sm(440, 8)
                        before(grp.rearrange("p (s g) -> p s g", s=2), 2, gr.rearrange("p (s g) -> p s g", s=2))
                        m4 = msk.rearrange("p (n e) -> p n e", e=4)
                        link(v_.tensor_scalar(gr, gr, 0.5, None, ALU.is_lt))
                        link(v_.tensor_scalar(m4, rank, 1.5, None, ALU.is_lt))
                        v_.tensor_tensor(m4, m4, bc(gr.unsqueeze(2), [P, 8, 4]), ALU.mult).then_inc(S["mask"], 1)
                        dve.wait_ge(S["mask"], l + 1)
                        gt = gates[:, :, 0:E]
                        a2, k2 = aff.rearrange("p (s e) -> p s e", s=2), msk.rearrange("p (s e) -> p s e", s=2)
                        link(v_.tensor_tensor(gt, a2, k2, ALU.mult))
                        link(v_.tensor_reduce(sm(320, 2), gt, X, ALU.add))
                        link(v_.reciprocal(sm(322, 2), sm(320, 2)))
                        link(v_.tensor_tensor(gt, gt, bc(sm(322, 2).unsqueeze(2), [P, 2, E]), ALU.mult))
                        dve.wait_ge(S["pos"], l + 1)
                        link(v_.tensor_scalar(posm[:, :, 0:E], PB[4][:, 32:64].rearrange("p (s e) -> p s e", s=2), 1.0, None, ALU.add))
                        link(v_.tensor_tensor(posm[:, :, 0:E], posm[:, :, 0:E], k2, ALU.mult))
                        link(v_.tensor_scalar(posm[:, :, 0:E], posm[:, :, 0:E], -1.0, None, ALU.add))
                    elif st == "moe":
                        iota = const[:, C_IOTA:C_IOTA + CAP]

                        def slots_of(i, dst, gated):
                            for s in range(NS):
                                for a in range(2):
                                    ps = posm[:, s, bass.ds(i * 2 + a, 1)]
                                    gs = gates[:, s, bass.ds(i * 2 + a, 1)]
                                    o = dst[:, s, CAP * a:CAP * a + CAP]
                                    if gated:
                                        ins = v_.tensor_scalar(o, iota, ps, gs, ALU.is_equal, ALU.mult)
                                    else:
                                        ins = v_.tensor_scalar(o, iota, ps, None, ALU.is_equal)
                            return ins

                        def accumulate(v, b):
                            dve.wait_ge(S["acc_d"], (2 * NP_ + 3) * l + 1)
                            dve.wait_ge(S["scat"], v * 2 + b + 1)
                            for c in range(2):
                                t = 1024 * b + 512 * c
                                ins = v_.tensor_tensor(accT[:, t:t + 512], accT[:, t:t + 512], PB[(6, 7, 0, 1)[2 * b + c]][:, :], ALU.add)
                            ins.then_inc(S["acc_d"], 1)

                        slots_of(0, pm, False).then_inc(S["pmat"], 1)
                        link(v_.tensor_reduce(sm(324, 1), PB[4][:, 64:80], X, ALU.max))
                        link(v_.tensor_scalar(sm(325, 1), sm(324, 1), CAP + 0.5, None, ALU.is_gt))
                        v_.tensor_copy(flag[0:1, 0:1], small[0:1, 325:326]).then_inc(S["posm"], 1)
                        v_.memset(pgT, 0.0).then_inc(S["pgt"], 1)
                        v_.memset(ytok[:, 0:512], 0.0).then_inc(S["ytok_a"], 1)
                        v_.memset(ytok[:, 512:1024], 0.0).then_inc(S["ytok_d"], 1)
                        dve.wait_ge(S["gat"], 2 * NP_ * l + 2)
                        v_.tensor_copy(hg[:, 4:8, :], PB[1][:, :].rearrange("p (k c) -> p k c", k=4)).then_inc(S["gat_d"], 1)

                        def pair(i, last):
                            v = i + NP_ * l
                            if not last:
                                slots_of(i + 1, pm, False).then_inc(S["pmat"], 1)
                            slots_of(i, pg, True)
                            dve.wait_ge(S["silu"], v + 1)
                            v_.tensor_tensor(hid, sg1, PB[3][:, :], ALU.mult).then_inc(S["hid"], 1)
                            if not last:
                                dve.wait_ge(S["gat"], v * 2 + 4)
                                v_.tensor_copy(hg[:, 4:8, :], PB[1][:, :].rearrange("p (k c) -> p k c", k=4)).then_inc(S["gat_d"], 1)
                            accumulate(v + l, 0)
                            accumulate(v + l, 1)
                            dve.wait_ge(S["yt"], v + 1)
                            v_.tensor_copy(ytok[:, 512:1024], PB[5][:, :]).then_inc(S["ytok_d"], 1)

                        with dve.Fori(0, NP_ - 1) as i:
                            pair(i, False)
                        pair(NP_ - 1, True)
                        accumulate((NP_ + 1) * (l + 1) - 1, 0)
                        accumulate((NP_ + 1) * (l + 1) - 1, 1)
                        over = dve.value_load(flag[0:1, 0:1], min_val=0, max_val=1)
                        O = OV[l]
                        with dve.If(over):
                            v_.tensor_copy(iotar, iota).then_inc(O["acc"], 1)
                            dve.wait_ge(O["acc"], 1)
                            with dve.Fori(1, ROUNDS) as r:
                                v_.tensor_scalar(iotar, iotar, float(CAP), None, ALU.add).then_inc(O["acc"], 1)
                                with dve.Fori(0, E) as e:
                                    q = (r - 1) * E + e
                                    dve.wait_ge(O["acc"], r + q + 1)
                                    for s in range(NS):
                                        ps, gs = posm[:, s, bass.ds(e, 1)], gates[:, s, bass.ds(e, 1)]
                                        v_.tensor_scalar(pm[:, s, 0:CAP], iotar, ps, None, ALU.is_equal)
                                        ins = v_.tensor_scalar(pg[:, s, 0:CAP], iotar, ps, gs, ALU.is_equal, ALU.mult)
                                    ins.then_inc(O["p"], 1)
                                    dve.wait_ge(O["gat"], q + 1)
                                    v_.tensor_copy(hg[:, :, 0:CAP], PB[0][:, :].rearrange("p (k c) -> p k c", k=KT)).then_inc(O["gat_c"], 1)
                                    dve.wait_ge(O["silu"], q + 1)
                                    v_.tensor_tensor(hid[0:CAP, :], sg1[0:CAP, :], PB[3][0:CAP, :], ALU.mult).then_inc(O["hid"], 1)
                                    dve.wait_ge(O["tr"], q + 1)
                                    v_.tensor_copy(hidT, PB[2][:, :].rearrange("p (f c) -> p f c", f=FT)).then_inc(O["hidt"], 1)
                                    dve.wait_ge(O["tr_p"], q + 1)
                                    v_.tensor_copy(pgT[0:CAP, :], PB[3][0:CAP, 0:256])
                                    v_.tensor_copy(ytok[0:CAP, 0:512], PB[4][0:CAP, :])
                                    v_.tensor_copy(ytok[0:CAP, 512:1024], PB[5][0:CAP, :]).then_inc(O["tr_c"], 1)
                                    dve.wait_ge(O["scat"], q + 1)
                                    for c in range(4):
                                        ins = v_.tensor_tensor(accT[:, 512 * c:512 * c + 512], accT[:, 512 * c:512 * c + 512],
                                                               PB[(6, 7, 0, 1)[c]][:, :], ALU.add)
                                    ins.then_inc(O["acc"], 1)
                            dve.wait_ge(O["acc"], ROUNDS + (ROUNDS - 1) * E)
                        dve.wait_ge(S["acc_d"], (2 * NP_ + 3) * (l + 1))
                        link(v_.tensor_copy(sm(328, 1), accT[:, 0:1]))
                        a4 = accT.rearrange("p (k s t) -> p k s t", k=KT, s=2)
                        for half in range(2):
                            for k in range(4 * half, 4 * half + 4):
                                for s in range(NS):
                                    ins = v_.scalar_tensor_tensor(out=xT[:, k, s, :], in0=a4[:, k, s, :], scalar=mod[:, 40 + k, s:s + 1],
                                                                  in1=xT[:, k, s, :], op0=ALU.mult, op1=ALU.add)
                            ins.then_inc(S["acc_end"], 1)
                            dve.wait_ge(S["acc_end"], 2 * l + half + 1)
                            if half == 0 and l + 1 < DEPTH:
                                squares(0)
            for j in range(4):
                if j % 2 == 0:
                    dve.wait_ge(S["fin_t"], j // 2 + 1)
                    v_.tensor_copy(x_tok[:, j // 2, 0:512], PB[j][:, :]).then_inc(S["fin_c"], 1)


_INS = ['x_prompt', 'x_sample', 'cache_k', 'cache_v', 'state_gla', 'c', 'c_ctx', 'w_in', 'w_out', 'sgu_w', 'sgu_b',
        'q_norm_g', 'k_norm_g', 'diff_lambda', 'diff_norm_g', 'gla_w2', 'gla_b', 'gla_norm_g', 'norm1_g', 'norm2_g',
        'ada_w', 'ada_b', 'router_w', 'router_bias', 'moe_w1', 'moe_w3', 'moe_w2']
_OUTS = [(1, P, D), (1, P, D), (1, DEPTH, H, 2, P, QK), (1, DEPTH, H, P, P), (1, DEPTH, 2, H, QK, QK)]


def kernel(**inputs):
    import numpy as _np
    import concourse.bacc as _bacc
    from concourse import mybir as _mybir
    from concourse.bass_utils import run_bass_kernel_spmd as _run

    nc = _bacc.Bacc("TRN2", target_bir_lowering=False, num_devices=1)
    arrays, aps = {}, {}
    given = {name: _np.ascontiguousarray(inputs[name]) for name in _INS}
    given["const"] = constants()
    for name, a in given.items():
        arrays[f"in_{name}_dram"] = a
        aps[name] = nc.dram_tensor(f"in_{name}_dram", a.shape, _mybir.dt.from_np(a.dtype), kind="ExternalInput").ap()
    outs = [nc.dram_tensor(f"out_{i}_dram", shape, _mybir.dt.float32, kind="ExternalOutput").ap()
            for i, shape in enumerate(_OUTS)]
    hybrid_step(nc, aps, outs)
    r = _run(nc, [arrays], core_ids=[0])
    return tuple(r.results[0][f"out_{i}_dram"] for i in range(len(_OUTS)))
```
